# Optimizing a Trainium2 kernel written in Bass

```python
import math
import jax, jax.numpy as jnp
from jax import lax
import numpy as np

D_MODEL = 1024
BATCH = 1
SEQ = 256
DEPTH = 2

N_HEADS = 16
HEAD_DIM = D_MODEL // N_HEADS
ROPE_DIM = HEAD_DIM // 4
ROPE_THETA = 500000.0
ATTN_SCALE = HEAD_DIM ** -0.5
DILATED_PAIRS = ((128, 1), (512, 4), (2048, 16))
N_DIL = len(DILATED_PAIRS)
BAND_BLOCK = 128
MOBA_BLOCK = 256
MOBA_TOPK = 3
MOBA_QCHUNK = 128
D_FF = 2816
CONV_WIDTH = 3
RMS_EPS = 1e-6
N_LAYERS_A = (DEPTH + 1) // 2
N_LAYERS_B = DEPTH // 2


def rmsnorm(x, gain):
    xf = x.astype(jnp.float32)
    y = xf * lax.rsqrt(jnp.mean(xf * xf, axis=-1, keepdims=True) + RMS_EPS)
    return (y * gain.astype(jnp.float32)).astype(x.dtype)

def rope_tables(seq_len):
    pos = jnp.arange(seq_len, dtype=jnp.float32)
    inv_freq = ROPE_THETA ** (-jnp.arange(0, ROPE_DIM, 2, dtype=jnp.float32) / ROPE_DIM)
    ang = pos[:, None] * inv_freq[None, :]
    return jnp.cos(ang), jnp.sin(ang)

def apply_partial_rope(x, cos, sin):
    extra = x.ndim - 3
    c = cos.reshape((cos.shape[0],) + (1,) * extra + (cos.shape[1],)).astype(x.dtype)
    s = sin.reshape((sin.shape[0],) + (1,) * extra + (sin.shape[1],)).astype(x.dtype)
    half = ROPE_DIM // 2
    x1, x2, xp = x[..., :half], x[..., half:ROPE_DIM], x[..., ROPE_DIM:]
    return jnp.concatenate([x1 * c - x2 * s, x2 * c + x1 * s, xp], axis=-1)

def band_attention(q, k, v, dil, window):
    S, H, hd = q.shape
    reach = window // dil
    assert reach <= BAND_BLOCK
    span = dil * BAND_BLOCK
    s_pad = -(-S // span) * span
    L = s_pad // dil
    nb = L // BAND_BLOCK

    def to_res(t):
        t = jnp.pad(t, ((0, s_pad - S), (0, 0), (0, 0)))
        return t.reshape(L, dil, H, hd).transpose(1, 0, 2, 3).reshape(dil, nb, BAND_BLOCK, H, hd)

    qr, kr, vr = to_res(q), to_res(k), to_res(v)

    def with_prev(t):
        prev = jnp.concatenate([jnp.zeros_like(t[:, :1]), t[:, :-1]], axis=1)
        return jnp.concatenate([prev, t], axis=2)

    kc, vc = with_prev(kr), with_prev(vr)
    scores = jnp.einsum('rnqhd,rnkhd->rnhqk', qr, kc).astype(jnp.float32) * ATTN_SCALE
    qi = jnp.arange(BAND_BLOCK)
    kj = jnp.arange(2 * BAND_BLOCK)
    dist = qi[:, None] + BAND_BLOCK - kj[None, :]
    kpos = jnp.arange(nb)[:, None] * BAND_BLOCK - BAND_BLOCK + kj[None, :]
    mask = ((dist >= 0) & (dist <= reach))[None] & (kpos >= 0)[:, None, :]
    scores = jnp.where(mask[None, :, None], scores, -jnp.inf)
    m = scores.max(axis=-1)
    p = jnp.exp(scores - m[..., None])
    den = p.sum(axis=-1)
    num = jnp.einsum('rnhqk,rnkhd->rnqhd', p, vc.astype(jnp.float32))
    m_t = m.transpose(0, 1, 3, 2)
    den_t = den.transpose(0, 1, 3, 2)
    o = num / den_t[..., None]

    def from_res(t):
        t = t.reshape((dil, L) + t.shape[3:])
        t = jnp.swapaxes(t, 0, 1)
        return t.reshape((s_pad,) + t.shape[2:])[:S]

    return from_res(o), from_res(m_t), from_res(den_t)

def mixer_dilated(h, w_qkv, q_gain, k_gain, w_o, cos, sin):
    B, S, _ = h.shape
    qkv = (h @ w_qkv).reshape(B, S, 3, N_DIL, N_HEADS, HEAD_DIM)
    q = apply_partial_rope(rmsnorm(qkv[:, :, 0], q_gain[:, None, :]), cos, sin)
    k = apply_partial_rope(rmsnorm(qkv[:, :, 1], k_gain[:, None, :]), cos, sin)
    v = qkv[:, :, 2]

    def one_sequence(args):
        qb, kb, vb = args
        outs, maxes, dens = [], [], []
        for g, (window, dil) in enumerate(DILATED_PAIRS):
            o, m, d = band_attention(qb[:, g], kb[:, g], vb[:, g], dil, window)
            outs.append(o)
            maxes.append(m)
            dens.append(d)
        o = jnp.stack(outs)
        m = jnp.stack(maxes)
        d = jnp.stack(dens)
        wgt = d * jnp.exp(m - m.max(axis=0, keepdims=True))
        wgt = wgt / wgt.sum(axis=0, keepdims=True)
        return jnp.einsum('gsh,gshd->shd', wgt, o)

    attn = lax.map(one_sequence, (q, k, v))
    return attn.reshape(B, S, N_HEADS * HEAD_DIM).astype(h.dtype) @ w_o

def mixer_moba(h, w_qkv, q_gain, k_gain, w_o, cos, sin):
    B, S, _ = h.shape
    qkv = (h @ w_qkv).reshape(B, S, 3, N_HEADS, HEAD_DIM)
    q = apply_partial_rope(rmsnorm(qkv[:, :, 0], q_gain), cos, sin)
    k = apply_partial_rope(rmsnorm(qkv[:, :, 1], k_gain), cos, sin)
    v = qkv[:, :, 2]
    s_pad = -(-S // MOBA_BLOCK) * MOBA_BLOCK
    nblk = s_pad // MOBA_BLOCK
    n_chunk = s_pad // MOBA_QCHUNK
    topk = min(MOBA_TOPK, nblk)

    def to_bhsd(t):
        return jnp.pad(t, ((0, 0), (0, s_pad - S), (0, 0), (0, 0))).transpose(0, 2, 1, 3)

    q, k, v = to_bhsd(q), to_bhsd(k), to_bhsd(v)
    k_blocks = k.reshape(B, N_HEADS, nblk, MOBA_BLOCK, HEAD_DIM)
    v_blocks = v.reshape(B, N_HEADS, nblk, MOBA_BLOCK, HEAD_DIM)
    k_mean = k_blocks.astype(jnp.float32).mean(axis=3)
    gate = jnp.einsum('bhsd,bhnd->bhsn', q.astype(jnp.float32), k_mean)
    own_blk = jnp.arange(s_pad) // MOBA_BLOCK
    fully_past = jnp.arange(nblk)[None, :] < own_blk[:, None]
    gate = jnp.where(fully_past, gate, -jnp.inf)
    _, sel = lax.top_k(gate, topk)

    def to_chunks(t):
        t = t.reshape(B, N_HEADS, n_chunk, MOBA_QCHUNK, t.shape[-1])
        return t.transpose(0, 2, 1, 3, 4).reshape(B * n_chunk, N_HEADS, MOBA_QCHUNK, t.shape[-1])

    q_chunks = to_chunks(q)
    sel_chunks = to_chunks(sel)
    chunk_ids = jnp.arange(B * n_chunk, dtype=jnp.int32)
    n_sel = topk * MOBA_BLOCK

    def one_chunk(args):
        qc, selc, cid = args
        b = cid // n_chunk
        c = cid % n_chunk
        kb = k_blocks[b]
        vb = v_blocks[b]
        qpos = c * MOBA_QCHUNK + jnp.arange(MOBA_QCHUNK)
        ob = (c * MOBA_QCHUNK) // MOBA_BLOCK
        h_idx = jnp.arange(N_HEADS)[:, None, None]
        k_sel = kb[h_idx, selc]
        v_sel = vb[h_idx, selc]
        s_sel = jnp.einsum('hqd,hqnkd->hqnk', qc, k_sel).astype(jnp.float32) * ATTN_SCALE
        valid = jnp.arange(topk) < ob
        s_sel = jnp.where(valid[None, None, :, None], s_sel, -jnp.inf)
        s_sel = s_sel.reshape(N_HEADS, MOBA_QCHUNK, n_sel)
        k_own = lax.dynamic_index_in_dim(kb, ob, axis=1, keepdims=False)
        v_own = lax.dynamic_index_in_dim(vb, ob, axis=1, keepdims=False)
        s_own = jnp.einsum('hqd,hkd->hqk', qc, k_own).astype(jnp.float32) * ATTN_SCALE
        kpos = ob * MOBA_BLOCK + jnp.arange(MOBA_BLOCK)
        s_own = jnp.where((kpos[None, :] <= qpos[:, None])[None], s_own, -jnp.inf)
        p = jax.nn.softmax(jnp.concatenate([s_sel, s_own], axis=-1), axis=-1).astype(v_sel.dtype)
        o = jnp.einsum('hqn,hqnd->hqd', p[..., :n_sel],
                       v_sel.reshape(N_HEADS, MOBA_QCHUNK, n_sel, HEAD_DIM))
        return o + jnp.einsum('hqk,hkd->hqd', p[..., n_sel:], v_own)

    out = lax.map(one_chunk, (q_chunks, sel_chunks, chunk_ids))
    out = out.reshape(B, n_chunk, N_HEADS, MOBA_QCHUNK, HEAD_DIM).transpose(0, 1, 3, 2, 4)
    out = out.reshape(B, s_pad, N_HEADS * HEAD_DIM)[:, :S]
    return out.astype(h.dtype) @ w_o

def conv_ffn(h, w_up, conv_w, conv_b, w_down):
    S = h.shape[1]
    u = h @ w_up
    up = jnp.pad(u, ((0, 0), (CONV_WIDTH - 1, 0), (0, 0)))
    uc = conv_b + sum(conv_w[j] * up[:, j:j + S] for j in range(CONV_WIDTH))
    gate, val = uc[..., :D_FF], uc[..., D_FF:]
    return (jax.nn.silu(gate) * val) @ w_down

def first_inputs(seed: int = 0) -> dict:
    key = jax.random.key(seed)
    ks = jax.random.split(key, 16)
    hd_all = N_HEADS * HEAD_DIM

    def w(k, shape, fan_in):
        return jax.random.normal(k, shape, jnp.float32) * fan_in ** -0.5

    def gain(k, shape):
        return 1.0 + 0.1 * jax.random.normal(k, shape, jnp.float32)

    return {
        'x': jax.random.normal(ks[0], (BATCH, SEQ, D_MODEL), jnp.float32),
        'attn_norm': gain(ks[1], (DEPTH, D_MODEL)),
        'a_w_qkv': w(ks[2], (N_LAYERS_A, D_MODEL, 3 * N_DIL * hd_all), D_MODEL),
        'a_q_norm': gain(ks[3], (N_LAYERS_A, N_DIL, HEAD_DIM)),
        'a_k_norm': gain(ks[4], (N_LAYERS_A, N_DIL, HEAD_DIM)),
        'a_w_o': w(ks[5], (N_LAYERS_A, hd_all, D_MODEL), hd_all),
        'b_w_qkv': w(ks[6], (N_LAYERS_B, D_MODEL, 3 * hd_all), D_MODEL),
        'b_q_norm': gain(ks[7], (N_LAYERS_B, HEAD_DIM)),
        'b_k_norm': gain(ks[8], (N_LAYERS_B, HEAD_DIM)),
        'b_w_o': w(ks[9], (N_LAYERS_B, hd_all, D_MODEL), hd_all),
        'ffn_norm': gain(ks[10], (DEPTH, D_MODEL)),
        'ffn_w_up': w(ks[11], (DEPTH, D_MODEL, 2 * D_FF), D_MODEL),
        'ffn_conv_w': w(ks[12], (DEPTH, CONV_WIDTH, 2 * D_FF), CONV_WIDTH),
        'ffn_conv_b': 0.01 * jax.random.normal(ks[13], (DEPTH, 2 * D_FF), jnp.float32),
        'ffn_w_down': w(ks[14], (DEPTH, D_FF, D_MODEL), D_FF),
    }

def first_block(x, attn_norm, a_w_qkv, a_q_norm, a_k_norm, a_w_o,
              b_w_qkv, b_q_norm, b_k_norm, b_w_o,
              ffn_norm, ffn_w_up, ffn_conv_w, ffn_conv_b, ffn_w_down):
    cos, sin = rope_tables(x.shape[1])
    for i in range(DEPTH):
        hn = rmsnorm(x, attn_norm[i])
        if i % 2 == 0:
            j = i // 2
            x = x + mixer_dilated(hn, a_w_qkv[j], a_q_norm[j], a_k_norm[j], a_w_o[j], cos, sin)
        else:
            j = i // 2
            x = x + mixer_moba(hn, b_w_qkv[j], b_q_norm[j], b_k_norm[j], b_w_o[j], cos, sin)
        hn = rmsnorm(x, ffn_norm[i])
        x = x + conv_ffn(hn, ffn_w_up[i], ffn_conv_w[i], ffn_conv_b[i], ffn_w_down[i])
    return x


DEPTH_2 = 1

DN_HEADS = 4
DN_HEAD_DIM = 128
DN_WIDTH = DN_HEADS * DN_HEAD_DIM
DN_QKV_WIDTH = 3 * DN_WIDTH
DN_CONV = 4
DN_CHUNK = 64
SWA_HEADS = 8
SWA_KV_HEADS = 2
SWA_HEAD_DIM = 64
SWA_GROUP = SWA_HEADS // SWA_KV_HEADS
SWA_WIDTH = SWA_HEADS * SWA_HEAD_DIM
SWA_KV_WIDTH = SWA_KV_HEADS * SWA_HEAD_DIM
WINDOW = 128
SWA_BLOCK = 128
REL_BUCKETS = 32
REL_MAX_DIST = 128
N_BRANCHES = 2
D_FF_2 = ((8 * D_MODEL // 3 + 255) // 256) * 256
D_IN = DN_QKV_WIDTH + DN_WIDTH + 2 * DN_HEADS + SWA_WIDTH + 2 * SWA_KV_WIDTH + N_BRANCHES * D_MODEL
EPS = 1e-6


def rms_norm(x, gain):
    xf = x.astype(jnp.float32)
    y = xf * lax.rsqrt(jnp.mean(xf * xf, axis=-1, keepdims=True) + EPS)
    return (y * gain.astype(jnp.float32)).astype(x.dtype)

def l2_norm(x):
    xf = x.astype(jnp.float32)
    return xf * lax.rsqrt(jnp.sum(xf * xf, axis=-1, keepdims=True) + EPS)

def causal_dwconv(x, w):
    k = w.shape[0]
    return lax.conv_general_dilated(
        x, w[:, None, :], window_strides=(1,), padding=((k - 1, 0),),
        dimension_numbers=("NWC", "WIO", "NWC"), feature_group_count=x.shape[-1])

def chunk_gated_delta_rule(q, k, v, g, beta):
    B, S, H, DK = q.shape
    DV = v.shape[-1]
    C = DN_CHUNK
    NC = S // C
    q = q * (DK ** -0.5)

    def to_chunks(t):
        return t.reshape(B, NC, C, H, t.shape[-1]).transpose(0, 3, 1, 2, 4)

    qc, kc, vc = to_chunks(q), to_chunks(k), to_chunks(v)
    gc = jnp.cumsum(g.reshape(B, NC, C, H).transpose(0, 3, 1, 2), axis=-1)
    bc = beta.reshape(B, NC, C, H).transpose(0, 3, 1, 2)[..., None]
    k_beta = kc * bc
    v_beta = vc * bc

    idx = jnp.arange(C)
    lower_incl = idx[:, None] >= idx[None, :]
    strict_lower = idx[:, None] > idx[None, :]
    decay = jnp.exp(jnp.where(lower_incl, gc[..., :, None] - gc[..., None, :], -jnp.inf))

    a_mat = jnp.where(strict_lower, jnp.einsum("bhncd,bhnsd->bhncs", k_beta, kc) * decay, 0.0)
    lhs = a_mat + jnp.eye(C, dtype=a_mat.dtype)
    rhs = jnp.concatenate([v_beta, k_beta * jnp.exp(gc)[..., None]], axis=-1)
    sol = lax.linalg.triangular_solve(lhs, rhs, left_side=True, lower=True, unit_diagonal=True)
    u, w = sol[..., :DV], sol[..., DV:]
    qk = jnp.einsum("bhncd,bhnsd->bhncs", qc, kc) * decay

    def step(state, inp):
        q_i, k_i, u_i, w_i, g_i, qk_i = inp
        v_new = u_i - jnp.einsum("bhck,bhkv->bhcv", w_i, state)
        o_i = (jnp.einsum("bhck,bhkv->bhcv", q_i * jnp.exp(g_i)[..., None], state)
               + jnp.einsum("bhcs,bhsv->bhcv", qk_i, v_new))
        g_last = g_i[..., -1]
        k_dec = k_i * jnp.exp(g_last[..., None] - g_i)[..., None]
        state = state * jnp.exp(g_last)[..., None, None] + jnp.einsum("bhck,bhcv->bhkv", k_dec, v_new)
        return state, o_i

    xs = tuple(jnp.moveaxis(t, 2, 0) for t in (qc, kc, u, w, gc, qk))
    state0 = jnp.zeros((B, H, DK, DV), jnp.float32)
    _, o = lax.scan(step, state0, xs)
    return o.transpose(1, 0, 3, 2, 4).reshape(B, S, H, DV)

def gated_deltanet_branch(qkv, z, b_raw, a_raw, conv_w, a_log, dt_bias, out_gain):
    B, S, _ = qkv.shape
    qkv = jax.nn.silu(causal_dwconv(qkv, conv_w))
    q, k, v = jnp.split(qkv, 3, axis=-1)
    q = l2_norm(q.reshape(B, S, DN_HEADS, DN_HEAD_DIM))
    k = l2_norm(k.reshape(B, S, DN_HEADS, DN_HEAD_DIM))
    v = v.reshape(B, S, DN_HEADS, DN_HEAD_DIM).astype(jnp.float32)
    beta = jax.nn.sigmoid(b_raw.astype(jnp.float32))
    g = -jnp.exp(a_log.astype(jnp.float32)) * jax.nn.softplus(a_raw.astype(jnp.float32) + dt_bias.astype(jnp.float32))
    o = chunk_gated_delta_rule(q, k, v, g, beta)
    o = rms_norm(o, out_gain) * jax.nn.silu(z.reshape(B, S, DN_HEADS, DN_HEAD_DIM).astype(jnp.float32))
    return o.reshape(B, S, DN_WIDTH).astype(qkv.dtype)

def t5_causal_bucket(dist):
    n = jnp.maximum(dist, 0)
    max_exact = REL_BUCKETS // 2
    nf = jnp.maximum(n, 1).astype(jnp.float32)
    large = max_exact + (jnp.log(nf / max_exact) / math.log(REL_MAX_DIST / max_exact)
                         * (REL_BUCKETS - max_exact)).astype(jnp.int32)
    large = jnp.minimum(large, REL_BUCKETS - 1)
    return jnp.where(n < max_exact, n, large)

def sliding_window_branch(q, k, v, q_gain, k_gain, sinks, rel_bias):
    B, S, _ = q.shape
    NB = S // SWA_BLOCK
    q = rms_norm(q.reshape(B, S, SWA_HEADS, SWA_HEAD_DIM), q_gain)
    k = rms_norm(k.reshape(B, S, SWA_KV_HEADS, SWA_HEAD_DIM), k_gain)
    v = v.reshape(B, S, SWA_KV_HEADS, SWA_HEAD_DIM)
    qb = q.reshape(B, NB, SWA_BLOCK, SWA_KV_HEADS, SWA_GROUP, SWA_HEAD_DIM).astype(jnp.float32)

    def band(t):
        tp = jnp.pad(t, ((0, 0), (SWA_BLOCK, 0), (0, 0), (0, 0)))
        tp = tp.reshape(B, NB + 1, SWA_BLOCK, SWA_KV_HEADS, SWA_HEAD_DIM)
        return jnp.concatenate([tp[:, :-1], tp[:, 1:]], axis=2).astype(jnp.float32)

    kb, vb = band(k), band(v)
    logits = jnp.einsum("bnqkgd,bnskd->bnkgqs", qb, kb) * (SWA_HEAD_DIM ** -0.5)

    qi = jnp.arange(SWA_BLOCK)[:, None]
    kj = jnp.arange(2 * SWA_BLOCK)[None, :]
    dist = SWA_BLOCK + qi - kj
    in_window = (dist >= 0) & (dist < WINDOW)
    key_pos = (jnp.arange(NB)[:, None] - 1) * SWA_BLOCK + jnp.arange(2 * SWA_BLOCK)[None, :]
    mask = in_window[None, :, :] & (key_pos >= 0)[:, None, :]

    bias = rel_bias.astype(jnp.float32)[t5_causal_bucket(dist)]
    bias = bias.transpose(2, 0, 1).reshape(SWA_KV_HEADS, SWA_GROUP, SWA_BLOCK, 2 * SWA_BLOCK)
    logits = jnp.where(mask[None, :, None, None], logits + bias, -jnp.inf)

    sink = sinks.astype(jnp.float32).reshape(SWA_KV_HEADS, SWA_GROUP)[None, None, :, :, None, None]
    m = jnp.maximum(jnp.max(logits, axis=-1, keepdims=True), sink)
    p = jnp.exp(logits - m)
    denom = jnp.sum(p, axis=-1, keepdims=True) + jnp.exp(sink - m)
    out = jnp.einsum("bnkgqs,bnskd->bnqkgd", p / denom, vb)
    return out.reshape(B, S, SWA_WIDTH).astype(q.dtype)

def split_combined(p):
    sizes = (DN_QKV_WIDTH, DN_WIDTH, DN_HEADS, DN_HEADS, SWA_WIDTH, SWA_KV_WIDTH, SWA_KV_WIDTH,
             N_BRANCHES * D_MODEL)
    return jnp.split(p, np.cumsum(sizes)[:-1].tolist(), axis=-1)

def second_inputs(seed: int = 0) -> dict:
    key = jax.random.key(seed)
    ks = jax.random.split(key, 20)
    f32 = jnp.float32
    L = DEPTH_2

    def nrm(k, shape, scale):
        return jax.random.normal(k, shape, f32) * scale

    dt = jnp.exp(jax.random.uniform(ks[5], (L, DN_HEADS), f32, math.log(1e-3), math.log(1e-1)))
    return {
        "x": nrm(ks[0], (BATCH, SEQ, D_MODEL), 1.0),
        "attn_norm": 1.0 + nrm(ks[1], (L, D_MODEL), 0.02),
        "w_in": nrm(ks[2], (L, D_MODEL, D_IN), D_MODEL ** -0.5),
        "dn_conv": nrm(ks[3], (L, DN_CONV, DN_QKV_WIDTH), DN_CONV ** -0.5),
        "dn_a_log": jnp.log(jax.random.uniform(ks[4], (L, DN_HEADS), f32, 1.0, 16.0)),
        "dn_dt_bias": dt + jnp.log(-jnp.expm1(-dt)),
        "dn_out_norm": 1.0 + nrm(ks[6], (L, DN_HEAD_DIM), 0.02),
        "swa_q_norm": 1.0 + nrm(ks[7], (L, SWA_HEAD_DIM), 0.02),
        "swa_k_norm": 1.0 + nrm(ks[8], (L, SWA_HEAD_DIM), 0.02),
        "swa_sinks": nrm(ks[9], (L, SWA_HEADS), 0.5),
        "rel_bias": nrm(ks[10], (REL_BUCKETS, SWA_HEADS), 0.1),
        "w_branch_dn": nrm(ks[11], (L, DN_WIDTH, D_MODEL), DN_WIDTH ** -0.5),
        "w_branch_swa": nrm(ks[12], (L, SWA_WIDTH, D_MODEL), SWA_WIDTH ** -0.5),
        "w_out": nrm(ks[13], (L, D_MODEL, D_MODEL), D_MODEL ** -0.5),
        "ffn_norm": 1.0 + nrm(ks[14], (L, D_MODEL), 0.02),
        "w_gate": nrm(ks[15], (L, D_MODEL, D_FF_2), D_MODEL ** -0.5),
        "w_up": nrm(ks[16], (L, D_MODEL, D_FF_2), D_MODEL ** -0.5),
        "w_down": nrm(ks[17], (L, D_FF_2, D_MODEL), D_FF_2 ** -0.5),
    }

def second_block(x, attn_norm, w_in, dn_conv, dn_a_log, dn_dt_bias, dn_out_norm, swa_q_norm,
              swa_k_norm, swa_sinks, rel_bias, w_branch_dn, w_branch_swa, w_out, ffn_norm,
              w_gate, w_up, w_down):
    B, S, _ = x.shape
    for l in range(DEPTH_2):
        h = rms_norm(x, attn_norm[l])
        proj = h @ w_in[l]
        dn_qkv, dn_z, dn_b, dn_a, sq, sk, sv, gate_raw = split_combined(proj)
        y_dn = gated_deltanet_branch(dn_qkv, dn_z, dn_b, dn_a, dn_conv[l], dn_a_log[l],
                                     dn_dt_bias[l], dn_out_norm[l])
        y_swa = sliding_window_branch(sq, sk, sv, swa_q_norm[l], swa_k_norm[l], swa_sinks[l], rel_bias)
        gates = jax.nn.sigmoid(gate_raw.astype(jnp.float32)).astype(x.dtype)
        gates = gates.reshape(B, S, N_BRANCHES, D_MODEL)
        merged = gates[:, :, 0] * (y_dn @ w_branch_dn[l]) + gates[:, :, 1] * (y_swa @ w_branch_swa[l])
        x = x + merged @ w_out[l]
        h2 = rms_norm(x, ffn_norm[l])
        x = x + (jax.nn.silu(h2 @ w_gate[l]) * (h2 @ w_up[l])) @ w_down[l]
    return x


def setup_inputs(seed=0):
    out = dict(first_inputs(seed))
    for name, value in second_inputs(seed + 1).items():
        if name != "x":
            out[name + "_2"] = value
    return out


def reference(
    x, attn_norm, a_w_qkv, a_q_norm, a_k_norm, a_w_o, b_w_qkv, b_q_norm, b_k_norm, b_w_o,
    ffn_norm, ffn_w_up, ffn_conv_w, ffn_conv_b, ffn_w_down, attn_norm_2, w_in_2, dn_conv_2,
    dn_a_log_2, dn_dt_bias_2, dn_out_norm_2, swa_q_norm_2, swa_k_norm_2, swa_sinks_2,
    rel_bias_2, w_branch_dn_2, w_branch_swa_2, w_out_2, ffn_norm_2, w_gate_2, w_up_2, w_down_2,
):
    x = first_block(
        x, attn_norm, a_w_qkv, a_q_norm, a_k_norm, a_w_o, b_w_qkv, b_q_norm, b_k_norm, b_w_o,
        ffn_norm, ffn_w_up, ffn_conv_w, ffn_conv_b, ffn_w_down,
    )
    return second_block(
        x, attn_norm_2, w_in_2, dn_conv_2, dn_a_log_2, dn_dt_bias_2, dn_out_norm_2,
        swa_q_norm_2, swa_k_norm_2, swa_sinks_2, rel_bias_2, w_branch_dn_2, w_branch_swa_2,
        w_out_2, ffn_norm_2, w_gate_2, w_up_2, w_down_2,
    )


_drawn_inputs = setup_inputs


def setup_inputs(seed=0):
    import zlib

    import numpy as np

    out = dict(_drawn_inputs(seed))
    spreads = {}
    factors = {'b_q_norm': 3.065,
     'b_k_norm': 3.444,
     'ffn_conv_b': 4.621,
     'attn_norm_2': 6.417,
     'dn_out_norm_2': 8.0,
     'swa_q_norm_2': 8.0,
     'swa_k_norm_2': 8.0,
     'swa_sinks_2': 200.0,
     'rel_bias_2': 24.108,
     'ffn_norm_2': 16.852}
    for name, (base, spread) in spreads.items():
        noise = np.random.default_rng([zlib.crc32(name.encode()), seed]).standard_normal(out[name].shape)
        drawn = base * np.exp(spread * noise) if base else spread * noise
        out[name] = __import__('jax').numpy.asarray(drawn.astype(out[name].dtype))
    for name, factor in factors.items():
        out[name] = (out[name] * factor).astype(out[name].dtype)
    return out
```

```python
from collections import deque
from contextlib import ExitStack

import numpy as np

import concourse.bass as bass
from concourse import mybir

F32 = mybir.dt.float32
F32R = mybir.dt.float32r
ALU = mybir.AluOpType
ACT = mybir.ActivationFunctionType
AX = mybir.AxisListType

P = 128
S = 256
D = 1024
FF = 2816
EPS = 1e-6
NEG = -1.0e30
BIG = 3.0e38
SCALE = 0.125
RAW, RING = 3, 3
DILATED = ((128, 1), (512, 4), (2048, 16))
DN0, Z0, BA0, SQ0, SK0, SV0, GT0 = 0, 1536, 2048, 2056, 2568, 2696, 2824


def r(a, b):
    return np.arange(a, b)


def cat(*a):
    return np.concatenate(a)


def plan():
    out = []

    def unit(name, layer, cols):
        for k in (0, 4):
            out.append((name, layer, list(range(k, k + 4)), cols))

    def wide(name, layer, n):
        for k in range(0, n, 2):
            out.append((name, layer, [k, k + 1], r(0, D)))

    def ffn(up, layer, off_gate, off_val, down):
        for i in range(12):
            if i < 11:
                g = r(256 * i, 256 * i + 256)
                if isinstance(up, tuple):
                    for k in (0, 4):
                        out.append((up, layer, list(range(k, k + 4)), g))
                else:
                    unit(up, layer, cat(g + off_gate, g + off_val))
            if i > 0:
                out.append((down, layer, [2 * i - 2, 2 * i - 1], r(0, D)))

    for half in range(2):
        for g in range(3):
            unit("a_w_qkv", 0, r(0, 512) + 6144 + 1024 * g + 512 * half)
        for hg in (2 * half, 2 * half + 1):
            for g in range(3):
                q = r(0, 256) + 1024 * g + 256 * hg
                unit("a_w_qkv", 0, cat(q, q + 3072))
    wide("a_w_o", 0, 8)
    ffn("ffn_w_up", 0, 0, FF, "ffn_w_down")
    for half in range(2):
        unit("b_w_qkv", 0, r(0, 512) + 2048 + 512 * half)
        for hg in (2 * half, 2 * half + 1):
            q = r(0, 256) + 256 * hg
            unit("b_w_qkv", 0, cat(q, q + 1024))
    wide("b_w_o", 0, 8)
    ffn("ffn_w_up", 1, 0, FF, "ffn_w_down")
    for i in range(3):
        unit("w_in_2", 0, r(0, 512) + DN0 + 512 * i)
    unit("w_in_2", 0, cat(r(BA0, BA0 + 8), r(SK0, SK0 + 256)))
    unit("w_in_2", 0, r(Z0, Z0 + 512))
    for i in range(4):
        unit("w_in_2", 0, r(0, 512) + GT0 + 512 * i)
    pairs = cat(*[cat(r(64 * h, 64 * h + 64), r(64 * h + 256, 64 * h + 320)) for h in range(4)])
    unit("w_in_2", 0, pairs + SQ0)
    wide("w_branch_dn_2", 0, 4)
    wide("w_branch_swa_2", 0, 4)
    wide("w_out_2", 0, 8)
    ffn(("w_gate_2", "w_up_2"), 0, 0, 0, "w_down_2")
    return out


class Table:

    def __init__(self):
        self.at, self.n = {}, 0

    def add(self, name, n):
        self.at[name] = (self.n, n)
        self.n += n


def tables():
    keep, a, b, c = Table(), Table(), Table(), Table()
    keep.add("ident", 128)
    for name in ("an0", "an1", "fn0", "fn1", "an2", "fn2"):
        keep.add(name, 8)
    keep.add("cw0", 176)
    keep.add("cw1", 176)
    keep.add("dnw", 48)
    keep.add("mhalf", 16)
    a.add("cos", 32)
    a.add("sin", 32)
    a.add("gain", 384)
    a.add("m0", 384)
    a.add("m1", 768)
    b.add("cos", 32)
    b.add("sin", 32)
    b.add("gain", 128)
    b.add("m0", 128)
    b.add("m1", 256)
    c.add("gq", 64)
    c.add("gk", 64)
    c.add("gout", 128)
    c.add("alog", 4)
    c.add("dtb", 4)
    c.add("sink", 8)
    c.add("relb", 8)
    c.add("cum", 128)
    c.add("blk", 128)
    c.add("sel", 256)
    c.add("strict", 128)
    c.add("inct", 128)
    c.add("lev", 768)
    c.add("lev0t", 128)
    return {"keep": keep, "a": a, "b": b, "c": c}


def constants():
    f = np.float32
    t = np.arange(S)
    inv = (500000.0 ** (-np.arange(0, 16, 2) / 16.0)).astype(f)
    ang = t.astype(f)[:, None] * inv[None, :]
    cos, sin = np.cos(ang), np.sin(ang)
    rope_c = np.concatenate([cos, cos], 1).reshape(2, P, 16).transpose(1, 0, 2).reshape(P, 32)
    rope_s = np.concatenate([-sin, sin], 1).reshape(2, P, 16).transpose(1, 0, 2).reshape(P, 32)
    dist = t[:, None] - t[None, :]

    def add(ok):
        return np.where(ok, 0.0, NEG).astype(f)

    dil = [add((dist >= 0) & (dist % d == 0) & (dist <= w)) for w, d in DILATED]
    causal = add(dist >= 0)
    i = np.arange(P)
    same = i[:, None] // 64 == i[None, :] // 64
    lev = []
    for n in range(6):
        b = 1 << n
        lev.append((i[None, :] // (2 * b) == i[:, None] // (2 * b)) & (i[None, :] % (2 * b) >= b) & (i[:, None] % (2 * b) < b))
    x = np.arange(384)
    sd = 255 - x
    ok = (sd >= 0) & (sd < 128)
    n = np.maximum(sd, 0)
    nf = np.maximum(n, 1).astype(f)
    large = np.minimum(16 + (np.log(nf / f(16)) / f(np.log(8.0)) * f(16)).astype(np.int32), 31)
    bucket = np.where(n < 16, n, large)
    onehot = np.where(ok[None, :] & (bucket[None, :] == np.arange(32)[:, None]), 8.0, 0.0).astype(f)
    return {
        "ident": np.eye(P, dtype=f),
        "cos": rope_c.astype(f), "sin": rope_s.astype(f),
        "am0": np.concatenate([m[:P, :P] for m in dil], 1), "am1": np.concatenate([m[P:] for m in dil], 1),
        "bm0": causal[:P, :P], "bm1": causal[P:],
        "cum": (same & (i[:, None] <= i[None, :])).astype(f),
        "blk": same.astype(f),
        "sel": np.concatenate([np.repeat((i[:, None] // 64 == c), P, 1) for c in range(2)], 1).astype(f),
        "strict": (same & (i[:, None] > i[None, :])).astype(f),
        "inct": (same & (i[:, None] <= i[None, :])).astype(f),
        "lev": np.concatenate(lev, 1).astype(f), "lev0t": lev[0].T.astype(f),
        "onehot": onehot,
        "edge": np.broadcast_to(add(ok)[None, :], (P, 384)),
    }



def build(nc, dram, out):
    slots = plan()
    tabs = tables()
    with ExitStack() as ctx:
        def sb(name, shape, dt=F32):
            return ctx.enter_context(nc.sbuf_tensor(name, shape, dt))

        ENG = ("sync", "tensor", "vector", "scalar", "gpsimd")
        queue = {e: [] for e in ENG}
        count = {e: 0 for e in ENG}
        seen = {e: {} for e in ENG}
        done = {e: ctx.enter_context(nc.semaphore("done_" + e)) for e in ENG}
        handle = dict(tensor=nc.tensor, vector=nc.vector, scalar=nc.scalar, gpsimd=nc.gpsimd, sync=nc.sync)

        def op(e, fn, waits=(), inc=True):
            for s, v, name in waits:
                if seen[e].get(name, 0) < v:
                    seen[e][name] = v
                    queue[e].append(lambda h=handle[e], s=s, v=v: h.wait_ge(s, v))
            if inc:
                count[e] += 1
                queue[e].append(lambda: fn(handle[e]).then_inc(done[e], 1))
            else:
                queue[e].append(lambda: fn(handle[e]))
            return (done[e], count[e], e)

        dmas = {}

        def dma(e, dst, src, sem, waits=()):
            if sem not in dmas:
                dmas[sem] = [ctx.enter_context(nc.semaphore("dma_" + sem)), 0]
            dmas[sem][1] += 16
            s, v = dmas[sem]
            for w, wv, name in waits:
                if seen[e].get(name, 0) < wv:
                    seen[e][name] = wv
                    queue[e].append(lambda h=handle[e], w=w, wv=wv: h.wait_ge(w, wv))
            queue[e].append(lambda: handle[e].dma_start(dst, src).then_inc(s, 16))
            return (s, v, "dma_" + sem)

        def V(fn, *w):
            return op("vector", fn, w)

        def A(fn, *w):
            return op("scalar", fn, w)

        def G(fn, *w):
            return op("gpsimd", fn, w)

        def MM(o, l, rh, start, stop, *w, inc=False):
            return op("tensor", lambda e: e.matmul(o, l, rh, start=start, stop=stop, skip_group_check=True), w, inc)

        def TR(o, i, idn, *w, inc=False):
            return op("tensor", lambda e: e.transpose(o, i, idn), w, inc)

        x = sb("x", [P, 2, D])
        XH, XL = sb("XH", [P, 8, S], F32R), sb("XL", [P, 8, S], F32R)
        HH, HL = sb("HH", [P, 8, S], F32R), sb("HL", [P, 8, S], F32R)
        raw = [sb(f"raw{i}", [P, 2048]) for i in range(RAW)]
        wh = [sb(f"wh{i}", [P, 2048], F32R) for i in range(RING)]
        wl = [sb(f"wl{i}", [P, 2048], F32R) for i in range(RING)]
        keep = sb("keep", [P, tabs["keep"].n])
        small = sb("small", [P, 192])
        NAR = 23300
        arena = sb("arena", [P, NAR])
        ps = ctx.enter_context(nc.psum_tensor("ps", [P, 4096], F32))
        bank = [ps[:, 512 * i:512 * i + 512] for i in range(8)]
        scr = nc.dram_tensor("scr", (P * 8 * 384,), F32).ap()

        def kt(name):
            o, n = tabs["keep"].at[name]
            return keep[:, o:o + n]

        ident = kt("ident")
        used = [0]

        def ar(n):
            o = used[0]
            used[0] += n
            assert used[0] <= NAR, used
            return arena[:, o:o + n]

        def bc(ap, shape):
            return ap.to_broadcast(shape)

        raw_tok, hi_tok, lo_tok, use_tok = {}, {}, {}, {}

        def width(n):
            _, _, ks, cols = slots[n]
            c = len(cols) * (2 if isinstance(slots[n][0], tuple) else 1)
            return len(ks), c

        def load(n):
            if n >= len(slots):
                return
            k, c = width(n)
            w = (hi_tok[n - RAW], lo_tok[n - RAW]) if n >= RAW else ()
            raw_tok[n] = dma("sync", raw[n % RAW][:, 0:k * c], dram["w"][n, :, 0:k * c], f"raw{n % RAW}", w)

        def split(n):
            if n >= len(slots):
                return
            k, c = width(n)
            a, h, l = raw[n % RAW][:, 0:k * c], wh[n % RING][:, 0:k * c], wl[n % RING][:, 0:k * c]
            free = (use_tok[n - RING],) if n >= RING else ()
            hi_tok[n] = A(lambda e: e.activation(h, a, ACT.Copy), raw_tok[n], *free)
            lo_tok[n] = V(lambda e: e.tensor_tensor(l, a, h.bitcast(F32), ALU.subtract), raw_tok[n], hi_tok[n], *free)
            load(n + RAW)

        cur = [0]
        hiq, loq = deque(), deque()

        def step(q):
            while q:
                try:
                    next(q[0])
                    return
                except StopIteration:
                    q.popleft()

        def pump():
            step(hiq)
            step(loq)

        def drain():
            while hiq or loq:
                step(hiq)
                step(loq)

        def rsqrt(v, n, eps, *w):
            t = V(lambda e: e.tensor_scalar(v, v, eps, None, ALU.add), *w)
            return G(lambda e: e.tensor_tensor(v, v, kt("mhalf")[:, 0:n], ALU.pow), t, keep_tok[0])

        keep_tok = [None]

        def slot_views(n):
            k, c = width(n)
            v = lambda t: t[:, 0:k * c].rearrange("p (k c) -> p k c", k=k)
            return v(wh[n % RING]), v(wl[n % RING]), (hi_tok[n], lo_tok[n])

        def next_slot():
            n = cur[0]
            cur[0] += 1
            return n

        def after(n, tok):
            use_tok[n] = tok
            split(n + RING - 1)

        def unit_tok(outs, act, free, nslots=2):
            tok = None
            for si in range(nslots):
                n = next_slot()
                h, l, w = slot_views(n)
                ah, al, aw = act
                c = width(n)[1]
                for tt in range(2):
                    ww = list(w) + list(aw) + (list(free) if si == 0 else [])
                    for j in range(4):
                        kk = 4 * si + j
                        t = slice(tt * P, tt * P + P)
                        first, last = kk == 0, kk == 4 * nslots - 1
                        o = outs[tt][:, 0:c]
                        MM(o, ah[:, kk, t], h[:, j, :], first, False, *ww)
                        MM(o, ah[:, kk, t], l[:, j, :], False, False)
                        tok = MM(o, al[:, kk, t], h[:, j, :], False, last, inc=(j == 3))
                        ww = []
                    if tt == 0:
                        pump()
                after(n, tok)
                pump()
            return tok

        def unit_chan(outs, act, free, pumps=True):
            tok = None
            for si in range(2):
                n = next_slot()
                h, l, w = slot_views(n)
                ah, al, aw = act
                for nt in range(4):
                    ww = list(w) + list(aw) + (list(free) if si == 0 else [])
                    o = outs[nt // 2][:, (nt % 2) * S:(nt % 2) * S + S]
                    cols = slice(nt * P, nt * P + P)
                    for j in range(4):
                        kk = 4 * si + j
                        MM(o, h[:, j, cols], ah[:, kk, :], kk == 0 and nt % 2 == 0, False, *ww)
                        MM(o, h[:, j, cols], al[:, kk, :], False, False)
                        tok = MM(o, l[:, j, cols], ah[:, kk, :], False, kk == 7, inc=(j == 3))
                        ww = []
                    if nt == 1:
                        pump()
                after(n, tok)
                pump()
            return tok

        def slot_wide(act, kbase, first, last, free):
            n = next_slot()
            h, l, w = slot_views(n)
            ah, al, aw = act
            tok = None
            for tt in range(2):
                for hf in range(2):
                    o = bank[2 * tt + hf]
                    ww = list(w) + list(aw) + list(free)
                    c = slice(512 * hf, 512 * hf + 512)
                    for j in range(2):
                        t = slice(tt * P, tt * P + P)
                        MM(o, ah[:, kbase + j, t], h[:, j, c], first and j == 0, False, *ww)
                        MM(o, ah[:, kbase + j, t], l[:, j, c], False, False)
                        tok = MM(o, al[:, kbase + j, t], h[:, j, c], False, last and j == 1, inc=(j == 1))
                        ww = []
                if tt == 0:
                    pump()
            after(n, tok)
            pump()
            return tok

        pt_free = [[], []]
        g_free = [[], []]
        ffn_free = [[], []]
        pt_n = [0]

        def pt():
            i = pt_n[0] % 2
            pt_n[0] += 1
            return i, bank[6 + i]

        def fence():
            now = [(done[e], count[e], e) for e in ("tensor", "vector", "scalar", "gpsimd")]
            for e in ("tensor", "vector", "scalar", "gpsimd"):
                for s, v, name in now:
                    if name != e and v and seen[e].get(name, 0) < v:
                        seen[e][name] = v
                        queue[e].append(lambda h=handle[e], s=s, v=v: h.wait_ge(s, v))
            return now

        def transposed(src, kts, gains, dh, dl, base, waits, wfree=()):
            toks = []
            for i0 in range(0, len(kts), 2):
                i, b = pt()
                grp = kts[i0:i0 + 2]
                w = list(waits) + pt_free[i]
                for gi, k in enumerate(grp):
                    for tt in range(2):
                        t = TR(b[:, gi * S + tt * P:gi * S + tt * P + P], src[:, tt, k * P:k * P + P], ident, *w,
                               inc=(gi == len(grp) - 1 and tt == 1))
                        w = []
                if gains is None:
                    n = len(grp)
                    o = slice(base + i0, base + i0 + n)
                    v = b[:, 0:n * S].rearrange("p (k t) -> p k t", k=n)
                    th = A(lambda e, o=o, v=v: e.activation(dh[:, o, :], v, ACT.Copy), t, *wfree)
                    tl = V(lambda e, o=o, v=v: e.tensor_tensor(dl[:, o, :], v, dh[:, o, :].bitcast(F32), ALU.subtract), t, th, *wfree)
                    toks += [th, tl]
                else:
                    each = [(b[:, gi * S:gi * S + S], base + i0 + gi, gains[:, k:k + 1]) for gi, k in enumerate(grp)]
                    for v, o, g in each:
                        th = A(lambda e, o=o, v=v, g=g: e.activation(dh[:, o, :], v, ACT.Copy, scale=g), t, *wfree)
                    for v, o, g in each:
                        tl = V(lambda e, o=o, v=v, g=g: e.scalar_tensor_tensor(dl[:, o, :], v, g, dh[:, o, :].bitcast(F32),
                                                                              ALU.mult, ALU.subtract), t, th, *wfree)
                    toks += [th, tl]
                pt_free[i] = [th, tl]
            return toks

        xs = arena[:, NAR - 2048:NAR].rearrange("p (t d) -> p t d", t=2)

        def norm_x(gains, xt):
            tn = []
            for tt in range(2):
                ss = small[:, tt:tt + 1]
                t = A(lambda e, tt=tt, ss=ss: e.activation(xs[:, tt, :], x[:, tt, :], ACT.Square, accum_out=ss), *xt[tt])
                t = rsqrt(ss, 1, D * EPS, t)
                tn.append(V(lambda e, tt=tt, rs=ss: e.tensor_scalar(xs[:, tt, :], x[:, tt, :], rs, 32.0, ALU.mult, ALU.mult), t))
            return transposed(xs, list(range(8)), gains, XH, XL, 0, tn)

        def residual(tok):
            out = []
            for tt in range(2):
                o, i = x[:, tt, :], ps[:, 1024 * tt:1024 * tt + 1024]
                out.append([V(lambda e, o=o, i=i: e.tensor_tensor(o, i, o, ALU.add), tok)])
            g_free[0] = g_free[1] = [out[0][0], out[1][0]]
            return out

        s_ps = ps[:, 2048:2048 + 768]
        s_free = [[]]

        def attention(items, Pb, PTb, st, finish):
            N = len(items)
            state = {}

            def scores(i):
                it = items[i]
                w = list(it["deps"]) + s_free[0]
                o = 0
                for si, (q, k, n) in enumerate(it["segs"]):
                    t = MM(s_ps[:, o:o + n], q, k, True, True, *w, inc=(si == len(it["segs"]) - 1))
                    w = []
                    o += n
                p = Pb[i % 2][:, 0:o]
                nm, den = st[:, i % 2:i % 2 + 1], st[:, 2 + i % 2:3 + i % 2]
                back = [state[i - 2]["pt"]] if i >= 2 else []
                m = it["mask"]
                t1 = V(lambda e: e.tensor_tensor_reduce(p, s_ps[:, 0:o], m, -SCALE, BIG, ALU.add, ALU.min, nm), t, *back)
                s_free[0] = [t1]
                if it.get("sink") is not None:
                    sk, es = it["sink"], st[:, 4 + i % 2:5 + i % 2]
                    t1 = V(lambda e: e.tensor_tensor(nm, nm, sk, ALU.min), t1)
                t2 = A(lambda e: e.activation(p, p, ACT.Exp, bias=nm, scale=-1.0, accum_out=den), t1)
                if it.get("sink") is not None:
                    t3 = A(lambda e: e.activation(es, sk, ACT.Exp, bias=nm, scale=-1.0), t1, *back)
                    t3 = V(lambda e: e.tensor_tensor(den, den, es, ALU.add), t2, t3)
                else:
                    t3 = t2
                rd = st[:, 6 + i % 4:7 + i % 4]
                tr = V(lambda e: e.reciprocal(rd, den), t3, *([state[i - 4]["on"]] if i >= 4 else []))
                state[i] = {"p": t2, "rd": tr, "n": o}

            def turn(i):
                s = state[i]
                nb = s["n"] // P
                toks = []
                for b0 in range(0, nb, 3):
                    bn = min(3, nb - b0)
                    j, bk = pt()
                    w = [s["p"]] + pt_free[j]
                    for b in range(bn):
                        t = TR(bk[:, b * P:b * P + P], Pb[i % 2][:, (b0 + b) * P:(b0 + b) * P + P], ident, *w, inc=(b == bn - 1))
                        w = []
                    o, c = PTb[i % 2][:, b0 * P:(b0 + bn) * P], bk[:, 0:bn * P]
                    back = [state[i - 2]["pv"]] if i >= 2 else []
                    if b0 == 0:
                        t2 = A(lambda e, o=o, c=c: e.activation(o, c, ACT.Copy), t, *back)
                    else:
                        t2 = V(lambda e, o=o, c=c: e.tensor_copy(o, c), t, *back)
                    pt_free[j] = [t2]
                    toks.append(t2)
                s["pt"] = t
                s["ptc"] = toks

            def pv(i):
                s, it = state[i], items[i]
                j, bk = pt()
                o = bk[:, 0:64]
                w = s["ptc"] + pt_free[j] + list(it["deps"])
                nb = s["n"] // P
                for b in range(nb):
                    t = MM(o, PTb[i % 2][:, b * P:b * P + P], it["v"][b], b == 0, b == nb - 1, *w, inc=(b == nb - 1))
                    w = []
                s["pv"] = t
                rd, dst = st[:, 6 + i % 4:7 + i % 4], it["dst"]
                s["on"] = V(lambda e: e.tensor_scalar(dst, o, rd, None, ALU.mult), t, s["rd"], *it.get("dfree", ()))
                pt_free[j] = [s["on"]]

            for i in range(N + 2):
                if i < N:
                    scores(i)
                if 1 <= i <= N:
                    turn(i - 1)
                if i >= 2:
                    pv(i - 2)
                yield
            yield from finish([state[i]["on"] for i in range(N)])

        v3 = lambda ap: ap.rearrange("p (h d) -> p h d", d=64)
        v4 = lambda ap: ap.rearrange("p (s h d) -> p s h d", s=2, d=64)

        def load_table(name, waits):
            n = tabs[name].n
            t = ar(n)
            tok = dma("gpsimd", t, dram[name], "tab_" + name, waits)
            return (lambda k: t[:, tabs[name].at[k][0]:tabs[name].at[k][0] + tabs[name].at[k][1]]), tok

        def rope_tables(tab, ng, GC, GS, dep):
            cosv = tab("cos").rearrange("p (t d) -> p t d", t=2)
            sinv = tab("sin").rearrange("p (t d) -> p t d", t=2)
            gv = tab("gain").rearrange("p (g s d) -> p g s d", g=ng, s=2)
            last = None
            for g in range(ng):
                for tt in range(2):
                    cb = bc(cosv[:, tt, :].unsqueeze(1), [P, 2, 16])
                    s0 = bc(sinv[:, tt, 0:8].unsqueeze(1), [P, 2, 8])
                    s1 = bc(sinv[:, tt, 8:16].unsqueeze(1), [P, 2, 8])
                    gg, cc, ss = gv[:, g], GC[:, g, tt], GS[:, g, tt]
                    V(lambda e, gg=gg, cc=cc: e.tensor_scalar(cc[:, :, 16:64], gg[:, :, 16:64], 8.0, None, ALU.mult), dep)
                    V(lambda e, gg=gg, cc=cc, cb=cb: e.scalar_tensor_tensor(cc[:, :, 0:16], gg[:, :, 0:16], 8.0, cb, ALU.mult, ALU.mult))
                    V(lambda e, gg=gg, ss=ss, s0=s0: e.scalar_tensor_tensor(ss[:, :, 0:8], gg[:, :, 8:16], 8.0, s0, ALU.mult, ALU.mult))
                    last = V(lambda e, gg=gg, ss=ss, s1=s1: e.scalar_tensor_tensor(ss[:, :, 8:16], gg[:, :, 0:8], 8.0, s1, ALU.mult, ALU.mult))
            return last

        def mixer(tabname, ng, norm_gain, xt):
            used[0] = 0
            now = fence()
            tab, tdep = load_table(tabname, now)
            GC = ar(ng * 256).rearrange("p (g t s d) -> p g t s d", g=ng, t=2, s=2)
            GS = ar(ng * 64).rearrange("p (g t s d) -> p g t s d", g=ng, t=2, s=2)
            Vt = ar(2 * ng * D).rearrange("p (t g n) -> p t g n", t=2, g=ng)
            qkT = [ar(ng * 1024).rearrange("p (g c t) -> p g c t", g=ng, c=4) for _ in range(2)]
            sq, qn, tp, ssb = [ar(512), ar(512)], [ar(512), ar(512)], [ar(128), ar(128)], small[:, 16:32]
            Pb, PTb = [ar(256 * ng), ar(256 * ng)], [ar(256 * ng), ar(256 * ng)]
            att = [ar(512).rearrange("p (t d) -> p t d", t=2) for _ in range(2)]
            assert used[0] <= NAR - 2048, used
            act = (XH, XL, norm_x(norm_gain, xt))
            td = rope_tables(tab, ng, GC, GS, tdep)
            vt, att_free, qk_free, out_tok = [], [[], []], [[], []], {}
            rope_done, turned = [[], []], [[], []]
            un = [0]

            def heads(pair, tok, g, dst, wfree, qt):
                free, fin = [], []
                for tt in range(2):
                    src, a, b = bank[2 * pair + tt], sq[tt], qn[tt]
                    ss = ssb[:, 8 * tt:8 * tt + 8]
                    t1 = A(lambda e, a=a, src=src: e.activation(a, src, ACT.Square), tok, *turned[tt])
                    t2 = V(lambda e, a=a, ss=ss: e.tensor_reduce(ss, v3(a), AX.X, ALU.add), t1)
                    t3 = rsqrt(ss, 8, 64 * EPS, t2)
                    rs = bc(ss.unsqueeze(2), [P, 8, 64])
                    t4 = V(lambda e, b=b, src=src, rs=rs: e.tensor_tensor(v3(b), v3(src), rs, ALU.mult), t3, tok, *rope_done[tt])
                    free += [t1, t4]
                    av, bv = v4(a), v4(b)
                    tpv = tp[tt].rearrange("p (s h d) -> p s h d", s=2, d=16)
                    gs = [bc(GS[:, g, tt, :, 8 * q:8 * q + 8].unsqueeze(2), [P, 2, 4, 8]) for q in range(2)]
                    t5 = t4
                    for s in range(2):
                        gc = bc(GC[:, g, tt, s].unsqueeze(1), [P, 4, 64])
                        t5 = V(lambda e, s=s, av=av, bv=bv, gc=gc: e.tensor_tensor(av[:, s], bv[:, s], gc, ALU.mult), t4, td)
                    for s in range(2):
                        for q in range(2):
                            o, i, m = tpv[:, s, :, 8 * q:8 * q + 8], bv[:, s, :, 8 - 8 * q:16 - 8 * q], gs[q][:, s]
                            t6 = G(lambda e, o=o, i=i, m=m: e.tensor_tensor(o, i, m, ALU.mult), t4, td)
                    tq = tp[tt].rearrange("p (h d) -> p h d", d=16)
                    t7 = G(lambda e, a=a, tq=tq: e.tensor_tensor(v3(a)[:, :, 0:16], v3(a)[:, :, 0:16], tq, ALU.add), t5, t6)
                    rope_done[tt] = [t7]
                    fin.append(t7)
                g_free[pair] = free

                def rest():
                    yield
                    for tt in range(2):
                        i, b = pt()
                        w = [fin[tt]] + pt_free[i]
                        for c in range(4):
                            t = TR(b[:, c * P:c * P + P], sq[tt][:, c * P:c * P + P], ident, *w, inc=(c == 3))
                            w = []
                        turned[tt] = [t]
                        o, v = dst[:, :, tt * P:tt * P + P], b.rearrange("p (c t) -> p c t", c=4)
                        t = A(lambda e, o=o, v=v: e.activation(o, v, ACT.Copy), t, *wfree)
                        pt_free[i] = [t]
                        qt.append(t)
                        yield
                hiq.append(rest())

            def finish_for(hg):
                def finish(toks):
                    qk_free[hg % 2] = toks
                    out_tok[hg] = transposed(att[hg % 2], [0, 1], None, HH, HL, 2 * hg, toks)
                    att_free[hg % 2] = [(done["tensor"], count["tensor"], "tensor")]
                    yield
                return finish

            def group(hg, qt):
                while len(qt) < 2 * ng:
                    yield
                items = []
                T = qkT[hg % 2]
                for h in range(4):
                    pr, row = h // 2, slice(64 * (h % 2), 64 * (h % 2) + 64)
                    hc = 64 * (4 * hg + h)
                    for tt in range(2):
                        n = P * (tt + 1)
                        segs = [(T[row, g, pr, tt * P:tt * P + P], T[row, g, 2 + pr, 0:n], n) for g in range(ng)]
                        v = [Vt[:, b, g, hc:hc + 64] for g in range(ng) for b in range(tt + 1)]
                        items.append(dict(segs=segs, mask=tab(f"m{tt}"), v=v, deps=qt + vt + [tdep],
                                          dst=att[hg % 2][:, tt, 64 * h:64 * h + 64], dfree=att_free[hg % 2]))
                yield from attention(items, Pb, PTb, small[:, 48:64], finish_for(hg))

            for half in range(2):
                for g in range(ng):
                    pair = un[0] % 2
                    un[0] += 1
                    tok = unit_tok([bank[2 * pair], bank[2 * pair + 1]], act, g_free[pair])
                    toks = []
                    for tt in range(2):
                        o, b = Vt[:, tt, g, 512 * half:512 * half + 512], bank[2 * pair + tt]
                        toks.append(A(lambda e, o=o, b=b: e.activation(o, b, ACT.Copy), tok))
                    vt += toks
                    g_free[pair] = toks
                for hg in (2 * half, 2 * half + 1):
                    while hg >= 2 and (hg - 2) not in out_tok:
                        pump()
                    qt = []
                    for g in range(ng):
                        pair = un[0] % 2
                        un[0] += 1
                        tok = unit_tok([bank[2 * pair], bank[2 * pair + 1]], act, g_free[pair])
                        heads(pair, tok, g, qkT[hg % 2][:, g], qk_free[hg % 2], qt)
                    loq.append(group(hg, qt))
            for i in range(4):
                while i not in out_tok:
                    pump()
                tok = slot_wide((HH, HL, out_tok[i]), 2 * i, i == 0, i == 3, g_free[0] + g_free[1])
            drain()
            return residual(tok)

        def so_far(*engines):
            return [(done[e], count[e], e) for e in engines]

        def ffn(cw, norm_gain, xt):
            used[0] = 0
            Y = [ar(1024).rearrange("p (n t) -> p n t", n=4) for _ in range(2)]
            act = (XH, XL, norm_x(norm_gain, xt))
            base = so_far("vector", "scalar")
            free, hfree, htok, yfree = [base, base], {}, {}, [base, base]
            for i in range(12):
                if i < 11:
                    p = i % 2
                    y = Y[p]
                    bb = [bank[4 + 2 * p], bank[5 + 2 * p]]
                    tok = unit_chan(bb, act, free[p])
                    u = [bb[n // 2][:, (n % 2) * S:(n % 2) * S + S] for n in range(4)]
                    if cw is None:
                        t = A(lambda e, y=y, b=bb[0]: e.activation(y[:, 0:2, :].rearrange("p n t -> p (n t)"), b, ACT.Silu), tok, *yfree[p])
                        t2 = V(lambda e, y=y, b=bb[1]: e.tensor_tensor(y[:, 2:4, :].rearrange("p n t -> p (n t)"),
                                                                       y[:, 0:2, :].rearrange("p n t -> p (n t)"), b, ALU.mult), t, tok, *yfree[p])
                        free[p] = [t, t2]
                    else:
                        ts, t1 = [], []
                        each = []
                        for n in range(4):
                            ch = 2 * i + n if n < 2 else 22 + 2 * i + n - 2
                            w = cw[:, 4 * ch:4 * ch + 4]
                            yn, un = y[:, n, :], u[n]
                            each.append((n, w, yn, un))
                            t1.append(A(lambda e, yn=yn, un=un, w=w: e.activation(yn, un, ACT.Identity, bias=w[:, 3:4], scale=w[:, 2:3]), tok, *yfree[p]))
                        for n, w, yn, un in each:
                            t2 = V(lambda e, yn=yn, un=un, w=w: e.scalar_tensor_tensor(yn[:, 1:S], un[:, 0:S - 1], w[:, 1:2], yn[:, 1:S], ALU.mult, ALU.add), t1[n | 1], tok)
                            t3 = V(lambda e, yn=yn, un=un, w=w: e.scalar_tensor_tensor(yn[:, 2:S], un[:, 0:S - 2], w[:, 0:1], yn[:, 2:S], ALU.mult, ALU.add), t2)
                            ts.append(t3)
                        free[p] = [t1[3], t3]
                        t = A(lambda e, y=y: e.activation(y[:, 0:2, :], y[:, 0:2, :], ACT.Silu), ts[1])
                        t2 = V(lambda e, y=y: e.tensor_tensor(y[:, 2:4, :], y[:, 0:2, :], y[:, 2:4, :], ALU.mult), t, ts[3])
                    k = (2 * i) % 8
                    back = [hfree[i - 4]] if i >= 4 else []
                    th = A(lambda e, y=y, k=k: e.activation(HH[:, k:k + 2, :], y[:, 2:4, :], ACT.Copy), t2, *back)
                    tl = V(lambda e, y=y, k=k: e.tensor_tensor(HL[:, k:k + 2, :], y[:, 2:4, :], HH[:, k:k + 2, :].bitcast(F32), ALU.subtract), th, *back)
                    htok[i] = [th, tl]
                    yfree[p] = [th, tl]
                if i > 0:
                    tok = slot_wide((HH, HL, htok[i - 1]), (2 * (i - 1)) % 8, i == 1, i == 11, g_free[0] + g_free[1])
                    hfree[i - 1] = tok
            return residual(tok)

        rot = [0]
        b45_free = [[], []]

        def rot4():
            i = rot[0] % 4
            rot[0] += 1
            return (b45_free, i) if i < 2 else (pt_free, i - 2), bank[4 + i]

        def third(norm_gain, xt):
            used[0] = 0
            now = fence()
            tab, tdep = load_table("c", now)
            R1, R2 = ar(3072), ar(3072).rearrange("p (t n) -> p t n", t=2)
            KQ = ar(2048)
            QE = ar(1024).rearrange("p (h t) -> p h t", h=4)
            KBE = ar(1024).rearrange("p (t n) -> p t n", t=2)
            Ar, AT = [ar(1024).rearrange("p (t n) -> p t n", t=2) for _ in range(2)]
            Er = ar(1024).rearrange("p (t n) -> p t n", t=2)
            QKT = ar(1024)
            ST = ar(512)
            kT = ar(256)
            SKV = ar(512).rearrange("p (t n) -> p t n", t=2)
            Z = ar(1024).rearrange("p (t n) -> p t n", t=2)
            GA = ar(4096)
            XT = R1.rearrange("p (c t) -> p c t", c=12)
            KQv = KQ.rearrange("p (t h n) -> p t h n", t=2, h=4)
            T = KQ[:, 0:1024].rearrange("p (t n) -> p t n", t=2)
            TT = KQ[:, 1024:2048].rearrange("p (t n) -> p t n", t=2)
            ARG, DM, DT = [R1[:, 1024 * i:1024 * i + 1024].rearrange("p (t n) -> p t n", t=2) for i in range(3)]
            QKTv = QKT.rearrange("p (t n) -> p t n", t=2)
            B = R1[:, 0:2048].rearrange("p (h n) -> p h n", h=8)
            h4 = lambda ap: ap.rearrange("p (h d) -> p h d", h=4)
            sv = lambda a, n: small[:, a:a + n]
            beta, gg, gc, eg, dk, bg = [sv(64 + 8 * i, 8) for i in range(6)]
            gl, egl, t8a, t8b, t8c, rsn = sv(112, 8), sv(120, 16), sv(136, 8), sv(144, 8), sv(152, 8), sv(160, 16)
            nsink, gq8, gk8 = sv(176, 8), tab("gq"), tab("gk")
            act = (XH, XL, norm_x(norm_gain, xt))

            onehot, edge = QKT[0:32, 0:384], QKT[:, 384:768]
            td1 = dma("gpsimd", onehot, dram["onehot"], "tab_onehot", now)
            td2 = dma("gpsimd", edge, dram["edge"], "tab_edge", now)
            relb = GA[0:32, 3072:4096].rearrange("p (h n) -> p h n", h=8)
            t = V(lambda e: e.tensor_copy(relb, bc(tab("relb")[0:32, :].unsqueeze(2), [32, 8, P])), tdep, *act[2])
            for q in (gq8, gk8):
                tg8 = V(lambda e, q=q: e.tensor_scalar(q, q, 8.0, None, ALU.mult), tdep)
            tg8 = V(lambda e: e.tensor_scalar(nsink, tab("sink"), -1.0, None, ALU.mult), tdep)
            rows = []
            for h in range(8):
                i, b = pt()
                tm = MM(b[:, 0:384], relb[:, h, :], onehot, True, True, t, td1, *pt_free[i], inc=True)
                tv = V(lambda e, h=h, b=b: e.tensor_tensor(GA[:, 384 * h:384 * h + 384], b[:, 0:384], edge, ALU.add), tm, td2, *act[2])
                pt_free[i] = [tv]
                rows.append(tv)
            ts = dma("gpsimd", scr.rearrange("(p n) -> p n", p=P), GA[:, 0:3072], "scr_out", rows)
            un = [0]

            def unit(chan=False):
                pair = un[0] % 2
                un[0] += 1
                outs = [bank[2 * pair], bank[2 * pair + 1]]
                return pair, outs, (unit_chan if chan else unit_tok)(outs, act, g_free[pair])

            silu_tok = {}
            dnw = kt("dnw")
            for i in range(3):
                pair, outs, tok = unit(True)
                each = [(4 * i + n, dnw[:, 16 * i + 4 * n:16 * i + 4 * n + 4], XT[:, 4 * i + n, :], outs[n // 2][:, (n % 2) * S:(n % 2) * S + S])
                        for n in range(4)]
                ta = [A(lambda e, yn=yn, u=u, w=w: e.activation(yn, u, ACT.Copy, scale=w[:, 3:4]), tok) for _, w, yn, u in each]
                for n, (ch, w, yn, u) in enumerate(each):
                    tv = ta[n | 1]
                    for d in range(1, 4):
                        tv = V(lambda e, yn=yn, u=u, w=w, d=d: e.scalar_tensor_tensor(yn[:, d:S], u[:, 0:S - d], w[:, 3 - d:4 - d], yn[:, d:S],
                                                                                     ALU.mult, ALU.add), tv, tok)
                    silu_tok[ch] = A(lambda e, yn=yn: e.activation(yn, yn, ACT.Silu), tv)
                g_free[pair] = [ta[3], tv]

            pair, outs, tok = unit()
            raws = []
            for tt in range(2):
                raw_row = Er[:, tt, 0:264]
                tok1 = A(lambda e, raw_row=raw_row, b=outs[tt]: e.activation(raw_row, b[:, 0:264], ACT.Copy), tok)
                raws.append(tok1)
                b, a = raw_row[:, 0:4], raw_row[:, 4:8]
                o = slice(4 * tt, 4 * tt + 4)
                t = A(lambda e, b=b, o=o: e.activation(t8a[:, o], b, ACT.Exp, scale=-1.0), tok1)
                t = V(lambda e, o=o: e.tensor_scalar(t8a[:, o], t8a[:, o], 1.0, None, ALU.add), t)
                tbeta = V(lambda e, o=o: e.reciprocal(beta[:, o], t8a[:, o]), t)
                z, q, u1 = gc[:, o], t8b[:, o], t8c[:, o]
                t = V(lambda e, z=z, a=a: e.tensor_tensor(z, a, tab("dtb"), ALU.add), tok1, tdep)
                tabs_ = V(lambda e, z=z, q=q: e.scalar_tensor_tensor(q, z, -1.0, z, ALU.mult, ALU.max), t)
                t = A(lambda e, q=q: e.activation(q, q, ACT.Exp, scale=-1.0), tabs_)
                t1 = V(lambda e, q=q, u1=u1: e.tensor_scalar(u1, q, 1.0, None, ALU.add), t)
                l = gg[:, o]
                tl = A(lambda e, l=l, u1=u1: e.activation(l, u1, ACT.Ln), t1)
                ri = t8a[:, o]
                t2 = V(lambda e, ri=ri, u1=u1: e.reciprocal(ri, u1), t1, tbeta)
                t3 = V(lambda e, u1=u1: e.tensor_scalar(u1, u1, -1.0, None, ALU.add), t2, tl)
                t3 = V(lambda e, q=q, u1=u1: e.tensor_tensor(q, q, u1, ALU.subtract), t3)
                t3 = V(lambda e, q=q, ri=ri: e.tensor_tensor(q, q, ri, ALU.mult), t3, t2)
                t3 = V(lambda e, l=l, q=q: e.tensor_tensor(l, l, q, ALU.add), t3, tl)
                t3 = V(lambda e, l=l, z=z: e.scalar_tensor_tensor(l, z, 0.0, l, ALU.max, ALU.add), t3)
                ta = A(lambda e, q=q: e.activation(q, tab("alog"), ACT.Exp), t3)
                tgg = V(lambda e, l=l, q=q: e.scalar_tensor_tensor(l, l, -1.0, q, ALU.mult, ALU.mult), ta, t3)
                k, kk = raw_row[:, 8:136], SKV[:, tt, 0:128]
                sk = rsn[:, 2 * tt:2 * tt + 2]
                k2 = lambda ap: ap.rearrange("p (h d) -> p h d", h=2)
                t = A(lambda e, k=k, kk=kk: e.activation(kk, k, ACT.Square), tok1)
                t = V(lambda e, kk=kk, sk=sk: e.tensor_reduce(sk, k2(kk), AX.X, ALU.add), t)
                t = rsqrt(sk, 2, 64 * EPS, t)
                t = V(lambda e, k=k, kk=kk, sk=sk: e.tensor_tensor(k2(kk), k2(k), bc(sk.unsqueeze(2), [P, 2, 64]), ALU.mult), t)
                tk = V(lambda e, kk=kk: e.tensor_tensor(k2(kk), k2(kk), bc(gk8.unsqueeze(1), [P, 2, 64]), ALU.mult), t, tg8)
                tvv = A(lambda e, b=raw_row, tt=tt: e.activation(SKV[:, tt, 128:256], b[:, 136:264], ACT.Copy), tok1)
            g_free[pair] = raws
            kdep, vdep, gdep, bdep = tk, tvv, tgg, tbeta

            st = {}

            def solve():
                vt = {}
                for tt in range(2):
                    for gidx in range(3):
                        i, b = pt()
                        w = [silu_tok[4 * gidx + 3]] + pt_free[i]
                        for c in range(4):
                            t = TR(b[:, c * P:c * P + P], XT[:, 4 * gidx + c, tt * P:tt * P + P], ident, *w, inc=(c == 3))
                            w = []
                        o = R2[:, tt, 512 * gidx:512 * gidx + 512]
                        if gidx == 2:
                            tb = bc(beta[:, 4 * tt:4 * tt + 4].unsqueeze(2), [P, 4, P])
                            tc = V(lambda e, o=o, b=b, tb=tb: e.tensor_tensor(h4(o), h4(b), tb, ALU.mult), t, bdep)
                        else:
                            s4 = rsn[:, 4 + 4 * (gidx + 2 * (tt % 2)) - 4:4 + 4 * (gidx + 2 * (tt % 2))]
                            ta = A(lambda e, b=b, tt=tt: e.activation(Er[:, tt, :], b, ACT.Square), t, *([vt["sum"]] if "sum" in vt else []), kdep, vdep, gdep, bdep)
                            t1 = V(lambda e, tt=tt, s4=s4: e.tensor_reduce(s4, h4(Er[:, tt, :]), AX.X, ALU.add), ta, kdep)
                            vt["sum"] = t1
                            t1 = rsqrt(s4, 4, EPS, t1)
                            if gidx == 0:
                                t1 = V(lambda e, s4=s4: e.tensor_scalar(s4, s4, float(P) ** -0.5, None, ALU.mult), t1)
                            tb = bc(s4.unsqueeze(2), [P, 4, P])
                            tc = V(lambda e, o=o, b=b, tb=tb: e.tensor_tensor(h4(o), h4(b), tb, ALU.mult), t1, t)
                        pt_free[i] = [tc]
                        vt[(tt, gidx)] = tc
                        yield
                (fl, fi), b = rot4()
                w = [gdep, tdep] + fl[fi]
                for tt in range(2):
                    gs = gg[:, 4 * tt:4 * tt + 4]
                    MM(b[:, 4 * tt:4 * tt + 4], tab("cum"), gs, True, True, *w)
                    MM(b[:, 8 + 4 * tt:12 + 4 * tt], tab("blk"), gs, True, True)
                    for c in range(2):
                        o = 16 + 8 * tt + 4 * c
                        t = MM(b[:, o:o + 4], tab("sel")[:, P * c:P * c + P], gs, True, True, inc=True)
                    w = []
                t1 = V(lambda e, b=b: e.tensor_copy(gc, b[:, 0:8]), t)
                t2 = V(lambda e, b=b: e.tensor_tensor(gl, b[:, 8:16], gc, ALU.subtract), t, t1)
                t3 = A(lambda e, b=b: e.activation(egl, b[:, 16:32], ACT.Exp), t2)
                t4 = A(lambda e: e.activation(eg, gc, ACT.Exp), t1)
                t5 = A(lambda e: e.activation(dk, gl, ACT.Exp), t2)
                t6 = V(lambda e: e.tensor_tensor(bg, beta, eg, ALU.mult), t4, bdep)
                fl[fi] = [t2, t3]
                st["egl"] = t3
                tkq = {}
                for tt in range(2):
                    for which, col in ((1, 0), (0, P)):
                        i, b = pt()
                        w = [vt[(tt, which)]] + pt_free[i]
                        for h in range(4):
                            t = TR(b[:, h * P:h * P + P], R2[:, tt, 512 * which + P * h:512 * which + P * h + P], ident, *w, inc=(h == 3))
                            w = []
                        o, v = KQv[:, tt, :, col:col + P], h4(b)
                        t = A(lambda e, o=o, v=v: e.activation(o, v, ACT.Copy), t)
                        pt_free[i] = [t]
                        tkq[(tt, which)] = t
                    yield
                    q, k = R2[:, tt, 0:512], R2[:, tt, 512:1024]
                    cs = slice(4 * tt, 4 * tt + 4)
                    f = lambda s: bc(s[:, cs].unsqueeze(2), [P, 4, P])
                    tkbe = G(lambda e, tt=tt, k=k, s=f(bg): e.tensor_tensor(h4(KBE[:, tt, :]), h4(k), s, ALU.mult), vt[(tt, 1)], t6)
                    tkd = G(lambda e, k=k, s=f(dk): e.tensor_tensor(h4(k), h4(k), s, ALU.mult), tkbe, t5, tkq[(tt, 1)])
                    tqe = V(lambda e, q=q, s=f(eg): e.tensor_tensor(h4(q), h4(q), s, ALU.mult), t4, tkq[(tt, 0)])
                    st[("kd", tt)] = tkd
                    st[("kbe", tt)] = tkbe
                    (fl, fi), b = rot4()
                    grow = ARG[:, tt, :]
                    gsrc = bc(gg[:, cs].unsqueeze(2), [P, 4, P])
                    t = G(lambda e, grow=grow, gsrc=gsrc: e.tensor_copy(h4(grow), gsrc), gdep, *[vt[(1, n)] for n in range(3)])
                    w = [t] + fl[fi]
                    for h in range(4):
                        t = MM(b[:, h * P:h * P + P], grow[:, h * P:h * P + P], tab("cum"), True, True, *w, inc=(h == 3))
                        w = []
                    t = V(lambda e, grow=grow, b=b, s=f(gc): e.tensor_tensor(h4(grow), s, h4(b), ALU.subtract), t, t1)
                    fl[fi] = [t]
                    d, dt = DM[:, tt, :], DT[:, tt, :]
                    ta = V(lambda e, d=d, grow=grow: e.tensor_scalar(d, grow, 0.0, None, ALU.min), t)
                    tb = V(lambda e, dt=dt, grow=grow: e.tensor_scalar(dt, grow, -1.0, 0.0, ALU.mult, ALU.min), t)
                    ta = A(lambda e, d=d: e.activation(d, d, ACT.Exp), ta)
                    tb = A(lambda e, dt=dt: e.activation(dt, dt, ACT.Exp), tb)
                    m1, m2 = bc(tab("strict").unsqueeze(1), [P, 4, P]), bc(tab("inct").unsqueeze(1), [P, 4, P])
                    ta = V(lambda e, d=d, m1=m1: e.tensor_tensor(h4(d), h4(d), m1, ALU.mult), ta)
                    ta = V(lambda e, d=d, s=f(beta): e.tensor_tensor(h4(d), h4(d), s, ALU.mult), ta)
                    tb = G(lambda e, dt=dt, m2=m2: e.tensor_tensor(h4(dt), h4(dt), m2, ALU.mult), tb)
                    yield
                    i, b = pt()
                    w = [tqe] + pt_free[i]
                    for h in range(4):
                        t = TR(b[:, h * P:h * P + P], q[:, h * P:h * P + P], ident, *w, inc=(h == 3))
                        w = []
                    o, v = QE[:, :, tt * P:tt * P + P], h4(b)
                    t = A(lambda e, o=o, v=v: e.activation(o, v, ACT.Copy), t)
                    pt_free[i] = [t]
                    st[("qe", tt)] = t
                    for hp in range(2):
                        (fl, fi), b = rot4()
                        w = [tkq[(tt, 0)], tkq[(tt, 1)]] + fl[fi]
                        for h in range(2):
                            kq = KQv[:, tt, 2 * hp + h, :]
                            t = MM(b[:, h * S:h * S + S], kq[:, 0:P], kq, True, True, *w, inc=(h == 1))
                            w = []
                        bv = b.rearrange("p (h n) -> p h n", h=2)
                        hs = slice(256 * hp, 256 * hp + 256)
                        v2 = lambda ap: ap.rearrange("p (h n) -> p h n", h=2)
                        tA = V(lambda e, tt=tt, hs=hs, bv=bv, d=d: e.tensor_tensor(v2(Ar[:, tt, hs]), bv[:, :, 0:P], v2(d[:, hs]), ALU.mult), t, ta)
                        tQ = V(lambda e, tt=tt, hs=hs, bv=bv, dt=dt: e.tensor_tensor(v2(QKTv[:, tt, hs]), bv[:, :, P:S], v2(dt[:, hs]), ALU.mult), t, tb)
                        fl[fi] = [tA, tQ]
                    st[("A", tt)] = tA
                    st["qk"] = tQ
                    yield
                lev = lambda n: bc(tab("lev")[:, P * n:P * n + P].unsqueeze(1), [P, 4, P])
                l0t, idb = bc(tab("lev0t").unsqueeze(1), [P, 4, P]), bc(ident.unsqueeze(1), [P, 4, P])
                tat, tT, tTT = {}, {}, {}
                for tt in range(2):
                    i, b = pt()
                    w = [st[("A", 0)], st[("A", 1)]] + pt_free[i]
                    for h in range(4):
                        t = TR(b[:, h * P:h * P + P], Ar[:, tt, h * P:h * P + P], ident, *w, inc=(h == 3))
                        w = []
                    t = A(lambda e, tt=tt, b=b: e.activation(AT[:, tt, :], b, ACT.Copy), t)
                    pt_free[i] = [t]
                    tat[tt] = t
                    a, q, qq = Ar[:, tt, :], T[:, tt, :], TT[:, tt, :]
                    t1 = V(lambda e, a=a, q=q: e.tensor_tensor(h4(q), h4(a), l0t, ALU.mult), st[("A", 1)], t)
                    tT[tt] = V(lambda e, q=q: e.tensor_tensor(h4(q), idb, h4(q), ALU.subtract), t1)
                    t1 = G(lambda e, tt=tt, qq=qq: e.tensor_tensor(h4(qq), h4(AT[:, tt, :]), lev(0), ALU.mult), t)
                    tTT[tt] = G(lambda e, qq=qq: e.tensor_tensor(h4(qq), idb, h4(qq), ALU.subtract), t1)
                    yield
                xfree, efree = {}, {}
                for n in range(1, 6):
                    tx = {}
                    for tt in range(2):
                        te = G(lambda e, tt=tt, n=n: e.tensor_tensor(h4(Er[:, tt, :]), h4(AT[:, tt, :]), lev(n), ALU.mult), tat[tt],
                               *efree.get(tt, []))
                        (fl, fi), b = rot4()
                        w = [te, tT[tt]] + fl[fi]
                        for h in range(4):
                            c = slice(h * P, h * P + P)
                            t = MM(b[:, c], Er[:, tt, c], T[:, tt, c], True, True, *w, inc=(h == 3))
                            w = []
                        efree[tt] = [t]
                        tx[tt] = A(lambda e, tt=tt, b=b: e.activation(Ar[:, tt, :], b, ACT.Copy), t, tT[tt], *xfree.get(tt, []))
                        fl[fi] = [tx[tt]]
                    yield
                    for tt in range(2):
                        (f1, i1), b1 = rot4()
                        (f2, i2), b2 = rot4()
                        w = [tx[tt], tTT[tt]] + f1[i1]
                        if n < 5:
                            for h in range(4):
                                c = slice(h * P, h * P + P)
                                t1 = MM(b1[:, c], TT[:, tt, c], Ar[:, tt, c], True, True, *w, inc=(h == 3))
                                w = []
                        w = w + f2[i2]
                        for h in range(4):
                            c = slice(h * P, h * P + P)
                            t2 = MM(b2[:, c], Ar[:, tt, c], TT[:, tt, c], True, True, *w, inc=(h == 3))
                            w = []
                        if n < 5:
                            tT[tt] = V(lambda e, tt=tt, b=b1: e.tensor_tensor(T[:, tt, :], T[:, tt, :], b, ALU.subtract), t1, t2)
                            f1[i1] = [tT[tt]]
                        tTT[tt] = V(lambda e, tt=tt, b=b2: e.tensor_tensor(TT[:, tt, :], TT[:, tt, :], b, ALU.subtract), t2, tTT[tt])
                        f2[i2] = [tTT[tt]]
                        xfree[tt] = [t2]
                    yield
                for tt in range(2):
                    (f1, i1), b1 = rot4()
                    (f2, i2), b2 = rot4()
                    w = [tTT[tt], vt[(tt, 2)]] + f1[i1]
                    u = R2[:, tt, 1024:1536]
                    for h in range(4):
                        c = slice(h * P, h * P + P)
                        t1 = MM(b1[:, c], TT[:, tt, c], u[:, c], True, True, *w, inc=(h == 3))
                        w = []
                    w = [st[("kbe", tt)]] + f2[i2]
                    for h in range(4):
                        c = slice(h * P, h * P + P)
                        t2 = MM(b2[:, c], KBE[:, tt, c], TT[:, tt, c], True, True, *w, inc=(h == 3))
                        w = []
                    st[("u", tt)] = V(lambda e, u=u, b=b1: e.tensor_copy(u, b), t1)
                    st[("w", tt)] = A(lambda e, tt=tt, b=b2: e.activation(Er[:, tt, :], b, ACT.Copy), t2, *efree[tt])
                    f1[i1], f2[i2] = [st[("u", tt)]], [st[("w", tt)]]
                    yield
                st["solved"] = True

            O = T

            def scan():
                tS = None
                ot = {}
                for n in range(4):
                    tt, ro = n // 2, 64 * (n % 2)
                    row = slice(ro, ro + 64)
                    u = R2[:, tt, 1024:1536]
                    k = R2[:, tt, 512:1024]
                    tv = st[("u", tt)]
                    if n:
                        i, b = pt()
                        w = [st[("w", tt)], tS] + pt_free[i]
                        for h in range(4):
                            c = slice(h * P, h * P + P)
                            t = MM(b[row, c], Er[:, tt, h * P + ro:h * P + ro + 64], ST[:, c], True, True, *w, inc=(h == 3))
                            w = []
                        tv = V(lambda e, u=u, b=b, row=row: e.tensor_tensor(u[row, :], u[row, :], b[row, :], ALU.subtract), t, tv)
                        pt_free[i] = [tv]
                        yield
                    if n < 3:
                        i, b = pt()
                        w = [tv, st[("kd", tt)]] + pt_free[i]
                        for h in range(4):
                            c = slice(h * P, h * P + P)
                            t = MM(b[:, c], k[row, c], u[row, c], True, True, *w, inc=(h == 3))
                            w = []
                        old = ot.get("read", [])
                    i2, b2 = pt()
                    w = [tv, st["qk"], st[("qe", tt)]] + pt_free[i2]
                    for h in range(4):
                        c = slice(h * P, h * P + P)
                        if n:
                            MM(b2[row, c], QE[:, h, tt * P + ro:tt * P + ro + 64], ST[:, c], True, False, *w)
                            w = []
                        t2 = MM(b2[row, c], QKTv[row, tt, h * P + ro:h * P + ro + 64], u[row, c], n == 0, True, *w, inc=(h == 3))
                        w = []
                    if n < 3:
                        if n == 0:
                            tS = V(lambda e, b=b: e.tensor_copy(ST, b), t)
                        else:
                            for h in range(4):
                                c = slice(h * P, h * P + P)
                                s = egl[:, 4 * n + h:4 * n + h + 1]
                                tS = V(lambda e, b=b, c=c, s=s: e.scalar_tensor_tensor(ST[:, c], ST[:, c], s, b[:, c], ALU.mult, ALU.add),
                                       t, t2, st["egl"])
                        pt_free[i] = [tS]
                    to = A(lambda e, tt=tt, row=row, b=b2: e.activation(O[row, tt, :], b[row, :], ACT.Copy), t2)
                    pt_free[i2] = [to]
                    ot[n] = to
                    yield
                done_o = []
                for tt in range(2):
                    o = O[:, tt, :]
                    s4 = rsn[:, 4 * tt:4 * tt + 4]
                    t = A(lambda e, tt=tt, o=o: e.activation(Er[:, tt, :], o, ACT.Square), ot[2 * tt], ot[2 * tt + 1])
                    t = V(lambda e, tt=tt, s4=s4: e.tensor_reduce(s4, h4(Er[:, tt, :]), AX.X, ALU.add), t)
                    t = rsqrt(s4, 4, P * EPS, t)
                    t = V(lambda e, s4=s4: e.tensor_scalar(s4, s4, float(P) ** 0.5, None, ALU.mult), t)
                    t = V(lambda e, o=o, s4=s4: e.tensor_tensor(h4(o), h4(o), bc(s4.unsqueeze(2), [P, 4, P]), ALU.mult), t)
                    t = V(lambda e, o=o, tt=tt: e.tensor_tensor(o, o, Z[:, tt, :], ALU.mult), t, st["z"])
                    done_o.append(t)
                yield
                st["ydn"] = transposed(O, [0, 1, 2, 3], None, HH, HL, 0, done_o)
                yield

            hiq.append(solve())
            pair, outs, tok = unit()
            g_free[pair] = []
            for tt in range(2):
                t = A(lambda e, tt=tt, b=outs[tt]: e.activation(Z[:, tt, :], b, ACT.Sigmoid), tok)
                t = V(lambda e, tt=tt, b=outs[tt]: e.tensor_tensor(Z[:, tt, :], Z[:, tt, :], b, ALU.mult), t, tok)
                g_free[pair].append(t)
                st["z"] = V(lambda e, tt=tt: e.tensor_tensor(h4(Z[:, tt, :]), h4(Z[:, tt, :]), bc(tab("gout").unsqueeze(1), [P, 4, P]), ALU.mult), t, tdep)
            GAv = GA.rearrange("p (w t n) -> p w t n", w=2, t=2)
            gate_tok = []
            for gi in range(4):
                pair, outs, tok = unit()
                ts2 = []
                for tt in range(2):
                    o = GAv[:, gi // 2, tt, 512 * (gi % 2):512 * (gi % 2) + 512]
                    ts2.append(A(lambda e, o=o, b=outs[tt]: e.activation(o, b, ACT.Sigmoid), tok, ts))
                g_free[pair] = ts2
                gate_tok += ts2
            while "solved" not in st:
                pump()
            tB = dma("gpsimd", B, bass.AP(scr.tensor, 127, [[3071, P], [384, 8], [1, 256]]), "scr_in", [ts, st["qk"], st[("A", 1)]])
            hiq.append(scan())
            pair, outs, tok = unit()
            qT = AT.rearrange("p t (a n) -> p (t a) n", a=2)
            qT4 = AT.rearrange("p t n -> p (t n)").rearrange("p (c t) -> p c t", c=4)
            kbe_done = [st[("w", 0)], st[("w", 1)]]
            fin = []
            for tt in range(2):
                a, b = KBE[:, tt, :], outs[tt]
                s8 = t8a if tt == 0 else t8b
                t = A(lambda e, a=a, b=b: e.activation(a, b, ACT.Square), tok, *kbe_done)
                t = V(lambda e, a=a, s8=s8: e.tensor_reduce(s8, v3(a), AX.X, ALU.add), t)
                t = rsqrt(s8, 8, 64 * EPS, t)
                t = V(lambda e, a=a, b=b, s8=s8: e.tensor_tensor(v3(a), v3(b), bc(s8.unsqueeze(2), [P, 8, 64]), ALU.mult), t)
                fin.append(V(lambda e, a=a: e.tensor_tensor(v3(a), v3(a), bc(gq8.unsqueeze(1), [P, 8, 64]), ALU.mult), t, tg8))
            g_free[pair] = fin
            qt = []
            for tt in range(2):
                i, b = pt()
                w = [fin[tt], st[("A", 1)]] + pt_free[i]
                for c in range(4):
                    t = TR(b[:, c * P:c * P + P], KBE[:, tt, c * P:c * P + P], ident, *w, inc=(c == 3))
                    w = []
                t = A(lambda e, tt=tt, b=b: e.activation(qT4[:, :, tt * P:tt * P + P], b.rearrange("p (c t) -> p c t", c=4), ACT.Copy), t, *kbe_done)
                pt_free[i] = [t]
                qt.append(t)
                i, b = pt()
                t = TR(b[:, 0:P], SKV[:, tt, 0:P], ident, kdep, *pt_free[i], inc=True)
                t = A(lambda e, tt=tt, b=b: e.activation(kT[:, tt * P:tt * P + P], b[:, 0:P], ACT.Copy), t)
                pt_free[i] = [t]
                qt.append(t)
            s_free[0] = s_free[0] + b45_free[0] + b45_free[1]
            PP = [R1[:, 2048 + 256 * i:2304 + 256 * i] for i in range(4)]
            Aout = Ar
            items = []
            for h in range(8):
                c, row = h % 4, slice(64 * (h // 4), 64 * (h // 4) + 64)
                for tt in range(2):
                    n = P * (tt + 1)
                    items.append(dict(segs=[(qT4[row, c, tt * P:tt * P + P], kT[row, 0:n], n)], mask=B[:, h, 256 - n:256],
                                      v=[SKV[:, b, 128 + 64 * (h // 4):192 + 64 * (h // 4)] for b in range(tt + 1)],
                                      deps=qt + [vdep, tB], sink=nsink[:, h:h + 1], dst=Aout[:, tt, 64 * h:64 * h + 64], dfree=kbe_done))

            def finish(toks):
                st["yswa"] = transposed(Aout, [0, 1, 2, 3], None, HH, HL, 4, toks)
                yield

            loq.append(attention(items, PP[0:2], PP[2:4], small[:, 48:64], finish))
            while "ydn" not in st:
                pump()
            gf = g_free[0] + g_free[1]
            for i in range(2):
                tok = slot_wide((HH, HL, st["ydn"]), 2 * i, i == 0, i == 1, gf)
            tm = []
            for tt in range(2):
                o, b = GAv[:, 0, tt, :], ps[:, 1024 * tt:1024 * tt + 1024]
                tm.append(V(lambda e, o=o, b=b: e.tensor_tensor(o, o, b, ALU.mult), tok, *gate_tok))
            while "yswa" not in st:
                pump()
            for i in range(2):
                tok = slot_wide((HH, HL, st["yswa"]), 4 + 2 * i, i == 0, i == 1, tm)
            tn = []
            for tt in range(2):
                m, o, b = GAv[:, 0, tt, :], GAv[:, 1, tt, :], ps[:, 1024 * tt:1024 * tt + 1024]
                t = V(lambda e, o=o, b=b: e.tensor_tensor(o, o, b, ALU.mult), tok)
                tn.append(V(lambda e, o=o, m=m: e.tensor_tensor(m, m, o, ALU.add), t))
            th = transposed(GAv[:, 0], list(range(8)), None, HH, HL, 0, tn)
            for i in range(4):
                tok = slot_wide((HH, HL, th), 2 * i, i == 0, i == 3, tn)
            return residual(tok)

        tk = dma("gpsimd", keep[:, :], dram["keep"], "keep")
        keep_tok[0] = tk
        tx = dma("gpsimd", x[:, :, :], dram["x"].rearrange("o (t p) d -> p (o t) d", p=P), "x")
        for n in range(RAW):
            load(n)
        for n in range(RING - 1):
            split(n)
        xt = [[tx, tk], [tx, tk]]
        stages = [lambda t: mixer("a", 3, kt("an0"), t), lambda t: ffn(kt("cw0"), kt("fn0"), t),
                  lambda t: mixer("b", 1, kt("an1"), t), lambda t: ffn(kt("cw1"), kt("fn1"), t),
                  lambda t: third(kt("an2"), t), lambda t: ffn(None, kt("fn2"), t)]
        for s in stages:
            xt = s(xt)
        assert cur[0] == len(slots), (cur, len(slots))
        to = dma("sync", out.rearrange("o (t p) d -> p (o t) d", p=P), x[:, :, :], "out", xt[0] + xt[1])
        queue["sync"].append(lambda: nc.sync.wait_ge(to[0], to[1]))
        for name, (s, v) in dmas.items():
            queue["sync"].append(lambda s=s, v=v: nc.sync.wait_ge(s, v))

        block = ctx.enter_context(nc.Block())

        @block.sync
        def _(e):
            for f in queue["sync"]:
                f()

        @block.gpsimd
        def _(e):
            for f in queue["gpsimd"]:
                f()

        @block.scalar
        def _(e):
            for f in queue["scalar"]:
                f()

        @block.vector
        def _(e):
            for f in queue["vector"]:
                f()

        @block.tensor
        def _(e):
            for f in queue["tensor"]:
                f()


def layout(inputs):
    a = {k: np.asarray(v) for k, v in inputs.items()}
    slots = plan()
    w = np.zeros((len(slots), P, 2048), np.float32)
    for n, (name, layer, ks, cols) in enumerate(slots):
        o = 0
        for k in ks:
            for nm in (name if isinstance(name, tuple) else (name,)):
                w[n, :, o:o + len(cols)] = a[nm][layer][k * P:k * P + P][:, cols]
                o += len(cols)
    con, tabs = constants(), tables()

    def rows(v):
        return np.broadcast_to(np.ascontiguousarray(v).reshape(1, -1), (P, v.size))

    def col(v):
        return v.reshape(-1, P).T

    def taps(*v):
        return np.stack([col(q) for q in v], 2).reshape(P, -1)

    relb = np.zeros((P, 8), np.float32)
    relb[0:32] = a["rel_bias_2"]
    cw, cb, dw = a["ffn_conv_w"], a["ffn_conv_b"], a["dn_conv_2"][0]
    values = {
        "keep": dict(ident=con["ident"], an0=col(a["attn_norm"][0]), an1=col(a["attn_norm"][1]), fn0=col(a["ffn_norm"][0]),
                     fn1=col(a["ffn_norm"][1]), an2=col(a["attn_norm_2"][0]), fn2=col(a["ffn_norm_2"][0]),
                     cw0=taps(cw[0, 0], cw[0, 1], cw[0, 2], cb[0]), cw1=taps(cw[1, 0], cw[1, 1], cw[1, 2], cb[1]),
                     dnw=taps(dw[0], dw[1], dw[2], dw[3]), mhalf=np.full((P, 16), -0.5, np.float32)),
        "a": dict(cos=con["cos"], sin=con["sin"], m0=con["am0"], m1=con["am1"],
                  gain=rows(np.stack([a["a_q_norm"][0], a["a_k_norm"][0]], 1))),
        "b": dict(cos=con["cos"], sin=con["sin"], m0=con["bm0"], m1=con["bm1"],
                  gain=rows(np.stack([a["b_q_norm"][0], a["b_k_norm"][0]], 0))),
        "c": dict(gq=rows(a["swa_q_norm_2"]), gk=rows(a["swa_k_norm_2"]), gout=rows(a["dn_out_norm_2"]), alog=rows(a["dn_a_log_2"]),
                  dtb=rows(a["dn_dt_bias_2"]), sink=rows(a["swa_sinks_2"]), relb=relb,
                  **{k: con[k] for k in ("cum", "blk", "sel", "strict", "inct", "lev", "lev0t")}),
    }
    arrays = {"x": a["x"], "w": w, "onehot": con["onehot"], "edge": np.ascontiguousarray(con["edge"])}
    for name, t in tabs.items():
        v = np.zeros((P, t.n), np.float32)
        for k, (o, n) in t.at.items():
            v[:, o:o + n] = values[name][k]
        arrays[name] = v
    return arrays


def kernel(**inputs):
    import concourse.bacc as bacc
    from concourse.bass_utils import run_bass_kernel_spmd

    nc = bacc.Bacc("TRN2", target_bir_lowering=False, num_devices=1)
    arrays = layout(inputs)
    dram = {k: nc.dram_tensor(f"in_{k}", v.shape, F32, kind="ExternalInput").ap() for k, v in arrays.items()}
    out = nc.dram_tensor("out", (1, S, D), F32, kind="ExternalOutput").ap()
    build(nc, dram, out)
    r = run_bass_kernel_spmd(nc, [{f"in_{k}": v for k, v in arrays.items()}], core_ids=[0])
    return r.results[0]["out"]
```

```python
from collections import deque
from contextlib import ExitStack

import numpy as np

import concourse.bass as bass
from concourse import mybir

F32 = mybir.dt.float32
F32R = mybir.dt.float32r
ALU = mybir.AluOpType
ACT = mybir.ActivationFunctionType
AX = mybir.AxisListType

P = 128
S = 256
D = 1024
FF = 2816
EPS = 1e-6
NEG = -1.0e30
BIG = 3.0e38
SCALE = 0.125
RAW, RING = 3, 3
DILATED = ((128, 1), (512, 4), (2048, 16))
DN0, Z0, BA0, SQ0, SK0, SV0, GT0 = 0, 1536, 2048, 2056, 2568, 2696, 2824


def r(a, b):
    return np.arange(a, b)


def cat(*a):
    return np.concatenate(a)


def qk_units(ng):
    return (((0, 0), (1, 0)), ((2, 0), (2, 1)), ((0, 1), (1, 1))) if ng == 3 else (((0, 0), (0, 1)),)


def plan():
    out = []

    def unit(name, layer, cols):
        for k in (0, 4):
            out.append((name, layer, list(range(k, k + 4)), cols))

    def wide(name, layer, n):
        for k in range(0, n, 2):
            out.append((name, layer, [k, k + 1], r(0, D)))

    def ffn(up, layer, off_gate, off_val, down):
        for i in range(13):
            if i < 11:
                g = r(256 * i, 256 * i + 256)
                if isinstance(up, tuple):
                    for k in (0, 4):
                        out.append((up, layer, list(range(k, k + 4)), g))
                else:
                    unit(up, layer, cat(g + off_gate, g + off_val))
            if i > 1:
                out.append((down, layer, [2 * i - 4, 2 * i - 3], r(0, D)))

    def qk(name, ng, hg):
        for blocks in qk_units(ng):
            unit(name, 0, cat(*[r(0, P) + 1024 * (ng * s + g) + 256 * hg + P * pr for g, pr in blocks for s in range(2)]))

    for half in range(2):
        for g in range(3):
            unit("a_w_qkv", 0, r(0, 512) + 6144 + 1024 * g + 512 * half)
        for hg in (2 * half, 2 * half + 1):
            qk("a_w_qkv", 3, hg)
    wide("a_w_o", 0, 8)
    ffn("ffn_w_up", 0, 0, FF, "ffn_w_down")
    for half in range(2):
        unit("b_w_qkv", 0, r(0, 512) + 2048 + 512 * half)
        for hg in (2 * half, 2 * half + 1):
            qk("b_w_qkv", 1, hg)
    wide("b_w_o", 0, 8)
    ffn("ffn_w_up", 1, 0, FF, "ffn_w_down")
    for i in range(3):
        unit("w_in_2", 0, r(0, 512) + DN0 + 512 * i)
    unit("w_in_2", 0, cat(r(BA0, BA0 + 8), r(SK0, SK0 + 256)))
    unit("w_in_2", 0, r(Z0, Z0 + 512))
    for i in range(4):
        unit("w_in_2", 0, r(0, 512) + GT0 + 512 * i)
    pairs = cat(*[cat(r(64 * h, 64 * h + 64), r(64 * h + 256, 64 * h + 320)) for h in range(4)])
    unit("w_in_2", 0, pairs + SQ0)
    wide("w_branch_dn_2", 0, 4)
    wide("w_branch_swa_2", 0, 4)
    wide("w_out_2", 0, 8)
    ffn(("w_gate_2", "w_up_2"), 0, 0, 0, "w_down_2")
    return out


class Table:

    def __init__(self):
        self.at, self.n = {}, 0

    def add(self, name, n):
        self.at[name] = (self.n, n)
        self.n += n


def tables():
    keep, a, b, c = Table(), Table(), Table(), Table()
    keep.add("ident", 128)
    for name in ("an0", "an1", "fn0", "fn1", "an2", "fn2"):
        keep.add(name, 8)
    keep.add("cw0", 176)
    keep.add("cw1", 176)
    keep.add("dnw", 48)
    keep.add("mhalf", 16)
    a.add("cos", 32)
    a.add("sin", 32)
    a.add("gain", 384)
    a.add("m0", 384)
    a.add("m1", 768)
    b.add("cos", 32)
    b.add("sin", 32)
    b.add("gain", 128)
    b.add("m0", 128)
    b.add("m1", 256)
    c.add("gq", 64)
    c.add("gk", 64)
    c.add("gout", 128)
    c.add("alog", 4)
    c.add("dtb", 4)
    c.add("sink", 8)
    c.add("relb", 8)
    c.add("cum", 128)
    c.add("blk", 128)
    c.add("sel", 256)
    c.add("strict", 128)
    c.add("inct", 128)
    c.add("lev", 768)
    c.add("lev0t", 128)
    return {"keep": keep, "a": a, "b": b, "c": c}


def constants():
    f = np.float32
    t = np.arange(S)
    inv = (500000.0 ** (-np.arange(0, 16, 2) / 16.0)).astype(f)
    ang = t.astype(f)[:, None] * inv[None, :]
    cos, sin = np.cos(ang), np.sin(ang)
    rope_c = np.concatenate([cos, cos], 1).reshape(2, P, 16).transpose(1, 0, 2).reshape(P, 32)
    rope_s = np.concatenate([-sin, sin], 1).reshape(2, P, 16).transpose(1, 0, 2).reshape(P, 32)
    dist = t[:, None] - t[None, :]

    def add(ok):
        return np.where(ok, 0.0, NEG).astype(f)

    dil = [add((dist >= 0) & (dist % d == 0) & (dist <= w)) for w, d in DILATED]
    causal = add(dist >= 0)
    i = np.arange(P)
    same = i[:, None] // 64 == i[None, :] // 64
    lev = []
    for n in range(6):
        b = 1 << n
        lev.append((i[None, :] // (2 * b) == i[:, None] // (2 * b)) & (i[None, :] % (2 * b) >= b) & (i[:, None] % (2 * b) < b))
    x = np.arange(384)
    sd = 255 - x
    ok = (sd >= 0) & (sd < 128)
    n = np.maximum(sd, 0)
    nf = np.maximum(n, 1).astype(f)
    large = np.minimum(16 + (np.log(nf / f(16)) / f(np.log(8.0)) * f(16)).astype(np.int32), 31)
    bucket = np.where(n < 16, n, large)
    onehot = np.where(ok[None, :] & (bucket[None, :] == np.arange(32)[:, None]), 8.0, 0.0).astype(f)
    return {
        "ident": np.eye(P, dtype=f),
        "cos": rope_c.astype(f), "sin": rope_s.astype(f),
        "am0": np.concatenate([m[:P, :P] for m in dil], 1), "am1": np.concatenate([m[P:] for m in dil], 1),
        "bm0": causal[:P, :P], "bm1": causal[P:],
        "cum": (same & (i[:, None] <= i[None, :])).astype(f),
        "blk": same.astype(f),
        "sel": np.concatenate([np.repeat((i[:, None] // 64 == c), P, 1) for c in range(2)], 1).astype(f),
        "strict": (same & (i[:, None] > i[None, :])).astype(f),
        "inct": (same & (i[:, None] <= i[None, :])).astype(f),
        "lev": np.concatenate(lev, 1).astype(f), "lev0t": lev[0].T.astype(f),
        "onehot": onehot,
        "edge": np.broadcast_to(add(ok)[None, :], (P, 384)),
    }



def build(nc, dram, out):
    slots = plan()
    tabs = tables()
    with ExitStack() as ctx:
        def sb(name, shape, dt=F32):
            return ctx.enter_context(nc.sbuf_tensor(name, shape, dt))

        ENG = ("sync", "tensor", "vector", "scalar", "gpsimd")
        queue = {e: [] for e in ENG}
        count = {e: 0 for e in ENG}
        seen = {e: {} for e in ENG}
        done = {e: ctx.enter_context(nc.semaphore("done_" + e)) for e in ENG}
        handle = dict(tensor=nc.tensor, vector=nc.vector, scalar=nc.scalar, gpsimd=nc.gpsimd, sync=nc.sync)

        def op(e, fn, waits=(), inc=True):
            for s, v, name in waits:
                if seen[e].get(name, 0) < v:
                    seen[e][name] = v
                    queue[e].append(lambda h=handle[e], s=s, v=v: h.wait_ge(s, v))
            if inc:
                count[e] += 1
                queue[e].append(lambda: fn(handle[e]).then_inc(done[e], 1))
            else:
                queue[e].append(lambda: fn(handle[e]))
            return (done[e], count[e], e)

        dmas = {}

        def dma(e, dst, src, sem, waits=()):
            if sem not in dmas:
                dmas[sem] = [ctx.enter_context(nc.semaphore("dma_" + sem)), 0]
            dmas[sem][1] += 16
            s, v = dmas[sem]
            for w, wv, name in waits:
                if seen[e].get(name, 0) < wv:
                    seen[e][name] = wv
                    queue[e].append(lambda h=handle[e], w=w, wv=wv: h.wait_ge(w, wv))
            queue[e].append(lambda: handle[e].dma_start(dst, src).then_inc(s, 16))
            return (s, v, "dma_" + sem)

        def V(fn, *w):
            return op("vector", fn, w)

        def A(fn, *w):
            return op("scalar", fn, w)

        def G(fn, *w):
            return op("gpsimd", fn, w)

        def MM(o, l, rh, start, stop, *w, inc=False):
            return op("tensor", lambda e: e.matmul(o, l, rh, start=start, stop=stop, skip_group_check=True), w, inc)

        def TR(o, i, idn, *w, inc=False):
            return op("tensor", lambda e: e.transpose(o, i, idn), w, inc)

        x = sb("x", [P, 2, D])
        XH, XL = sb("XH", [P, 8, S], F32R), sb("XL", [P, 8, S], F32R)
        HH, HL = sb("HH", [P, 8, S], F32R), sb("HL", [P, 8, S], F32R)
        raw = [sb(f"raw{i}", [P, 2048]) for i in range(RAW)]
        wh = [sb(f"wh{i}", [P, 2048], F32R) for i in range(RING)]
        wl = [sb(f"wl{i}", [P, 2048], F32R) for i in range(RING)]
        keep = sb("keep", [P, tabs["keep"].n])
        small = sb("small", [P, 256])
        NAR = 23300
        arena = sb("arena", [P, NAR])
        ps = ctx.enter_context(nc.psum_tensor("ps", [P, 4096], F32))
        bank = [ps[:, 512 * i:512 * i + 512] for i in range(8)]
        scr = nc.dram_tensor("scr", (P * 8 * 384,), F32).ap()

        def kt(name):
            o, n = tabs["keep"].at[name]
            return keep[:, o:o + n]

        ident = kt("ident")
        used = [0]

        def ar(n):
            o = used[0]
            used[0] += n
            assert used[0] <= NAR, used
            return arena[:, o:o + n]

        def bc(ap, shape):
            return ap.to_broadcast(shape)

        raw_tok, hi_tok, lo_tok, use_tok = {}, {}, {}, {}

        def width(n):
            _, _, ks, cols = slots[n]
            c = len(cols) * (2 if isinstance(slots[n][0], tuple) else 1)
            return len(ks), c

        def load(n):
            if n >= len(slots):
                return
            k, c = width(n)
            w = (hi_tok[n - RAW], lo_tok[n - RAW]) if n >= RAW else ()
            raw_tok[n] = dma("sync", raw[n % RAW][:, 0:k * c], dram["w"][n, :, 0:k * c], f"raw{n % RAW}", w)

        def split(n):
            if n >= len(slots):
                return
            k, c = width(n)
            a, h, l = raw[n % RAW][:, 0:k * c], wh[n % RING][:, 0:k * c], wl[n % RING][:, 0:k * c]
            free = (use_tok[n - RING],) if n >= RING else ()
            m = k * c // 2
            sides = (slice(0, m), slice(m, 2 * m))
            th = {}

            def high(i):
                o = sides[i]
                th[i] = A(lambda e: e.activation(h[:, o], a[:, o], ACT.Copy), raw_tok[n], *free)

            def low(i):
                o = sides[i]
                t = V(lambda e: e.tensor_tensor(l[:, o], a[:, o], h[:, o].bitcast(F32), ALU.subtract), raw_tok[n], th[i], *free)
                if i:
                    hi_tok[n], lo_tok[n] = th[1], t
                    load(n + RAW)
            late.extend([[(high, 0)], [(high, 1), (low, 0)], [(low, 1)]])

        def hurry():
            for f, i in late.popleft():
                f(i)

        cur = [0]
        hiq, loq, late = deque(), deque(), deque()

        def step(q):
            while q:
                try:
                    next(q[0])
                    return
                except StopIteration:
                    q.popleft()

        def pump():
            for g in list(hiq):
                try:
                    next(g)
                except StopIteration:
                    hiq.remove(g)
            step(loq)
            if late:
                hurry()

        def drain():
            while hiq or loq:
                pump()

        def rsqrt(v, n, eps, *w):
            t = V(lambda e: e.tensor_scalar(v, v, eps, None, ALU.add), *w)
            return G(lambda e: e.tensor_tensor(v, v, kt("mhalf")[:, 0:n], ALU.pow), t, keep_tok[0])

        keep_tok = [None]

        def slot_views(n):
            while n not in lo_tok:
                hurry()
            k, c = width(n)
            v = lambda t: t[:, 0:k * c].rearrange("p (k c) -> p k c", k=k)
            return v(wh[n % RING]), v(wl[n % RING]), (hi_tok[n], lo_tok[n])

        def next_slot():
            n = cur[0]
            cur[0] += 1
            return n

        def after(n, tok):
            use_tok[n] = tok
            split(n + RING)

        def unit_tok(outs, act, free, nslots=2):
            tok = None
            for si in range(nslots):
                n = next_slot()
                h, l, w = slot_views(n)
                ah, al, aw = act
                c = width(n)[1]
                for tt in range(2):
                    ww = list(w) + list(aw[tt]) + (list(free) if si == 0 else [])
                    for j in range(4):
                        kk = 4 * si + j
                        t = slice(tt * P, tt * P + P)
                        first, last = kk == 0, kk == 4 * nslots - 1
                        o = outs[tt][:, 0:c]
                        MM(o, ah[:, kk, t], h[:, j, :], first, False, *ww)
                        MM(o, ah[:, kk, t], l[:, j, :], False, False)
                        tok = MM(o, al[:, kk, t], h[:, j, :], False, last, inc=(j == 3))
                        ww = []
                        if j == 3 and tt == 1:
                            after(n, tok)
                        if j % 2:
                            pump()
            return tok

        def unit_chan(outs, act, free, pumps=True):
            tok = None
            for si in range(2):
                n = next_slot()
                h, l, w = slot_views(n)
                ah, al, aw = act
                for nt in range(4):
                    ww = list(w) + aw[0] + aw[1] + (list(free) if si == 0 else [])
                    o = outs[nt // 2][:, (nt % 2) * S:(nt % 2) * S + S]
                    cols = slice(nt * P, nt * P + P)
                    for j in range(4):
                        kk = 4 * si + j
                        MM(o, h[:, j, cols], ah[:, kk, :], kk == 0 and nt % 2 == 0, False, *ww)
                        MM(o, h[:, j, cols], al[:, kk, :], False, False)
                        tok = MM(o, l[:, j, cols], ah[:, kk, :], False, kk == 7, inc=(j == 3))
                        ww = []
                    if nt == 3:
                        after(n, tok)
                    pump()
            return tok

        def slot_wide(act, kbase, first, last, free):
            n = next_slot()
            h, l, w = slot_views(n)
            ah, al, aw = act
            toks = []
            for tt in range(2):
                for hf in range(2):
                    o = bank[2 * tt + hf]
                    ww = list(w) + list(aw) + (list(free(tt)) if first else [])
                    c = slice(512 * hf, 512 * hf + 512)
                    for j in range(2):
                        t = slice(tt * P, tt * P + P)
                        MM(o, ah[:, kbase + j, t], h[:, j, c], first and j == 0, False, *ww)
                        MM(o, ah[:, kbase + j, t], l[:, j, c], False, False)
                        tok = MM(o, al[:, kbase + j, t], h[:, j, c], False, last and j == 1, inc=(j == 1))
                        ww = []
                    toks.append(tok)
                    if tt == 1 and hf == 1:
                        after(n, tok)
                    pump()
            return toks

        pt_free = [[], []]
        g_free = [[], []]
        ffn_free = [[], []]
        pt_n = [0]

        def pt():
            i = pt_n[0] % 2
            pt_n[0] += 1
            return i, bank[6 + i]

        def so_far(*engines):
            return [(done[e], count[e], e) for e in engines]

        def fence(now):
            for e in ("tensor", "vector", "scalar", "gpsimd"):
                for s, v, name in now:
                    if name != e and v and seen[e].get(name, 0) < v:
                        seen[e][name] = v
                        queue[e].append(lambda h=handle[e], s=s, v=v: h.wait_ge(s, v))

        def transposed(src, kts, dh, dl, base, waits):
            toks = []
            for i0 in range(0, len(kts), 2):
                i, b = pt()
                grp = kts[i0:i0 + 2]
                n = len(grp)
                w = list(waits) + pt_free[i]
                for gi, k in enumerate(grp):
                    for tt in range(2):
                        t = TR(b[:, gi * S + tt * P:gi * S + tt * P + P], src[:, tt, k * P:k * P + P], ident, *w, inc=(gi == n - 1 and tt == 1))
                        w = []
                o = slice(base + i0, base + i0 + n)
                v = b[:, 0:n * S].rearrange("p (k t) -> p k t", k=n)
                th = A(lambda e, o=o, v=v: e.activation(dh[:, o, :], v, ACT.Copy), t)
                tl = V(lambda e, o=o, v=v: e.tensor_tensor(dl[:, o, :], v, dh[:, o, :].bitcast(F32), ALU.subtract), t, th)
                toks += [th, tl]
                pt_free[i] = [th, tl]
            return toks

        xs = arena[:, NAR - 2048:NAR].rearrange("p (t d) -> p t d", t=2)
        xt = []

        def residual(tok, tt):
            out = []
            for hf in range(2):
                o, i = x[:, tt, 512 * hf:512 * hf + 512], bank[2 * tt + hf]
                out.append(V(lambda e, o=o, i=i: e.tensor_tensor(o, i, o, ALU.add), tok[2 * tt + hf]))
            g_free[tt] = out
            return out

        def norm_x(gains, tok, between=lambda: None):
            sums, rs, scaled, toks = small[:, 0:4], small[:, 4:6], [], [[], []]
            for tt in range(2):
                tx = residual(tok, tt) if tok else xt[tt]
                ts = []
                for hf in range(2):
                    c = slice(512 * hf, 512 * hf + 512)
                    ts.append(A(lambda e, tt=tt, c=c, s=sums[:, 2 * tt + hf:2 * tt + hf + 1]: e.activation(
                        xs[:, tt, c], x[:, tt, c], ACT.Square, accum_out=s), tx[hf]))
                a, b, v = sums[:, 2 * tt:2 * tt + 1], sums[:, 2 * tt + 1:2 * tt + 2], rs[:, tt:tt + 1]
                t = V(lambda e, a=a, b=b, v=v: e.scalar_tensor_tensor(v, a, D * EPS, b, ALU.add, ALU.add), *ts)
                scaled.append(G(lambda e, v=v: e.tensor_tensor(v, v, kt("mhalf")[:, 0:1], ALU.pow), t, keep_tok[0]))
            between()
            for tt in range(2):
                scaled[tt] = V(lambda e, tt=tt, v=rs[:, tt:tt + 1]: e.tensor_scalar(xs[:, tt, :], x[:, tt, :], v, 32.0, ALU.mult, ALU.mult), scaled[tt])
            for tt in range(2):
                for k0 in (0, 4):
                    i, b = pt()
                    w = [scaled[tt], keep_tok[0]] + pt_free[i]
                    for k in range(4):
                        t = TR(b[:, k * P:k * P + P], xs[:, tt, (k0 + k) * P:(k0 + k) * P + P], ident, *w, inc=(k == 3))
                        w = []
                    each = [(b[:, k * P:k * P + P], XH[:, k0 + k, tt * P:tt * P + P], XL[:, k0 + k, tt * P:tt * P + P],
                             gains[:, k0 + k:k0 + k + 1]) for k in range(4)]
                    for v, h, l, g in each:
                        th = A(lambda e, v=v, h=h, g=g: e.activation(h, v, ACT.Copy, scale=g), t)
                    for v, h, l, g in each:
                        tl = V(lambda e, v=v, h=h, l=l, g=g: e.scalar_tensor_tensor(l, v, g, h.bitcast(F32), ALU.mult, ALU.subtract), t, th)
                    toks[tt] += [th, tl]
                    pt_free[i] = [th, tl]
            return toks

        s_free = [[], []]

        def attention(items, area, Pb, PTb, st, finish, parts, halves):
            N = len(items)
            R = len(Pb)
            state = {}

            def scores(i):
                it = items[i]
                for ut in it["need"]:
                    it["deps"] = it["deps"] + ut
                sp, f = area[i % len(area)], i % len(area)
                w = list(it["deps"]) + s_free[f]
                o, spans = 0, []
                for pi, segs in enumerate(it["segs"]):
                    o0 = o
                    for si, (q, k, n) in enumerate(segs):
                        t = MM(sp[:, o:o + n], q, k, True, True, *w, inc=(si == len(segs) - 1))
                        w = []
                        o += n
                    spans.append((o0, o))
                back = [state[i - R]["pt"]] if i >= R else []
                c = 2 * (i % 4)
                nm = st[:, c:c + 2]
                for pi, (a, b) in enumerate(spans):
                    t1 = V(lambda e, a=a, b=b, pi=pi, m=it["mask"][pi], p=Pb[i % R]: e.tensor_tensor_reduce(
                        p[:, a:b], sp[:, a:b], m, -SCALE, BIG, ALU.add, ALU.min, nm[:, pi:pi + 1]), t, *back)
                s_free[f] = [t1]
                if it.get("sink") is not None:
                    sk, es = bc(it["sink"], [P, 2]), st[:, 24 + c:26 + c]
                    t1 = V(lambda e: e.tensor_tensor(nm, nm, sk, ALU.min), t1)
                    t3 = V(lambda e: e.tensor_tensor(es, nm, sk, ALU.subtract), t1)
                    state[i, "es"] = A(lambda e: e.activation(es, es, ACT.Exp), t3)
                state[i] = {"m": t1, "n": o, "spans": spans}

            def exps(i):
                s, p, c = state[i], Pb[i % R], 2 * (i % 4)
                for pi, (a, b) in enumerate(s["spans"]):
                    nm, den = st[:, c + pi:c + pi + 1], st[:, 8 + c + pi:9 + c + pi]
                    s["p"] = A(lambda e, a=a, b=b, nm=nm, den=den: e.activation(p[:, a:b], p[:, a:b], ACT.Exp, bias=nm, scale=-1.0, accum_out=den), s["m"])

            def turn(i):
                s = state[i]
                nb = s["n"] // P
                toks = []
                back = [state[i - 2]["pv"]] if i >= 2 else []
                for b0 in range(0, nb, 3):
                    bn = min(3, nb - b0)
                    j, bk = pt()
                    w = [s["p"]] + pt_free[j]
                    for b in range(bn):
                        t = TR(bk[:, b * P:b * P + P], Pb[i % R][:, (b0 + b) * P:(b0 + b) * P + P], ident, *w, inc=(b == bn - 1))
                        w = []
                    o, c = PTb[i % 2][:, b0 * P:(b0 + bn) * P], bk[:, 0:bn * P]
                    if b0 == 0:
                        t2 = A(lambda e, o=o, c=c: e.activation(o, c, ACT.Copy), t, *back)
                    else:
                        t2 = V(lambda e, o=o, c=c: e.tensor_copy(o, c), t, *back)
                    pt_free[j] = [t2]
                    toks.append(t2)
                s["pt"] = t
                s["ptc"] = toks
                c = 2 * (i % 4)
                den, rd = st[:, 8 + c:8 + c + parts], st[:, 16 + c:16 + c + parts]
                t3 = s["p"]
                if (i, "es") in state:
                    es = st[:, 24 + c:24 + c + parts]
                    t3 = V(lambda e: e.tensor_tensor(den, den, es, ALU.add), t3, state[i, "es"])
                s["rd"] = V(lambda e: e.reciprocal(rd, den), t3, *([state[i - 4]["on"]] if i >= 4 else []))

            def pv(i):
                s, it = state[i], items[i]
                j, bk = pt()
                w = s["ptc"] + pt_free[j] + list(it["deps"])
                for pi, (a, e) in enumerate(s["spans"]):
                    nb = (e - a) // P
                    for b in range(nb):
                        t = MM(bk[:, 64 * pi:64 * pi + 64], PTb[i % 2][:, a + b * P:a + b * P + P], it["v"][pi][b], b == 0, b == nb - 1, *w,
                               inc=(b == nb - 1 and pi == parts - 1))
                        w = []
                s["pv"] = t
                c = 2 * (i % 4)
                rd, dst = bc(st[:, 16 + c:16 + c + parts].unsqueeze(2), [P, parts, 64]), it["dst"]
                o = bk[:, 0:64 * parts].rearrange("p (a d) -> p a d", a=parts)
                s["on"] = V(lambda e: e.tensor_tensor(dst, o, rd, ALU.mult), t, s["rd"], *it.get("dfree", ()))
                pt_free[j] = [s["on"]]

            lag = 2 if halves else 3
            for i in range(N + lag + 1):
                while i < N and any(len(ut) < 2 for ut in items[i]["need"]):
                    yield
                if i > lag:
                    pv(i - lag - 1)
                if halves:
                    if i < N:
                        scores(i)
                    yield
                if lag <= i < N + lag:
                    turn(i - lag)
                if halves:
                    if i < N:
                        exps(i)
                else:
                    if 1 <= i <= N:
                        exps(i - 1)
                    if i < N:
                        scores(i)
                yield
            yield from finish([state[i]["on"] for i in range(N)])

        v3 = lambda ap: ap.rearrange("p (h d) -> p h d", d=64)
        v4 = lambda ap: ap.rearrange("p (s h d) -> p s h d", s=2, d=64)

        def load_table(name, waits):
            n = tabs[name].n
            t = ar(n)
            tok = dma("gpsimd", t, dram[name], "tab_" + name, waits)
            return (lambda k: t[:, tabs[name].at[k][0]:tabs[name].at[k][0] + tabs[name].at[k][1]]), tok

        def rope_tables(tab, ng, GC, GS, dep):
            cosv = tab("cos").rearrange("p (t d) -> p t d", t=2)
            sinv = tab("sin").rearrange("p (t d) -> p t d", t=2)
            gv = tab("gain").rearrange("p (g s d) -> p g s d", g=ng, s=2)
            last = None
            for g in range(ng):
                for tt in range(2):
                    cb = bc(cosv[:, tt, :].unsqueeze(1), [P, 2, 16])
                    s0 = bc(sinv[:, tt, 0:8].unsqueeze(1), [P, 2, 8])
                    s1 = bc(sinv[:, tt, 8:16].unsqueeze(1), [P, 2, 8])
                    gg, cc, ss = gv[:, g], GC[:, g, tt], GS[:, g, tt]
                    V(lambda e, gg=gg, cc=cc: e.tensor_scalar(cc[:, :, 16:64], gg[:, :, 16:64], 8.0, None, ALU.mult), dep)
                    V(lambda e, gg=gg, cc=cc, cb=cb: e.scalar_tensor_tensor(cc[:, :, 0:16], gg[:, :, 0:16], 8.0, cb, ALU.mult, ALU.mult))
                    V(lambda e, gg=gg, ss=ss, s0=s0: e.scalar_tensor_tensor(ss[:, :, 0:8], gg[:, :, 8:16], 8.0, s0, ALU.mult, ALU.mult))
                    last = V(lambda e, gg=gg, ss=ss, s1=s1: e.scalar_tensor_tensor(ss[:, :, 8:16], gg[:, :, 0:8], 8.0, s1, ALU.mult, ALU.mult))
            return last

        def mixer(tabname, ng, norm_gain, last, between=lambda: None):
            used[0] = 0
            now = so_far("tensor", "vector", "scalar", "gpsimd")
            tab, tdep = load_table(tabname, now)
            GC = ar(ng * 256).rearrange("p (g t s d) -> p g t s d", g=ng, t=2, s=2)
            GS = ar(ng * 64).rearrange("p (g t s d) -> p g t s d", g=ng, t=2, s=2)
            Vt = ar(2 * ng * D).rearrange("p (t g n) -> p t g n", t=2, g=ng)
            qkT = [ar(ng * 1024).rearrange("p (g c t) -> p g c t", g=ng, c=4) for _ in range(2)]
            sqs, qn, tp, ssb = [[ar(512), ar(512)]], [ar(512), ar(512)], [ar(128), ar(128)], small[:, 16:32]
            sqs.append([arena[:, NAR - 1280 + 512 * i:NAR - 768 + 512 * i] for i in range(2)])
            np_ = 768 if ng == 3 else 384
            Pb, PTb = [ar(np_), ar(np_), arena[:, NAR - 2048:NAR - 2048 + np_]], [ar(np_), ar(np_)]
            att = [ar(512).rearrange("p (t d) -> p t d", t=2) for _ in range(2)]
            assert used[0] <= NAR - 2048, used
            act = (XH, XL, norm_x(norm_gain, last, between))
            fence(now)
            td = rope_tables(tab, ng, GC, GS, tdep)
            vt, att_free, qk_free, out_tok = [], [[], []], [[], []], {}
            rope_done, turned, nq = [[], []], [[[], []], [[], []]], [0]
            un = [0]

            def heads(pair, tok, blocks, T, wfree, ut, wait):
                sq, was = sqs[nq[0] % 2], turned[nq[0] % 2]
                nq[0] += 1
                sqt = [A(lambda e, a=sq[tt], src=bank[2 * pair + tt]: e.activation(a, src, ACT.Square), tok, *was[tt]) for tt in range(2)]

                def go():
                    for tt in range(2):
                        t2 = V(lambda e, a=sq[tt], ss=ssb[:, 8 * tt:8 * tt + 8]: e.tensor_reduce(ss, v3(a), AX.X, ALU.add), sqt[tt])
                    t3 = rsqrt(ssb, 16, 64 * EPS, t2)
                    yield
                    yield
                    free, fin = list(sqt), []
                    for tt in range(2):
                        src, a, b = bank[2 * pair + tt], sq[tt], qn[tt]
                        rs = bc(ssb[:, 8 * tt:8 * tt + 8].unsqueeze(2), [P, 8, 64])
                        t4 = V(lambda e, b=b, src=src, rs=rs: e.tensor_tensor(v3(b), v3(src), rs, ALU.mult), t3, tok, *rope_done[tt])
                        free.append(t4)
                        v5 = lambda ap, d: ap.rearrange("p (j s h d) -> p j s h d", j=2, s=2, d=d)
                        av, bv, tv = v5(a, 64), v5(b, 64), v5(tp[tt], 16)
                        for bl, (g, _) in enumerate(blocks):
                            gc = bc(GC[:, g, tt].unsqueeze(2), [P, 2, 2, 64])
                            t5 = V(lambda e, bl=bl, av=av, bv=bv, gc=gc: e.tensor_tensor(av[:, bl], bv[:, bl], gc, ALU.mult), t4, td)
                        for bl, (g, _) in enumerate(blocks):
                            for q in range(2):
                                m = bc(GS[:, g, tt, :, 8 * q:8 * q + 8].unsqueeze(2), [P, 2, 2, 8])
                                o, i = tv[:, bl, :, :, 8 * q:8 * q + 8], bv[:, bl, :, :, 8 - 8 * q:16 - 8 * q]
                                t6 = G(lambda e, o=o, i=i, m=m: e.tensor_tensor(o, i, m, ALU.mult), t4, td)
                        tq = tp[tt].rearrange("p (h d) -> p h d", d=16)
                        t7 = G(lambda e, a=a, tq=tq: e.tensor_tensor(v3(a)[:, :, 0:16], v3(a)[:, :, 0:16], tq, ALU.add), t5, t6)
                        rope_done[tt] = [t7]
                        fin.append(t7)
                    g_free[pair] = free
                    for _ in range(wait):
                        yield
                    for tt in range(2):
                        i, b = pt()
                        w = [fin[tt]] + pt_free[i]
                        for c in range(4):
                            t = TR(b[:, c * P:c * P + P], sq[tt][:, c * P:c * P + P], ident, *w, inc=(c == 3))
                            w = []
                        was[tt] = [t]
                        (g, pr), ts_ = blocks[0], slice(tt * P, tt * P + P)
                        if blocks[1][0] == g:
                            o = T[:, g].rearrange("p (s r) t -> p r s t", s=2)[:, :, :, ts_]
                        else:
                            o = T[:, g:g + 2].rearrange("p g (s r) t -> p g s r t", s=2)[:, :, :, pr, ts_]
                        v = b.rearrange("p (j s t) -> p j s t", j=2, s=2)
                        t = A(lambda e, o=o, v=v: e.activation(o, v, ACT.Copy), t, *wfree)
                        pt_free[i] = [t]
                        ut.append(t)
                        yield
                g_free[pair] = None
                hiq.append(go())

            def finish_for(hg):
                def finish(toks):
                    qk_free[hg % 2] = toks
                    yield
                    out_tok[hg] = transposed(att[hg % 2], [0, 1], HH, HL, 2 * hg, toks)
                    att_free[hg % 2] = [(done["tensor"], count["tensor"], "tensor")]
                    yield
                return finish

            def group(hg, units):
                items = []
                T = qkT[hg % 2]
                tiles = [(0,), (1,)] if ng == 3 else [(0, 1)]
                for h in range(4):
                    pr, row = h // 2, slice(64 * (h % 2), 64 * (h % 2) + 64)
                    hc = 64 * (4 * hg + h)
                    need = [ut for bl, ut in units if any(b[1] == pr for b in bl)]
                    for tts in tiles:
                        segs = [[(T[row, g, pr, tt * P:tt * P + P], T[row, g, 2 + pr, 0:P * (tt + 1)], P * (tt + 1)) for g in range(ng)] for tt in tts]
                        v = [[Vt[:, b, g, hc:hc + 64] for g in range(ng) for b in range(tt + 1)] for tt in tts]
                        items.append(dict(segs=segs, mask=[tab(f"m{tt}") for tt in tts], v=v, need=need, deps=vt + [tdep],
                                          dst=att[hg % 2][:, tts[0]:tts[-1] + 1, 64 * h:64 * h + 64], dfree=att_free[hg % 2]))
                area = [ps[:, 2048:2048 + 768]] if ng == 3 else [bank[4], bank[5]]
                yield from attention(items, area, Pb, PTb, small[:, 192:224], finish_for(hg), len(tiles[0]), ng == 3)

            def free_of(pair):
                while g_free[pair] is None:
                    pump()
                return g_free[pair]

            for half in range(2):
                for g in range(ng):
                    pair = un[0] % 2
                    un[0] += 1
                    tok = unit_tok([bank[2 * pair], bank[2 * pair + 1]], act, free_of(pair))
                    toks = []
                    for tt in range(2):
                        o, b = Vt[:, tt, g, 512 * half:512 * half + 512], bank[2 * pair + tt]
                        toks.append(A(lambda e, o=o, b=b: e.activation(o, b, ACT.Copy), tok))
                    vt += toks
                    g_free[pair] = toks
                for hg in (2 * half, 2 * half + 1):
                    while hg >= 2 and (hg - 2) not in out_tok:
                        pump()
                    units = [(blocks, []) for blocks in qk_units(ng)]
                    loq.append(group(hg, units))
                    for blocks, ut in units:
                        pair = un[0] % 2
                        un[0] += 1
                        tok = unit_tok([bank[2 * pair], bank[2 * pair + 1]], act, free_of(pair))
                        heads(pair, tok, blocks, qkT[hg % 2], qk_free[hg % 2], ut, 3 if hg == 3 and ut is units[-1][1] else 6)
            for i in range(4):
                while i not in out_tok:
                    pump()
                tok = slot_wide((HH, HL, out_tok[i]), 2 * i, i == 0, i == 3, free_of)
            drain()
            return tok

        def ffn(cw, norm_gain, last):
            used[0] = 0
            Y = [ar(1024).rearrange("p (n t) -> p n t", n=4) for _ in range(2)]
            act = (XH, XL, norm_x(norm_gain, last))
            base = so_far("vector", "scalar")
            free, hfree, htok, yfree = [base, base], {}, {}, [base, base]
            for i in range(13):
                if i < 11:
                    p = i % 2
                    y = Y[p]
                    bb = [bank[4 + 2 * p], bank[5 + 2 * p]]
                    tok = unit_chan(bb, act, free[p])
                    u = [bb[n // 2][:, (n % 2) * S:(n % 2) * S + S] for n in range(4)]
                    if cw is None:
                        t = A(lambda e, y=y, b=bb[0]: e.activation(y[:, 0:2, :].rearrange("p n t -> p (n t)"), b, ACT.Silu), tok, *yfree[p])
                        t2 = V(lambda e, y=y, b=bb[1]: e.tensor_tensor(y[:, 2:4, :].rearrange("p n t -> p (n t)"),
                                                                       y[:, 0:2, :].rearrange("p n t -> p (n t)"), b, ALU.mult), t, tok, *yfree[p])
                        free[p] = [t, t2]
                    else:
                        ts, t1 = [], []
                        each = []
                        for n in range(4):
                            ch = 2 * i + n if n < 2 else 22 + 2 * i + n - 2
                            w = cw[:, 4 * ch:4 * ch + 4]
                            yn, un = y[:, n, :], u[n]
                            each.append((n, w, yn, un))
                            t1.append(A(lambda e, yn=yn, un=un, w=w: e.activation(yn, un, ACT.Identity, bias=w[:, 3:4], scale=w[:, 2:3]), tok, *yfree[p]))
                        for n, w, yn, un in each:
                            t2 = V(lambda e, yn=yn, un=un, w=w: e.scalar_tensor_tensor(yn[:, 1:S], un[:, 0:S - 1], w[:, 1:2], yn[:, 1:S], ALU.mult, ALU.add), t1[n | 1], tok)
                            t3 = V(lambda e, yn=yn, un=un, w=w: e.scalar_tensor_tensor(yn[:, 2:S], un[:, 0:S - 2], w[:, 0:1], yn[:, 2:S], ALU.mult, ALU.add), t2)
                            ts.append(t3)
                        free[p] = [t1[3], t3]
                        t = A(lambda e, y=y: e.activation(y[:, 0:2, :], y[:, 0:2, :], ACT.Silu), ts[1])
                        t2 = V(lambda e, y=y: e.tensor_tensor(y[:, 2:4, :], y[:, 0:2, :], y[:, 2:4, :], ALU.mult), t, ts[3])
                    k = (2 * i) % 8
                    back = [hfree[i - 4]] if i >= 4 else []
                    th = A(lambda e, y=y, k=k: e.activation(HH[:, k:k + 2, :], y[:, 2:4, :], ACT.Copy), t2, *back)
                    tl = V(lambda e, y=y, k=k: e.tensor_tensor(HL[:, k:k + 2, :], y[:, 2:4, :], HH[:, k:k + 2, :].bitcast(F32), ALU.subtract), th, *back)
                    htok[i] = [th, tl]
                    yfree[p] = [th, tl]
                if i > 1:
                    d = i - 2
                    tok = slot_wide((HH, HL, htok[d]), (2 * d) % 8, d == 0, d == 10, lambda tt: g_free[tt])
                    hfree[d] = tok[3]
            return tok

        rot = [0]
        b45_free = [[], []]

        def rot4():
            i = rot[0] % 4
            rot[0] += 1
            return (b45_free, i) if i < 2 else (pt_free, i - 2), bank[4 + i]

        def third(norm_gain, last):
            used[0] = 0
            now = so_far("tensor", "vector", "scalar", "gpsimd")
            tab, tdep = load_table("c", now)
            R1, R2 = ar(3072), ar(3072).rearrange("p (t n) -> p t n", t=2)
            KQ = ar(2048)
            QE = ar(1024).rearrange("p (h t) -> p h t", h=4)
            KBE = ar(1024).rearrange("p (t n) -> p t n", t=2)
            Ar, AT = [ar(1024).rearrange("p (t n) -> p t n", t=2) for _ in range(2)]
            Er = ar(1024).rearrange("p (t n) -> p t n", t=2)
            QKT = ar(1024)
            ST = ar(512)
            kT = ar(256)
            SKV = ar(512).rearrange("p (t n) -> p t n", t=2)
            Z = ar(1024).rearrange("p (t n) -> p t n", t=2)
            GA = ar(4096)
            XT = R1.rearrange("p (c t) -> p c t", c=12)
            KQv = KQ.rearrange("p (t h n) -> p t h n", t=2, h=4)
            T = KQ[:, 0:1024].rearrange("p (t n) -> p t n", t=2)
            TT = KQ[:, 1024:2048].rearrange("p (t n) -> p t n", t=2)
            ARG, DM, DT = [R1[:, 1024 * i:1024 * i + 1024].rearrange("p (t n) -> p t n", t=2) for i in range(3)]
            QKTv = QKT.rearrange("p (t n) -> p t n", t=2)
            B = R1[:, 0:2048].rearrange("p (h n) -> p h n", h=8)
            h4 = lambda ap: ap.rearrange("p (h d) -> p h d", h=4)
            sv = lambda a, n: small[:, a:a + n]
            beta, gg, gc, eg, dk, bg = [sv(64 + 8 * i, 8) for i in range(6)]
            gl, egl, t8a, t8b, t8c, rsn = sv(112, 8), sv(120, 16), sv(136, 8), sv(144, 8), sv(152, 8), sv(160, 16)
            nsink, gq8, gk8 = sv(176, 8), tab("gq"), tab("gk")
            act = (XH, XL, norm_x(norm_gain, last))
            fence(now)
            act_tok = act[2][0] + act[2][1]

            onehot, edge = QKT[0:32, 0:384], QKT[:, 384:768]
            td1 = dma("gpsimd", onehot, dram["onehot"], "tab_onehot", now)
            td2 = dma("gpsimd", edge, dram["edge"], "tab_edge", now)
            relb = GA[0:32, 3072:4096].rearrange("p (h n) -> p h n", h=8)
            t = V(lambda e: e.tensor_copy(relb, bc(tab("relb")[0:32, :].unsqueeze(2), [32, 8, P])), tdep, *act_tok)
            for q in (gq8, gk8):
                tg8 = V(lambda e, q=q: e.tensor_scalar(q, q, 8.0, None, ALU.mult), tdep)
            tg8 = V(lambda e: e.tensor_scalar(nsink, tab("sink"), -1.0, None, ALU.mult), tdep)
            rows = []
            for h in range(8):
                i, b = pt()
                tm = MM(b[:, 0:384], relb[:, h, :], onehot, True, True, t, td1, *pt_free[i], inc=True)
                tv = V(lambda e, h=h, b=b: e.tensor_tensor(GA[:, 384 * h:384 * h + 384], b[:, 0:384], edge, ALU.add), tm, td2, *act_tok)
                pt_free[i] = [tv]
                rows.append(tv)
            ts = dma("gpsimd", scr.rearrange("(p n) -> p n", p=P), GA[:, 0:3072], "scr_out", rows)
            un = [0]

            def unit(chan=False):
                pair = un[0] % 2
                un[0] += 1
                outs = [bank[2 * pair], bank[2 * pair + 1]]
                return pair, outs, (unit_chan if chan else unit_tok)(outs, act, g_free[pair])

            silu_tok = {}
            dnw = kt("dnw")
            for i in range(3):
                pair, outs, tok = unit(True)
                each = [(4 * i + n, dnw[:, 16 * i + 4 * n:16 * i + 4 * n + 4], XT[:, 4 * i + n, :], outs[n // 2][:, (n % 2) * S:(n % 2) * S + S])
                        for n in range(4)]
                ta = [A(lambda e, yn=yn, u=u, w=w: e.activation(yn, u, ACT.Copy, scale=w[:, 3:4]), tok) for _, w, yn, u in each]
                for n, (ch, w, yn, u) in enumerate(each):
                    tv = ta[n | 1]
                    for d in range(1, 4):
                        tv = V(lambda e, yn=yn, u=u, w=w, d=d: e.scalar_tensor_tensor(yn[:, d:S], u[:, 0:S - d], w[:, 3 - d:4 - d], yn[:, d:S],
                                                                                     ALU.mult, ALU.add), tv, tok)
                    silu_tok[ch] = A(lambda e, yn=yn: e.activation(yn, yn, ACT.Silu), tv)
                g_free[pair] = [ta[3], tv]

            pair, outs, tok = unit()
            raws = []
            for tt in range(2):
                raw_row = Er[:, tt, 0:264]
                tok1 = A(lambda e, raw_row=raw_row, b=outs[tt]: e.activation(raw_row, b[:, 0:264], ACT.Copy), tok)
                raws.append(tok1)
                b, a = raw_row[:, 0:4], raw_row[:, 4:8]
                o = slice(4 * tt, 4 * tt + 4)
                t = A(lambda e, b=b, o=o: e.activation(t8a[:, o], b, ACT.Exp, scale=-1.0), tok1)
                t = V(lambda e, o=o: e.tensor_scalar(t8a[:, o], t8a[:, o], 1.0, None, ALU.add), t)
                tbeta = V(lambda e, o=o: e.reciprocal(beta[:, o], t8a[:, o]), t)
                z, q, u1 = gc[:, o], t8b[:, o], t8c[:, o]
                t = V(lambda e, z=z, a=a: e.tensor_tensor(z, a, tab("dtb"), ALU.add), tok1, tdep)
                tabs_ = V(lambda e, z=z, q=q: e.scalar_tensor_tensor(q, z, -1.0, z, ALU.mult, ALU.max), t)
                t = A(lambda e, q=q: e.activation(q, q, ACT.Exp, scale=-1.0), tabs_)
                t1 = V(lambda e, q=q, u1=u1: e.tensor_scalar(u1, q, 1.0, None, ALU.add), t)
                l = gg[:, o]
                tl = A(lambda e, l=l, u1=u1: e.activation(l, u1, ACT.Ln), t1)
                ri = t8a[:, o]
                t2 = V(lambda e, ri=ri, u1=u1: e.reciprocal(ri, u1), t1, tbeta)
                t3 = V(lambda e, u1=u1: e.tensor_scalar(u1, u1, -1.0, None, ALU.add), t2, tl)
                t3 = V(lambda e, q=q, u1=u1: e.tensor_tensor(q, q, u1, ALU.subtract), t3)
                t3 = V(lambda e, q=q, ri=ri: e.tensor_tensor(q, q, ri, ALU.mult), t3, t2)
                t3 = V(lambda e, l=l, q=q: e.tensor_tensor(l, l, q, ALU.add), t3, tl)
                t3 = V(lambda e, l=l, z=z: e.scalar_tensor_tensor(l, z, 0.0, l, ALU.max, ALU.add), t3)
                ta = A(lambda e, q=q: e.activation(q, tab("alog"), ACT.Exp), t3)
                tgg = V(lambda e, l=l, q=q: e.scalar_tensor_tensor(l, l, -1.0, q, ALU.mult, ALU.mult), ta, t3)
                k, kk = raw_row[:, 8:136], SKV[:, tt, 0:128]
                sk = rsn[:, 2 * tt:2 * tt + 2]
                k2 = lambda ap: ap.rearrange("p (h d) -> p h d", h=2)
                t = A(lambda e, k=k, kk=kk: e.activation(kk, k, ACT.Square), tok1)
                t = V(lambda e, kk=kk, sk=sk: e.tensor_reduce(sk, k2(kk), AX.X, ALU.add), t)
                t = rsqrt(sk, 2, 64 * EPS, t)
                t = V(lambda e, k=k, kk=kk, sk=sk: e.tensor_tensor(k2(kk), k2(k), bc(sk.unsqueeze(2), [P, 2, 64]), ALU.mult), t)
                tk = V(lambda e, kk=kk: e.tensor_tensor(k2(kk), k2(kk), bc(gk8.unsqueeze(1), [P, 2, 64]), ALU.mult), t, tg8)
                tvv = A(lambda e, b=raw_row, tt=tt: e.activation(SKV[:, tt, 128:256], b[:, 136:264], ACT.Copy), tok1)
            g_free[pair] = raws
            kdep, vdep, gdep, bdep = tk, tvv, tgg, tbeta

            st = {}

            def solve():
                vt = {}
                for tt in range(2):
                    for gidx in range(3):
                        i, b = pt()
                        w = [silu_tok[4 * gidx + 3]] + pt_free[i]
                        for c in range(4):
                            t = TR(b[:, c * P:c * P + P], XT[:, 4 * gidx + c, tt * P:tt * P + P], ident, *w, inc=(c == 3))
                            w = []
                        o = R2[:, tt, 512 * gidx:512 * gidx + 512]
                        if gidx == 2:
                            tb = bc(beta[:, 4 * tt:4 * tt + 4].unsqueeze(2), [P, 4, P])
                            tc = V(lambda e, o=o, b=b, tb=tb: e.tensor_tensor(h4(o), h4(b), tb, ALU.mult), t, bdep)
                        else:
                            s4 = rsn[:, 4 + 4 * (gidx + 2 * (tt % 2)) - 4:4 + 4 * (gidx + 2 * (tt % 2))]
                            ta = A(lambda e, b=b, tt=tt: e.activation(Er[:, tt, :], b, ACT.Square), t, *([vt["sum"]] if "sum" in vt else []), kdep, vdep, gdep, bdep)
                            t1 = V(lambda e, tt=tt, s4=s4: e.tensor_reduce(s4, h4(Er[:, tt, :]), AX.X, ALU.add), ta, kdep)
                            vt["sum"] = t1
                            t1 = rsqrt(s4, 4, EPS, t1)
                            if gidx == 0:
                                t1 = V(lambda e, s4=s4: e.tensor_scalar(s4, s4, float(P) ** -0.5, None, ALU.mult), t1)
                            tb = bc(s4.unsqueeze(2), [P, 4, P])
                            tc = V(lambda e, o=o, b=b, tb=tb: e.tensor_tensor(h4(o), h4(b), tb, ALU.mult), t1, t)
                        pt_free[i] = [tc]
                        vt[(tt, gidx)] = tc
                        yield
                (fl, fi), b = rot4()
                w = [gdep, tdep] + fl[fi]
                for tt in range(2):
                    gs = gg[:, 4 * tt:4 * tt + 4]
                    MM(b[:, 4 * tt:4 * tt + 4], tab("cum"), gs, True, True, *w)
                    MM(b[:, 8 + 4 * tt:12 + 4 * tt], tab("blk"), gs, True, True)
                    for c in range(2):
                        o = 16 + 8 * tt + 4 * c
                        t = MM(b[:, o:o + 4], tab("sel")[:, P * c:P * c + P], gs, True, True, inc=True)
                    w = []
                t1 = V(lambda e, b=b: e.tensor_copy(gc, b[:, 0:8]), t)
                t2 = V(lambda e, b=b: e.tensor_tensor(gl, b[:, 8:16], gc, ALU.subtract), t, t1)
                t3 = A(lambda e, b=b: e.activation(egl, b[:, 16:32], ACT.Exp), t2)
                t4 = A(lambda e: e.activation(eg, gc, ACT.Exp), t1)
                t5 = A(lambda e: e.activation(dk, gl, ACT.Exp), t2)
                t6 = V(lambda e: e.tensor_tensor(bg, beta, eg, ALU.mult), t4, bdep)
                fl[fi] = [t2, t3]
                st["egl"] = t3
                tkq = {}
                for tt in range(2):
                    for which, col in ((1, 0), (0, P)):
                        i, b = pt()
                        w = [vt[(tt, which)]] + pt_free[i]
                        for h in range(4):
                            t = TR(b[:, h * P:h * P + P], R2[:, tt, 512 * which + P * h:512 * which + P * h + P], ident, *w, inc=(h == 3))
                            w = []
                        o, v = KQv[:, tt, :, col:col + P], h4(b)
                        t = A(lambda e, o=o, v=v: e.activation(o, v, ACT.Copy), t)
                        pt_free[i] = [t]
                        tkq[(tt, which)] = t
                    yield
                    q, k = R2[:, tt, 0:512], R2[:, tt, 512:1024]
                    cs = slice(4 * tt, 4 * tt + 4)
                    f = lambda s: bc(s[:, cs].unsqueeze(2), [P, 4, P])
                    tkbe = G(lambda e, tt=tt, k=k, s=f(bg): e.tensor_tensor(h4(KBE[:, tt, :]), h4(k), s, ALU.mult), vt[(tt, 1)], t6)
                    tkd = G(lambda e, k=k, s=f(dk): e.tensor_tensor(h4(k), h4(k), s, ALU.mult), tkbe, t5, tkq[(tt, 1)])
                    tqe = V(lambda e, q=q, s=f(eg): e.tensor_tensor(h4(q), h4(q), s, ALU.mult), t4, tkq[(tt, 0)])
                    st[("kd", tt)] = tkd
                    st[("kbe", tt)] = tkbe
                    (fl, fi), b = rot4()
                    grow = ARG[:, tt, :]
                    gsrc = bc(gg[:, cs].unsqueeze(2), [P, 4, P])
                    t = G(lambda e, grow=grow, gsrc=gsrc: e.tensor_copy(h4(grow), gsrc), gdep, *[vt[(1, n)] for n in range(3)])
                    w = [t] + fl[fi]
                    for h in range(4):
                        t = MM(b[:, h * P:h * P + P], grow[:, h * P:h * P + P], tab("cum"), True, True, *w, inc=(h == 3))
                        w = []
                    t = V(lambda e, grow=grow, b=b, s=f(gc): e.tensor_tensor(h4(grow), s, h4(b), ALU.subtract), t, t1)
                    fl[fi] = [t]
                    d, dt = DM[:, tt, :], DT[:, tt, :]
                    ta = V(lambda e, d=d, grow=grow: e.tensor_scalar(d, grow, 0.0, None, ALU.min), t)
                    tb = V(lambda e, dt=dt, grow=grow: e.tensor_scalar(dt, grow, -1.0, 0.0, ALU.mult, ALU.min), t)
                    ta = A(lambda e, d=d: e.activation(d, d, ACT.Exp), ta)
                    tb = A(lambda e, dt=dt: e.activation(dt, dt, ACT.Exp), tb)
                    m1, m2 = bc(tab("strict").unsqueeze(1), [P, 4, P]), bc(tab("inct").unsqueeze(1), [P, 4, P])
                    ta = V(lambda e, d=d, m1=m1: e.tensor_tensor(h4(d), h4(d), m1, ALU.mult), ta)
                    ta = V(lambda e, d=d, s=f(beta): e.tensor_tensor(h4(d), h4(d), s, ALU.mult), ta)
                    tb = G(lambda e, dt=dt, m2=m2: e.tensor_tensor(h4(dt), h4(dt), m2, ALU.mult), tb)
                    yield
                    i, b = pt()
                    w = [tqe] + pt_free[i]
                    for h in range(4):
                        t = TR(b[:, h * P:h * P + P], q[:, h * P:h * P + P], ident, *w, inc=(h == 3))
                        w = []
                    o, v = QE[:, :, tt * P:tt * P + P], h4(b)
                    t = A(lambda e, o=o, v=v: e.activation(o, v, ACT.Copy), t)
                    pt_free[i] = [t]
                    st[("qe", tt)] = t
                    for hp in range(2):
                        (fl, fi), b = rot4()
                        w = [tkq[(tt, 0)], tkq[(tt, 1)]] + fl[fi]
                        for h in range(2):
                            kq = KQv[:, tt, 2 * hp + h, :]
                            t = MM(b[:, h * S:h * S + S], kq[:, 0:P], kq, True, True, *w, inc=(h == 1))
                            w = []
                        bv = b.rearrange("p (h n) -> p h n", h=2)
                        hs = slice(256 * hp, 256 * hp + 256)
                        v2 = lambda ap: ap.rearrange("p (h n) -> p h n", h=2)
                        tA = V(lambda e, tt=tt, hs=hs, bv=bv, d=d: e.tensor_tensor(v2(Ar[:, tt, hs]), bv[:, :, 0:P], v2(d[:, hs]), ALU.mult), t, ta)
                        tQ = V(lambda e, tt=tt, hs=hs, bv=bv, dt=dt: e.tensor_tensor(v2(QKTv[:, tt, hs]), bv[:, :, P:S], v2(dt[:, hs]), ALU.mult), t, tb)
                        fl[fi] = [tA, tQ]
                    st[("A", tt)] = tA
                    st["qk"] = tQ
                    yield
                lev = lambda n: bc(tab("lev")[:, P * n:P * n + P].unsqueeze(1), [P, 4, P])
                l0t, idb = bc(tab("lev0t").unsqueeze(1), [P, 4, P]), bc(ident.unsqueeze(1), [P, 4, P])
                tat, tT, tTT = {}, {}, {}
                for tt in range(2):
                    i, b = pt()
                    w = [st[("A", 0)], st[("A", 1)]] + pt_free[i]
                    for h in range(4):
                        t = TR(b[:, h * P:h * P + P], Ar[:, tt, h * P:h * P + P], ident, *w, inc=(h == 3))
                        w = []
                    t = A(lambda e, tt=tt, b=b: e.activation(AT[:, tt, :], b, ACT.Copy), t)
                    pt_free[i] = [t]
                    tat[tt] = t
                    a, q, qq = Ar[:, tt, :], T[:, tt, :], TT[:, tt, :]
                    t1 = V(lambda e, a=a, q=q: e.tensor_tensor(h4(q), h4(a), l0t, ALU.mult), st[("A", 1)], t)
                    tT[tt] = V(lambda e, q=q: e.tensor_tensor(h4(q), idb, h4(q), ALU.subtract), t1)
                    t1 = G(lambda e, tt=tt, qq=qq: e.tensor_tensor(h4(qq), h4(AT[:, tt, :]), lev(0), ALU.mult), t)
                    tTT[tt] = G(lambda e, qq=qq: e.tensor_tensor(h4(qq), idb, h4(qq), ALU.subtract), t1)
                    yield
                xfree, efree = {}, {}
                for n in range(1, 6):
                    tx = {}
                    for tt in range(2):
                        te = G(lambda e, tt=tt, n=n: e.tensor_tensor(h4(Er[:, tt, :]), h4(AT[:, tt, :]), lev(n), ALU.mult), tat[tt],
                               *efree.get(tt, []))
                        (fl, fi), b = rot4()
                        w = [te, tT[tt]] + fl[fi]
                        for h in range(4):
                            c = slice(h * P, h * P + P)
                            t = MM(b[:, c], Er[:, tt, c], T[:, tt, c], True, True, *w, inc=(h == 3))
                            w = []
                        efree[tt] = [t]
                        tx[tt] = A(lambda e, tt=tt, b=b: e.activation(Ar[:, tt, :], b, ACT.Copy), t, tT[tt], *xfree.get(tt, []))
                        fl[fi] = [tx[tt]]
                    yield
                    for tt in range(2):
                        (f1, i1), b1 = rot4()
                        (f2, i2), b2 = rot4()
                        w = [tx[tt], tTT[tt]] + f1[i1]
                        if n < 5:
                            for h in range(4):
                                c = slice(h * P, h * P + P)
                                t1 = MM(b1[:, c], TT[:, tt, c], Ar[:, tt, c], True, True, *w, inc=(h == 3))
                                w = []
                        w = w + f2[i2]
                        for h in range(4):
                            c = slice(h * P, h * P + P)
                            t2 = MM(b2[:, c], Ar[:, tt, c], TT[:, tt, c], True, True, *w, inc=(h == 3))
                            w = []
                        if n < 5:
                            tT[tt] = V(lambda e, tt=tt, b=b1: e.tensor_tensor(T[:, tt, :], T[:, tt, :], b, ALU.subtract), t1, t2)
                            f1[i1] = [tT[tt]]
                        tTT[tt] = V(lambda e, tt=tt, b=b2: e.tensor_tensor(TT[:, tt, :], TT[:, tt, :], b, ALU.subtract), t2, tTT[tt])
                        f2[i2] = [tTT[tt]]
                        xfree[tt] = [t2]
                    yield
                for tt in range(2):
                    (f1, i1), b1 = rot4()
                    (f2, i2), b2 = rot4()
                    w = [tTT[tt], vt[(tt, 2)]] + f1[i1]
                    u = R2[:, tt, 1024:1536]
                    for h in range(4):
                        c = slice(h * P, h * P + P)
                        t1 = MM(b1[:, c], TT[:, tt, c], u[:, c], True, True, *w, inc=(h == 3))
                        w = []
                    w = [st[("kbe", tt)]] + f2[i2]
                    for h in range(4):
                        c = slice(h * P, h * P + P)
                        t2 = MM(b2[:, c], KBE[:, tt, c], TT[:, tt, c], True, True, *w, inc=(h == 3))
                        w = []
                    st[("u", tt)] = V(lambda e, u=u, b=b1: e.tensor_copy(u, b), t1)
                    st[("w", tt)] = A(lambda e, tt=tt, b=b2: e.activation(Er[:, tt, :], b, ACT.Copy), t2, *efree[tt])
                    f1[i1], f2[i2] = [st[("u", tt)]], [st[("w", tt)]]
                    yield
                st["solved"] = True

            O = T

            def scan():
                tS = None
                ot = {}
                for n in range(4):
                    tt, ro = n // 2, 64 * (n % 2)
                    row = slice(ro, ro + 64)
                    u = R2[:, tt, 1024:1536]
                    k = R2[:, tt, 512:1024]
                    tv = st[("u", tt)]
                    if n:
                        i, b = pt()
                        w = [st[("w", tt)], tS] + pt_free[i]
                        for h in range(4):
                            c = slice(h * P, h * P + P)
                            t = MM(b[row, c], Er[:, tt, h * P + ro:h * P + ro + 64], ST[:, c], True, True, *w, inc=(h == 3))
                            w = []
                        tv = V(lambda e, u=u, b=b, row=row: e.tensor_tensor(u[row, :], u[row, :], b[row, :], ALU.subtract), t, tv)
                        pt_free[i] = [tv]
                        yield
                    if n < 3:
                        i, b = pt()
                        w = [tv, st[("kd", tt)]] + pt_free[i]
                        for h in range(4):
                            c = slice(h * P, h * P + P)
                            t = MM(b[:, c], k[row, c], u[row, c], True, True, *w, inc=(h == 3))
                            w = []
                        old = ot.get("read", [])
                    i2, b2 = pt()
                    w = [tv, st["qk"], st[("qe", tt)]] + pt_free[i2]
                    for h in range(4):
                        c = slice(h * P, h * P + P)
                        if n:
                            MM(b2[row, c], QE[:, h, tt * P + ro:tt * P + ro + 64], ST[:, c], True, False, *w)
                            w = []
                        t2 = MM(b2[row, c], QKTv[row, tt, h * P + ro:h * P + ro + 64], u[row, c], n == 0, True, *w, inc=(h == 3))
                        w = []
                    if n < 3:
                        if n == 0:
                            tS = V(lambda e, b=b: e.tensor_copy(ST, b), t)
                        else:
                            for h in range(4):
                                c = slice(h * P, h * P + P)
                                s = egl[:, 4 * n + h:4 * n + h + 1]
                                tS = V(lambda e, b=b, c=c, s=s: e.scalar_tensor_tensor(ST[:, c], ST[:, c], s, b[:, c], ALU.mult, ALU.add),
                                       t, t2, st["egl"])
                        pt_free[i] = [tS]
                    to = A(lambda e, tt=tt, row=row, b=b2: e.activation(O[row, tt, :], b[row, :], ACT.Copy), t2)
                    pt_free[i2] = [to]
                    ot[n] = to
                    yield
                done_o = []
                for tt in range(2):
                    o = O[:, tt, :]
                    s4 = rsn[:, 4 * tt:4 * tt + 4]
                    t = A(lambda e, tt=tt, o=o: e.activation(Er[:, tt, :], o, ACT.Square), ot[2 * tt], ot[2 * tt + 1])
                    t = V(lambda e, tt=tt, s4=s4: e.tensor_reduce(s4, h4(Er[:, tt, :]), AX.X, ALU.add), t)
                    t = rsqrt(s4, 4, P * EPS, t)
                    t = V(lambda e, s4=s4: e.tensor_scalar(s4, s4, float(P) ** 0.5, None, ALU.mult), t)
                    t = V(lambda e, o=o, s4=s4: e.tensor_tensor(h4(o), h4(o), bc(s4.unsqueeze(2), [P, 4, P]), ALU.mult), t)
                    t = V(lambda e, o=o, tt=tt: e.tensor_tensor(o, o, Z[:, tt, :], ALU.mult), t, st["z"])
                    done_o.append(t)
                yield
                st["ydn"] = transposed(O, [0, 1, 2, 3], HH, HL, 0, done_o)
                yield

            hiq.append(solve())
            pair, outs, tok = unit()
            g_free[pair] = []
            for tt in range(2):
                t = A(lambda e, tt=tt, b=outs[tt]: e.activation(Z[:, tt, :], b, ACT.Sigmoid), tok)
                t = V(lambda e, tt=tt, b=outs[tt]: e.tensor_tensor(Z[:, tt, :], Z[:, tt, :], b, ALU.mult), t, tok)
                g_free[pair].append(t)
                st["z"] = V(lambda e, tt=tt: e.tensor_tensor(h4(Z[:, tt, :]), h4(Z[:, tt, :]), bc(tab("gout").unsqueeze(1), [P, 4, P]), ALU.mult), t, tdep)
            GAv = GA.rearrange("p (w t n) -> p w t n", w=2, t=2)
            gate_tok = []
            for gi in range(4):
                pair, outs, tok = unit()
                ts2 = []
                for tt in range(2):
                    o = GAv[:, gi // 2, tt, 512 * (gi % 2):512 * (gi % 2) + 512]
                    ts2.append(A(lambda e, o=o, b=outs[tt]: e.activation(o, b, ACT.Sigmoid), tok, ts))
                g_free[pair] = ts2
                gate_tok += ts2
            while "solved" not in st:
                pump()
            tB = dma("gpsimd", B, bass.AP(scr.tensor, 127, [[3071, P], [384, 8], [1, 256]]), "scr_in", [ts, st["qk"], st[("A", 1)]])
            hiq.append(scan())
            pair, outs, tok = unit()
            qT = AT.rearrange("p t (a n) -> p (t a) n", a=2)
            qT4 = AT.rearrange("p t n -> p (t n)").rearrange("p (c t) -> p c t", c=4)
            kbe_done = [st[("w", 0)], st[("w", 1)]]
            fin = []
            for tt in range(2):
                a, b = KBE[:, tt, :], outs[tt]
                s8 = t8a if tt == 0 else t8b
                t = A(lambda e, a=a, b=b: e.activation(a, b, ACT.Square), tok, *kbe_done)
                t = V(lambda e, a=a, s8=s8: e.tensor_reduce(s8, v3(a), AX.X, ALU.add), t)
                t = rsqrt(s8, 8, 64 * EPS, t)
                t = V(lambda e, a=a, b=b, s8=s8: e.tensor_tensor(v3(a), v3(b), bc(s8.unsqueeze(2), [P, 8, 64]), ALU.mult), t)
                fin.append(V(lambda e, a=a: e.tensor_tensor(v3(a), v3(a), bc(gq8.unsqueeze(1), [P, 8, 64]), ALU.mult), t, tg8))
            g_free[pair] = fin
            qt = []
            for tt in range(2):
                i, b = pt()
                w = [fin[tt], st[("A", 1)]] + pt_free[i]
                for c in range(4):
                    t = TR(b[:, c * P:c * P + P], KBE[:, tt, c * P:c * P + P], ident, *w, inc=(c == 3))
                    w = []
                t = A(lambda e, tt=tt, b=b: e.activation(qT4[:, :, tt * P:tt * P + P], b.rearrange("p (c t) -> p c t", c=4), ACT.Copy), t, *kbe_done)
                pt_free[i] = [t]
                qt.append(t)
                i, b = pt()
                t = TR(b[:, 0:P], SKV[:, tt, 0:P], ident, kdep, *pt_free[i], inc=True)
                t = A(lambda e, tt=tt, b=b: e.activation(kT[:, tt * P:tt * P + P], b[:, 0:P], ACT.Copy), t)
                pt_free[i] = [t]
                qt.append(t)
            s_free[0], s_free[1] = s_free[0] + b45_free[0], s_free[1] + b45_free[1]
            PP = [R1[:, 2048:2432], R1[:, 2432:2816], KQ[:, 1024:1408], KQ[:, 1408:1792], ar(384)]
            Aout = Ar
            items = []
            for h in range(8):
                c, row = h % 4, slice(64 * (h // 4), 64 * (h // 4) + 64)
                segs = [[(qT4[row, c, tt * P:tt * P + P], kT[row, 0:P * (tt + 1)], P * (tt + 1))] for tt in range(2)]
                items.append(dict(segs=segs, mask=[B[:, h, 128:256], B[:, h, 0:256]],
                                  v=[[SKV[:, b, 128 + 64 * (h // 4):192 + 64 * (h // 4)] for b in range(tt + 1)] for tt in range(2)],
                                  need=[], deps=qt + [vdep, tB], sink=nsink[:, h:h + 1], dst=Aout[:, :, 64 * h:64 * h + 64], dfree=kbe_done))

            def finish(toks):
                st["yswa"] = transposed(Aout, [0, 1, 2, 3], HH, HL, 4, toks)
                yield

            loq.append(attention(items, [bank[4], bank[5]], PP[0:3], PP[3:5], small[:, 192:224], finish, 2, False))
            while "ydn" not in st:
                pump()
            for i in range(2):
                tok = slot_wide((HH, HL, st["ydn"]), 2 * i, i == 0, i == 1, lambda tt: g_free[tt])
            tm = []
            for tt in range(2):
                o, b = GAv[:, 0, tt, :], ps[:, 1024 * tt:1024 * tt + 1024]
                tm.append(V(lambda e, o=o, b=b: e.tensor_tensor(o, o, b, ALU.mult), tok[2 * tt + 1], *gate_tok))
            while "yswa" not in st:
                pump()
            for i in range(2):
                tok = slot_wide((HH, HL, st["yswa"]), 4 + 2 * i, i == 0, i == 1, lambda tt: [tm[tt]])
            tn = []
            for tt in range(2):
                m, o, b = GAv[:, 0, tt, :], GAv[:, 1, tt, :], ps[:, 1024 * tt:1024 * tt + 1024]
                t = V(lambda e, o=o, b=b: e.tensor_tensor(o, o, b, ALU.mult), tok[2 * tt + 1])
                tn.append(V(lambda e, o=o, m=m: e.tensor_tensor(m, m, o, ALU.add), t))
            th = transposed(GAv[:, 0], list(range(8)), HH, HL, 0, tn)
            for i in range(4):
                tok = slot_wide((HH, HL, th), 2 * i, i == 0, i == 3, lambda tt: [tn[tt]])
            return tok

        keep_tok[0] = dma("scalar", keep[:, :], dram["keep"], "keep")
        for tt in range(2):
            xt.append([dma("sync", x[:, tt, :], dram["x"][0, tt * P:tt * P + P, :], f"x{tt}")] * 2)
        for n in range(RAW):
            load(n)
        for n in range(RING):
            split(n)
        stages = [lambda t: mixer("a", 3, kt("an0"), t, lambda: [hurry() for _ in range(3)]), lambda t: ffn(kt("cw0"), kt("fn0"), t),
                  lambda t: mixer("b", 1, kt("an1"), t), lambda t: ffn(kt("cw1"), kt("fn1"), t),
                  lambda t: third(kt("an2"), t), lambda t: ffn(None, kt("fn2"), t)]
        tok = None
        for s in stages:
            tok = s(tok)
        ends = residual(tok, 0) + residual(tok, 1)
        assert cur[0] == len(slots), (cur, len(slots))
        for tt in range(2):
            dma("sync", out[0, tt * P:tt * P + P, :], x[:, tt, :], f"out{tt}", ends[2 * tt:2 * tt + 2])
        for name, (s, v) in dmas.items():
            queue["sync"].append(lambda s=s, v=v: nc.sync.wait_ge(s, v))

        block = ctx.enter_context(nc.Block())

        @block.sync
        def _(e):
            for f in queue["sync"]:
                f()

        @block.gpsimd
        def _(e):
            for f in queue["gpsimd"]:
                f()

        @block.scalar
        def _(e):
            for f in queue["scalar"]:
                f()

        @block.vector
        def _(e):
            for f in queue["vector"]:
                f()

        @block.tensor
        def _(e):
            for f in queue["tensor"]:
                f()


def layout(inputs):
    a = {k: np.asarray(v) for k, v in inputs.items()}
    slots = plan()
    w = np.zeros((len(slots), P, 2048), np.float32)
    for n, (name, layer, ks, cols) in enumerate(slots):
        o = 0
        for k in ks:
            for nm in (name if isinstance(name, tuple) else (name,)):
                w[n, :, o:o + len(cols)] = a[nm][layer][k * P:k * P + P][:, cols]
                o += len(cols)
    con, tabs = constants(), tables()

    def rows(v):
        return np.broadcast_to(np.ascontiguousarray(v).reshape(1, -1), (P, v.size))

    def col(v):
        return v.reshape(-1, P).T

    def taps(*v):
        return np.stack([col(q) for q in v], 2).reshape(P, -1)

    relb = np.zeros((P, 8), np.float32)
    relb[0:32] = a["rel_bias_2"]
    cw, cb, dw = a["ffn_conv_w"], a["ffn_conv_b"], a["dn_conv_2"][0]
    values = {
        "keep": dict(ident=con["ident"], an0=col(a["attn_norm"][0]), an1=col(a["attn_norm"][1]), fn0=col(a["ffn_norm"][0]),
                     fn1=col(a["ffn_norm"][1]), an2=col(a["attn_norm_2"][0]), fn2=col(a["ffn_norm_2"][0]),
                     cw0=taps(cw[0, 0], cw[0, 1], cw[0, 2], cb[0]), cw1=taps(cw[1, 0], cw[1, 1], cw[1, 2], cb[1]),
                     dnw=taps(dw[0], dw[1], dw[2], dw[3]), mhalf=np.full((P, 16), -0.5, np.float32)),
        "a": dict(cos=con["cos"], sin=con["sin"], m0=con["am0"], m1=con["am1"],
                  gain=rows(np.stack([a["a_q_norm"][0], a["a_k_norm"][0]], 1))),
        "b": dict(cos=con["cos"], sin=con["sin"], m0=con["bm0"], m1=con["bm1"],
                  gain=rows(np.stack([a["b_q_norm"][0], a["b_k_norm"][0]], 0))),
        "c": dict(gq=rows(a["swa_q_norm_2"]), gk=rows(a["swa_k_norm_2"]), gout=rows(a["dn_out_norm_2"]), alog=rows(a["dn_a_log_2"]),
                  dtb=rows(a["dn_dt_bias_2"]), sink=rows(a["swa_sinks_2"]), relb=relb,
                  **{k: con[k] for k in ("cum", "blk", "sel", "strict", "inct", "lev", "lev0t")}),
    }
    arrays = {"x": a["x"], "w": w, "onehot": con["onehot"], "edge": np.ascontiguousarray(con["edge"])}
    for name, t in tabs.items():
        v = np.zeros((P, t.n), np.float32)
        for k, (o, n) in t.at.items():
            v[:, o:o + n] = values[name][k]
        arrays[name] = v
    return arrays


def kernel(**inputs):
    import concourse.bacc as bacc
    from concourse.bass_utils import run_bass_kernel_spmd

    nc = bacc.Bacc("TRN2", target_bir_lowering=False, num_devices=1)
    arrays = layout(inputs)
    dram = {k: nc.dram_tensor(f"in_{k}", v.shape, F32, kind="ExternalInput").ap() for k, v in arrays.items()}
    out = nc.dram_tensor("out", (1, S, D), F32, kind="ExternalOutput").ap()
    build(nc, dram, out)
    r = run_bass_kernel_spmd(nc, [{f"in_{k}": v for k, v in arrays.items()}], core_ids=[0])
    return r.results[0]["out"]
```

```python
from collections import deque
from contextlib import ExitStack

import numpy as np

import concourse.bass as bass
from concourse import mybir

F32 = mybir.dt.float32
F32R = mybir.dt.float32r
ALU = mybir.AluOpType
ACT = mybir.ActivationFunctionType
AX = mybir.AxisListType

P = 128
S = 256
D = 1024
FF = 2816
EPS = 1e-6
NEG = -1.0e30
BIG = 3.0e38
SCALE = 0.125
RAW, RING = 3, 3
DILATED = ((128, 1), (512, 4), (2048, 16))
DN0, Z0, BA0, SQ0, SK0, SV0, GT0 = 0, 1536, 2048, 2056, 2568, 2696, 2824


def r(a, b):
    return np.arange(a, b)


def cat(*a):
    return np.concatenate(a)


def qk_units(ng):
    return (((0, 0), (1, 0)), ((2, 0), (2, 1)), ((0, 1), (1, 1))) if ng == 3 else (((0, 0), (0, 1)),)


def plan():
    out = []

    def unit(name, layer, cols):
        for k in (0, 4):
            out.append((name, layer, list(range(k, k + 4)), cols))

    def wide(name, layer, n):
        for k in range(0, n, 2):
            out.append((name, layer, [k, k + 1], r(0, D)))

    def ffn(up, layer, off_gate, off_val, down):
        for i in range(13):
            if i < 11:
                g = r(256 * i, 256 * i + 256)
                if isinstance(up, tuple):
                    for k in (0, 4):
                        out.append((up, layer, list(range(k, k + 4)), g))
                else:
                    unit(up, layer, cat(g + off_gate, g + off_val))
            if i > 1:
                out.append((down, layer, [2 * i - 4, 2 * i - 3], r(0, D)))

    def qk(name, ng, hg):
        for blocks in qk_units(ng):
            unit(name, 0, cat(*[r(0, P) + 1024 * (ng * s + g) + 256 * hg + P * pr for g, pr in blocks for s in range(2)]))

    for half in range(2):
        for g in range(3):
            unit("a_w_qkv", 0, r(0, 512) + 6144 + 1024 * g + 512 * half)
        for hg in (2 * half, 2 * half + 1):
            qk("a_w_qkv", 3, hg)
    wide("a_w_o", 0, 8)
    ffn("ffn_w_up", 0, 0, FF, "ffn_w_down")
    for half in range(2):
        unit("b_w_qkv", 0, r(0, 512) + 2048 + 512 * half)
        for hg in (2 * half, 2 * half + 1):
            qk("b_w_qkv", 1, hg)
    wide("b_w_o", 0, 8)
    ffn("ffn_w_up", 1, 0, FF, "ffn_w_down")
    unit("w_in_2", 0, cat(r(BA0, BA0 + 8), r(SK0, SK0 + 256)))
    pairs = cat(*[cat(r(64 * h, 64 * h + 64), r(64 * h + 256, 64 * h + 320)) for h in range(4)])
    unit("w_in_2", 0, pairs + SQ0)
    for i in range(3):
        unit("w_in_2", 0, r(0, 512) + DN0 + 512 * i)
    unit("w_in_2", 0, r(Z0, Z0 + 512))
    for i in range(4):
        unit("w_in_2", 0, r(0, 512) + GT0 + 512 * i)
    wide("w_branch_swa_2", 0, 4)
    wide("w_branch_dn_2", 0, 4)
    wide("w_out_2", 0, 8)
    ffn(("w_gate_2", "w_up_2"), 0, 0, 0, "w_down_2")
    return out


class Table:

    def __init__(self):
        self.at, self.n = {}, 0

    def add(self, name, n):
        self.at[name] = (self.n, n)
        self.n += n


def tables():
    keep, a, b, c = Table(), Table(), Table(), Table()
    keep.add("ident", 128)
    for name in ("an0", "an1", "fn0", "fn1", "an2", "fn2"):
        keep.add(name, 8)
    keep.add("cw0", 176)
    keep.add("cw1", 176)
    keep.add("dnw", 48)
    keep.add("mhalf", 16)
    a.add("cos", 32)
    a.add("sin", 32)
    a.add("gain", 384)
    a.add("m0", 384)
    a.add("m1", 768)
    b.add("cos", 32)
    b.add("sin", 32)
    b.add("gain", 128)
    b.add("m0", 128)
    b.add("m1", 256)
    c.add("gq", 64)
    c.add("gk", 64)
    c.add("gout", 128)
    c.add("alog", 4)
    c.add("dtb", 4)
    c.add("sink", 8)
    c.add("relb", 8)
    c.add("cum", 128)
    c.add("blk", 128)
    c.add("sel", 256)
    c.add("strict", 128)
    c.add("lev", 768)
    c.add("lev0t", 128)
    return {"keep": keep, "a": a, "b": b, "c": c}


def constants():
    f = np.float32
    t = np.arange(S)
    inv = (500000.0 ** (-np.arange(0, 16, 2) / 16.0)).astype(f)
    ang = t.astype(f)[:, None] * inv[None, :]
    cos, sin = np.cos(ang), np.sin(ang)
    rope_c = np.concatenate([cos, cos], 1).reshape(2, P, 16).transpose(1, 0, 2).reshape(P, 32)
    rope_s = np.concatenate([-sin, sin], 1).reshape(2, P, 16).transpose(1, 0, 2).reshape(P, 32)
    dist = t[:, None] - t[None, :]

    def add(ok):
        return np.where(ok, 0.0, NEG).astype(f)

    dil = [add((dist >= 0) & (dist % d == 0) & (dist <= w)) for w, d in DILATED]
    causal = add(dist >= 0)
    i = np.arange(P)
    same = i[:, None] // 64 == i[None, :] // 64
    lev = []
    for n in range(6):
        b = 1 << n
        lev.append((i[None, :] // (2 * b) == i[:, None] // (2 * b)) & (i[None, :] % (2 * b) >= b) & (i[:, None] % (2 * b) < b))
    x = np.arange(384)
    sd = 255 - x
    ok = (sd >= 0) & (sd < 128)
    n = np.maximum(sd, 0)
    nf = np.maximum(n, 1).astype(f)
    large = np.minimum(16 + (np.log(nf / f(16)) / f(np.log(8.0)) * f(16)).astype(np.int32), 31)
    bucket = np.where(n < 16, n, large)
    onehot = np.where(ok[None, :] & (bucket[None, :] == np.arange(32)[:, None]), 8.0, 0.0).astype(f)[:, P:2 * P]
    return {
        "ident": np.eye(P, dtype=f),
        "cos": rope_c.astype(f), "sin": rope_s.astype(f),
        "am0": np.concatenate([m[:P, :P] for m in dil], 1), "am1": np.concatenate([m[P:] for m in dil], 1),
        "bm0": causal[:P, :P], "bm1": causal[P:],
        "cum": (same & (i[:, None] <= i[None, :])).astype(f),
        "blk": same.astype(f),
        "sel": np.concatenate([np.repeat((i[:, None] // 64 == c), P, 1) for c in range(2)], 1).astype(f),
        "strict": (same & (i[:, None] > i[None, :])).astype(f),
        "lev": np.concatenate(lev, 1).astype(f), "lev0t": lev[0].T.astype(f),
        "onehot": np.ascontiguousarray(onehot),
    }


def build(nc, dram, out):
    slots = plan()
    tabs = tables()
    with ExitStack() as ctx:
        def sb(name, shape, dt=F32):
            return ctx.enter_context(nc.sbuf_tensor(name, shape, dt))

        ENG = ("sync", "tensor", "vector", "scalar", "gpsimd")
        queue = {e: [] for e in ENG}
        count = {e: 0 for e in ENG}
        seen = {e: {} for e in ENG}
        done = {e: ctx.enter_context(nc.semaphore("done_" + e)) for e in ENG}
        handle = dict(tensor=nc.tensor, vector=nc.vector, scalar=nc.scalar, gpsimd=nc.gpsimd, sync=nc.sync)

        def op(e, fn, waits=(), inc=True):
            for s, v, name in waits:
                if seen[e].get(name, 0) < v:
                    seen[e][name] = v
                    queue[e].append(lambda h=handle[e], s=s, v=v: h.wait_ge(s, v))
            if inc:
                count[e] += 1
                queue[e].append(lambda: fn(handle[e]).then_inc(done[e], 1))
            else:
                queue[e].append(lambda: fn(handle[e]))
            return (done[e], count[e], e)

        dmas = {}

        def dma(e, dst, src, sem, waits=()):
            if sem not in dmas:
                dmas[sem] = [ctx.enter_context(nc.semaphore("dma_" + sem)), 0]
            dmas[sem][1] += 16
            s, v = dmas[sem]
            for w, wv, name in waits:
                if seen[e].get(name, 0) < wv:
                    seen[e][name] = wv
                    queue[e].append(lambda h=handle[e], w=w, wv=wv: h.wait_ge(w, wv))
            queue[e].append(lambda: handle[e].dma_start(dst, src).then_inc(s, 16))
            return (s, v, "dma_" + sem)

        def V(fn, *w):
            return op("vector", fn, w)

        def A(fn, *w):
            return op("scalar", fn, w)

        def G(fn, *w):
            return op("gpsimd", fn, w)

        def MM(o, l, rh, start, stop, *w, inc=False):
            return op("tensor", lambda e: e.matmul(o, l, rh, start=start, stop=stop, skip_group_check=True), w, inc)

        def TR(o, i, idn, *w, inc=False):
            return op("tensor", lambda e: e.transpose(o, i, idn), w, inc)

        x = sb("x", [P, 2, D])
        XH, XL = sb("XH", [P, 8, S], F32R), sb("XL", [P, 8, S], F32R)
        HH, HL = sb("HH", [P, 8, S], F32R), sb("HL", [P, 8, S], F32R)
        raw = [sb(f"raw{i}", [P, 2048]) for i in range(RAW)]
        wh = [sb(f"wh{i}", [P, 2048], F32R) for i in range(RING)]
        wl = [sb(f"wl{i}", [P, 2048], F32R) for i in range(RING)]
        keep = sb("keep", [P, tabs["keep"].n])
        small = sb("small", [P, 256])
        NAR = 23300
        arena = sb("arena", [P, NAR])
        ps = ctx.enter_context(nc.psum_tensor("ps", [P, 4096], F32))
        bank = [ps[:, 512 * i:512 * i + 512] for i in range(8)]
        scr = nc.dram_tensor("scr", (P * 8 * 384,), F32).ap()

        def kt(name):
            o, n = tabs["keep"].at[name]
            return keep[:, o:o + n]

        ident = kt("ident")
        used = [0]

        def ar(n):
            o = used[0]
            used[0] += n
            assert used[0] <= NAR, used
            return arena[:, o:o + n]

        def bc(ap, shape):
            return ap.to_broadcast(shape)

        raw_tok, hi_tok, lo_tok, use_tok = {}, {}, {}, {}

        def width(n):
            _, _, ks, cols = slots[n]
            c = len(cols) * (2 if isinstance(slots[n][0], tuple) else 1)
            return len(ks), c

        def load(n):
            if n >= len(slots):
                return
            k, c = width(n)
            w = (hi_tok[n - RAW], lo_tok[n - RAW]) if n >= RAW else ()
            raw_tok[n] = dma("sync", raw[n % RAW][:, 0:k * c], dram["w"][n, :, 0:k * c], f"raw{n % RAW}", w)

        def split(n):
            if n >= len(slots):
                return
            k, c = width(n)
            a, h, l = raw[n % RAW][:, 0:k * c], wh[n % RING][:, 0:k * c], wl[n % RING][:, 0:k * c]
            free = (use_tok[n - RING],) if n >= RING else ()
            m = k * c // 2
            sides = (slice(0, m), slice(m, 2 * m))
            th = {}

            def high(i):
                o = sides[i]
                th[i] = A(lambda e: e.activation(h[:, o], a[:, o], ACT.Copy), raw_tok[n], *free)

            def low(i):
                o = sides[i]
                t = V(lambda e: e.tensor_tensor(l[:, o], a[:, o], h[:, o].bitcast(F32), ALU.subtract), raw_tok[n], th[i], *free)
                if i:
                    hi_tok[n], lo_tok[n] = th[1], t
                    load(n + RAW)
            late.extend([[(high, 0)], [(high, 1), (low, 0)], [(low, 1)]])

        def hurry():
            for f, i in late.popleft():
                f(i)

        cur = [0]
        hiq, loq, late = deque(), deque(), deque()

        def step(q):
            while q:
                try:
                    next(q[0])
                    return
                except StopIteration:
                    q.popleft()

        def pump():
            for g in list(hiq):
                try:
                    next(g)
                except StopIteration:
                    hiq.remove(g)
            step(loq)
            if late:
                hurry()

        def drain():
            while hiq or loq:
                pump()

        def rsqrt(v, n, eps, *w):
            t = V(lambda e: e.tensor_scalar(v, v, eps, None, ALU.add), *w)
            return G(lambda e: e.tensor_tensor(v, v, kt("mhalf")[:, 0:n], ALU.pow), t, keep_tok[0])

        keep_tok = [None]

        def slot_views(n):
            while n not in lo_tok:
                hurry()
            k, c = width(n)
            v = lambda t: t[:, 0:k * c].rearrange("p (k c) -> p k c", k=k)
            return v(wh[n % RING]), v(wl[n % RING]), (hi_tok[n], lo_tok[n])

        def next_slot():
            n = cur[0]
            cur[0] += 1
            return n

        def after(n, tok):
            use_tok[n] = tok
            split(n + RING)

        def unit_tok(outs, act, free, nslots=2):
            tok = None
            for si in range(nslots):
                n = next_slot()
                h, l, w = slot_views(n)
                ah, al, aw = act
                c = width(n)[1]
                for tt in range(2):
                    ww = list(w) + aw[tt][si] + (list(free) if si == 0 else [])
                    for j in range(4):
                        kk = 4 * si + j
                        t = slice(tt * P, tt * P + P)
                        first, last = kk == 0, kk == 4 * nslots - 1
                        o = outs[tt][:, 0:c]
                        MM(o, ah[:, kk, t], h[:, j, :], first, False, *ww)
                        MM(o, ah[:, kk, t], l[:, j, :], False, False)
                        tok = MM(o, al[:, kk, t], h[:, j, :], False, last, inc=(j == 3))
                        ww = []
                        if j == 3 and tt == 1:
                            after(n, tok)
                        if j % 2:
                            pump()
            return tok

        def unit_chan(outs, act, free, pumps=True):
            tok = None
            for si in range(2):
                n = next_slot()
                h, l, w = slot_views(n)
                ah, al, aw = act
                for nt in range(4):
                    ww = list(w) + aw[0][si] + aw[1][si] + (list(free) if si == 0 else [])
                    o = outs[nt // 2][:, (nt % 2) * S:(nt % 2) * S + S]
                    cols = slice(nt * P, nt * P + P)
                    for j in range(4):
                        kk = 4 * si + j
                        MM(o, h[:, j, cols], ah[:, kk, :], kk == 0 and nt % 2 == 0, False, *ww)
                        MM(o, h[:, j, cols], al[:, kk, :], False, False)
                        tok = MM(o, l[:, j, cols], ah[:, kk, :], False, kk == 7, inc=(j == 3))
                        ww = []
                    if nt == 3:
                        after(n, tok)
                    pump()
            return tok

        def slot_wide(act, kbase, first, last, free):
            n = next_slot()
            h, l, w = slot_views(n)
            ah, al, aw = act
            toks = []
            for tt in range(2):
                for hf in range(2):
                    o = bank[2 * tt + hf]
                    ww = list(w) + list(aw) + (list(free(tt)) if first else [])
                    c = slice(512 * hf, 512 * hf + 512)
                    for j in range(2):
                        t = slice(tt * P, tt * P + P)
                        MM(o, ah[:, kbase + j, t], h[:, j, c], first and j == 0, False, *ww)
                        MM(o, ah[:, kbase + j, t], l[:, j, c], False, False)
                        tok = MM(o, al[:, kbase + j, t], h[:, j, c], False, last and j == 1, inc=(j == 1))
                        ww = []
                    toks.append(tok)
                    if tt == 1 and hf == 1:
                        after(n, tok)
                    if not (last and tt == 1 and hf == 1):
                        pump()
            return toks

        pt_free = [[], []]
        g_free = [[], []]
        ffn_free = [[], []]
        s_free, b45_free = [[], []], [[], []]
        pt_n = [0]

        def pt():
            i = pt_n[0] % 2
            pt_n[0] += 1
            return i, bank[6 + i]

        def so_far(*engines):
            return [(done[e], count[e], e) for e in engines]

        def fence(now):
            for e in ("tensor", "vector", "scalar", "gpsimd"):
                for s, v, name in now:
                    if name != e and v and seen[e].get(name, 0) < v:
                        seen[e][name] = v
                        queue[e].append(lambda h=handle[e], s=s, v=v: h.wait_ge(s, v))

        def transposed(src, kts, dh, dl, base, waits):
            toks = []
            for i0 in range(0, len(kts), 2):
                i, b = pt()
                grp = kts[i0:i0 + 2]
                n = len(grp)
                w = list(waits) + pt_free[i]
                for gi, k in enumerate(grp):
                    for tt in range(2):
                        t = TR(b[:, gi * S + tt * P:gi * S + tt * P + P], src[:, tt, k * P:k * P + P], ident, *w, inc=(gi == n - 1 and tt == 1))
                        w = []
                o = slice(base + i0, base + i0 + n)
                v = b[:, 0:n * S].rearrange("p (k t) -> p k t", k=n)
                th = A(lambda e, o=o, v=v: e.activation(dh[:, o, :], v, ACT.Copy), t)
                tl = V(lambda e, o=o, v=v: e.tensor_tensor(dl[:, o, :], v, dh[:, o, :].bitcast(F32), ALU.subtract), t, th)
                toks += [th, tl]
                pt_free[i] = [th, tl]
            return toks

        xs = arena[:, NAR - 2048:NAR].rearrange("p (t d) -> p t d", t=2)
        xt = []

        def residual(tok, tt):
            out = []
            for hf in range(2):
                o, i = x[:, tt, 512 * hf:512 * hf + 512], bank[2 * tt + hf]
                out.append(V(lambda e, o=o, i=i: e.tensor_tensor(o, i, o, ALU.add), tok[2 * tt + hf]))
            g_free[tt] = out
            return out

        def norm_x(gains, tok, between=lambda: None):
            base = so_far("vector", "scalar", "gpsimd")
            sums, rs, scaled, toks = small[:, 0:4], small[:, 4:6], [], [[], []]
            for tt in range(2):
                tx = residual(tok, tt) if tok else xt[tt]
                ts = []
                for hf in range(2):
                    c = slice(512 * hf, 512 * hf + 512)
                    ts.append(A(lambda e, tt=tt, c=c, s=sums[:, 2 * tt + hf:2 * tt + hf + 1]: e.activation(
                        xs[:, tt, c], x[:, tt, c], ACT.Square, accum_out=s), tx[hf]))
                a, b, v = sums[:, 2 * tt:2 * tt + 1], sums[:, 2 * tt + 1:2 * tt + 2], rs[:, tt:tt + 1]
                t = V(lambda e, a=a, b=b, v=v: e.scalar_tensor_tensor(v, a, D * EPS, b, ALU.add, ALU.add), *ts)
                scaled.append(G(lambda e, v=v: e.tensor_tensor(v, v, kt("mhalf")[:, 0:1], ALU.pow), t, keep_tok[0]))
            for tt in range(2):
                scaled[tt] = [V(lambda e, tt=tt, v=rs[:, tt:tt + 1], c=slice(512 * hf, 512 * hf + 512): e.tensor_scalar(
                    xs[:, tt, c], x[:, tt, c], v, 32.0, ALU.mult, ALU.mult), scaled[tt]) for hf in range(2)]
            free = {n: g_free[1] if n in (2, 3) else base for n in range(2, 8)}
            for tt in range(2):
                if tt:
                    between()
                for ci, n in enumerate(((4, 5, 6, 7), (2, 3, 4, 5))[tt]):
                    b, k0 = bank[n], 2 * ci
                    w = [scaled[tt][k0 // 4], keep_tok[0]] + free[n]
                    for k in range(2):
                        t = TR(b[:, k * P:k * P + P], xs[:, tt, (k0 + k) * P:(k0 + k) * P + P], ident, *w, inc=(k == 1))
                        w = []
                    each = [(b[:, k * P:k * P + P], XH[:, k0 + k, tt * P:tt * P + P], XL[:, k0 + k, tt * P:tt * P + P],
                             gains[:, k0 + k:k0 + k + 1]) for k in range(2)]
                    for v, h, l, g in each:
                        th = A(lambda e, v=v, h=h, g=g: e.activation(h, v, ACT.Copy, scale=g), t)
                    for v, h, l, g in each:
                        tl = V(lambda e, v=v, h=h, l=l, g=g: e.scalar_tensor_tensor(l, v, g, h.bitcast(F32), ALU.mult, ALU.subtract), t, th)
                    free[n] = [th, tl]
                    toks[tt].append([th, tl])
            toks = [[a[0] + a[1], a[2] + a[3]] for a in toks]
            g_free[1] = free[2] + free[3]
            s_free[0] = s_free[1] = b45_free[0] = b45_free[1] = free[4] + free[5]
            pt_free[0], pt_free[1] = free[6], free[7]
            return toks

        def attention(items, area, Pb, PTb, st, finish, parts, halves):
            N = len(items)
            R = len(Pb)
            state = {}

            def scores(i):
                it = items[i]
                for ut in it["need"]:
                    it["deps"] = it["deps"] + ut
                sp, f = area[i % len(area)], i % len(area)
                w = list(it["deps"]) + s_free[f]
                o, spans = 0, []
                for pi, segs in enumerate(it["segs"]):
                    o0 = o
                    for si, (q, k, n) in enumerate(segs):
                        t = MM(sp[:, o:o + n], q, k, True, True, *w, inc=(si == len(segs) - 1))
                        w = []
                        o += n
                    spans.append((o0, o))
                back = [state[i - R]["pt"]] if i >= R else []
                c = 2 * (i % 4)
                nm = st[:, c:c + 2]
                for pi, (a, b) in enumerate(spans):
                    t1 = V(lambda e, a=a, b=b, pi=pi, m=it["mask"][pi], p=Pb[i % R]: e.tensor_tensor_reduce(
                        p[:, a:b], sp[:, a:b], m, -SCALE, BIG, ALU.add, ALU.min, nm[:, pi:pi + 1]), t, *back)
                s_free[f] = [t1]
                if it.get("sink") is not None:
                    sk, es = bc(it["sink"], [P, 2]), st[:, 24 + c:26 + c]
                    t1 = V(lambda e: e.tensor_tensor(nm, nm, sk, ALU.min), t1)
                    t3 = V(lambda e: e.tensor_tensor(es, nm, sk, ALU.subtract), t1)
                    state[i, "es"] = A(lambda e: e.activation(es, es, ACT.Exp), t3)
                state[i] = {"m": t1, "n": o, "spans": spans}

            def exps(i):
                s, p, c = state[i], Pb[i % R], 2 * (i % 4)
                for pi, (a, b) in enumerate(s["spans"]):
                    nm, den = st[:, c + pi:c + pi + 1], st[:, 8 + c + pi:9 + c + pi]
                    s["p"] = A(lambda e, a=a, b=b, nm=nm, den=den: e.activation(p[:, a:b], p[:, a:b], ACT.Exp, bias=nm, scale=-1.0, accum_out=den), s["m"])

            def turn(i):
                s = state[i]
                nb = s["n"] // P
                toks = []
                back = [state[i - 2]["pv"]] if i >= 2 else []
                for b0 in range(0, nb, 3):
                    bn = min(3, nb - b0)
                    j, bk = pt()
                    w = [s["p"]] + pt_free[j]
                    for b in range(bn):
                        t = TR(bk[:, b * P:b * P + P], Pb[i % R][:, (b0 + b) * P:(b0 + b) * P + P], ident, *w, inc=(b == bn - 1))
                        w = []
                    o, c = PTb[i % 2][:, b0 * P:(b0 + bn) * P], bk[:, 0:bn * P]
                    if b0 == 0:
                        t2 = A(lambda e, o=o, c=c: e.activation(o, c, ACT.Copy), t, *back)
                    else:
                        t2 = V(lambda e, o=o, c=c: e.tensor_copy(o, c), t, *back)
                    pt_free[j] = [t2]
                    toks.append(t2)
                s["pt"] = t
                s["ptc"] = toks
                c = 2 * (i % 4)
                den, rd = st[:, 8 + c:8 + c + parts], st[:, 16 + c:16 + c + parts]
                t3 = s["p"]
                if (i, "es") in state:
                    es = st[:, 24 + c:24 + c + parts]
                    t3 = V(lambda e: e.tensor_tensor(den, den, es, ALU.add), t3, state[i, "es"])
                s["rd"] = V(lambda e: e.reciprocal(rd, den), t3, *([state[i - 4]["on"]] if i >= 4 else []))

            def pv(i):
                s, it = state[i], items[i]
                j, bk = pt()
                w = s["ptc"] + pt_free[j] + list(it["deps"])
                for pi, (a, e) in enumerate(s["spans"]):
                    nb = (e - a) // P
                    for b in range(nb):
                        t = MM(bk[:, 64 * pi:64 * pi + 64], PTb[i % 2][:, a + b * P:a + b * P + P], it["v"][pi][b], b == 0, b == nb - 1, *w,
                               inc=(b == nb - 1 and pi == parts - 1))
                        w = []
                s["pv"] = t
                c = 2 * (i % 4)
                rd, dst = bc(st[:, 16 + c:16 + c + parts].unsqueeze(2), [P, parts, 64]), it["dst"]
                o = bk[:, 0:64 * parts].rearrange("p (a d) -> p a d", a=parts)
                s["on"] = V(lambda e: e.tensor_tensor(dst, o, rd, ALU.mult), t, s["rd"], *it.get("dfree", ()))
                pt_free[j] = [s["on"]]

            lag = 2 if halves else 3
            for i in range(N + lag + 1):
                while i < N and any(len(ut) < 2 for ut in items[i]["need"]):
                    yield
                if i > lag:
                    pv(i - lag - 1)
                if halves:
                    if i < N:
                        scores(i)
                    yield
                if lag <= i < N + lag:
                    turn(i - lag)
                if halves:
                    if i < N:
                        exps(i)
                else:
                    if 1 <= i <= N:
                        exps(i - 1)
                    if i < N:
                        scores(i)
                yield
            yield from finish([state[i]["on"] for i in range(N)])

        v3 = lambda ap: ap.rearrange("p (h d) -> p h d", d=64)
        v4 = lambda ap: ap.rearrange("p (s h d) -> p s h d", s=2, d=64)

        def load_table(name, waits):
            n = tabs[name].n
            t = ar(n)
            tok = dma("gpsimd", t, dram[name], "tab_" + name, waits)
            return (lambda k: t[:, tabs[name].at[k][0]:tabs[name].at[k][0] + tabs[name].at[k][1]]), tok

        def rope_tables(tab, ng, GC, GS, dep):
            cosv = tab("cos").rearrange("p (t d) -> p t d", t=2)
            sinv = tab("sin").rearrange("p (t d) -> p t d", t=2)
            gv = tab("gain").rearrange("p (g s d) -> p g s d", g=ng, s=2)
            last = None
            for g in range(ng):
                for tt in range(2):
                    cb = bc(cosv[:, tt, :].unsqueeze(1), [P, 2, 16])
                    s0 = bc(sinv[:, tt, 0:8].unsqueeze(1), [P, 2, 8])
                    s1 = bc(sinv[:, tt, 8:16].unsqueeze(1), [P, 2, 8])
                    gg, cc, ss = gv[:, g], GC[:, g, tt], GS[:, g, tt]
                    V(lambda e, gg=gg, cc=cc: e.tensor_scalar(cc[:, :, 16:64], gg[:, :, 16:64], 8.0, None, ALU.mult), dep)
                    V(lambda e, gg=gg, cc=cc, cb=cb: e.scalar_tensor_tensor(cc[:, :, 0:16], gg[:, :, 0:16], 8.0, cb, ALU.mult, ALU.mult))
                    V(lambda e, gg=gg, ss=ss, s0=s0: e.scalar_tensor_tensor(ss[:, :, 0:8], gg[:, :, 8:16], 8.0, s0, ALU.mult, ALU.mult))
                    last = V(lambda e, gg=gg, ss=ss, s1=s1: e.scalar_tensor_tensor(ss[:, :, 8:16], gg[:, :, 0:8], 8.0, s1, ALU.mult, ALU.mult))
            return last

        def mixer(tabname, ng, norm_gain, last, between=lambda: None):
            used[0] = 0
            now = so_far("tensor", "vector", "scalar", "gpsimd")
            tab, tdep = load_table(tabname, now)
            GC = ar(ng * 256).rearrange("p (g t s d) -> p g t s d", g=ng, t=2, s=2)
            GS = ar(ng * 64).rearrange("p (g t s d) -> p g t s d", g=ng, t=2, s=2)
            Vt = ar(2 * ng * D).rearrange("p (t g n) -> p t g n", t=2, g=ng)
            qkT = [ar(ng * 1024).rearrange("p (g c t) -> p g c t", g=ng, c=4) for _ in range(2)]
            sqs, qn, tp, ssb = [[ar(512), ar(512)]], [ar(512), ar(512)], [ar(128), ar(128)], small[:, 16:32]
            sqs.append([arena[:, NAR - 1280 + 512 * i:NAR - 768 + 512 * i] for i in range(2)])
            np_ = 768 if ng == 3 else 384
            Pb, PTb = [ar(np_), ar(np_), arena[:, NAR - 2048:NAR - 2048 + np_]], [ar(np_), ar(np_)]
            att = [ar(512).rearrange("p (t d) -> p t d", t=2) for _ in range(2)]
            assert used[0] <= NAR - 2048, used
            act = (XH, XL, norm_x(norm_gain, last, between))
            fence(now)
            td = rope_tables(tab, ng, GC, GS, tdep)
            vt, att_free, qk_free, out_tok = [], [[], []], [[], []], {}
            rope_done, turned, nq = [[], []], [[[], []], [[], []]], [0]
            un = [0]

            def heads(pair, tok, blocks, T, wfree, ut, wait):
                sq, was = sqs[nq[0] % 2], turned[nq[0] % 2]
                nq[0] += 1
                sqt = [A(lambda e, a=sq[tt], src=bank[2 * pair + tt]: e.activation(a, src, ACT.Square), tok, *was[tt]) for tt in range(2)]

                def go():
                    for tt in range(2):
                        t2 = V(lambda e, a=sq[tt], ss=ssb[:, 8 * tt:8 * tt + 8]: e.tensor_reduce(ss, v3(a), AX.X, ALU.add), sqt[tt])
                    t3 = rsqrt(ssb, 16, 64 * EPS, t2)
                    yield
                    yield
                    free, fin = list(sqt), []
                    for tt in range(2):
                        src, a, b = bank[2 * pair + tt], sq[tt], qn[tt]
                        rs = bc(ssb[:, 8 * tt:8 * tt + 8].unsqueeze(2), [P, 8, 64])
                        t4 = V(lambda e, b=b, src=src, rs=rs: e.tensor_tensor(v3(b), v3(src), rs, ALU.mult), t3, tok, *rope_done[tt])
                        free.append(t4)
                        v5 = lambda ap, d: ap.rearrange("p (j s h d) -> p j s h d", j=2, s=2, d=d)
                        av, bv, tv = v5(a, 64), v5(b, 64), v5(tp[tt], 16)
                        for bl, (g, _) in enumerate(blocks):
                            gc = bc(GC[:, g, tt].unsqueeze(2), [P, 2, 2, 64])
                            t5 = V(lambda e, bl=bl, av=av, bv=bv, gc=gc: e.tensor_tensor(av[:, bl], bv[:, bl], gc, ALU.mult), t4, td)
                        for bl, (g, _) in enumerate(blocks):
                            for q in range(2):
                                m = bc(GS[:, g, tt, :, 8 * q:8 * q + 8].unsqueeze(2), [P, 2, 2, 8])
                                o, i = tv[:, bl, :, :, 8 * q:8 * q + 8], bv[:, bl, :, :, 8 - 8 * q:16 - 8 * q]
                                t6 = G(lambda e, o=o, i=i, m=m: e.tensor_tensor(o, i, m, ALU.mult), t4, td)
                        tq = tp[tt].rearrange("p (h d) -> p h d", d=16)
                        t7 = G(lambda e, a=a, tq=tq: e.tensor_tensor(v3(a)[:, :, 0:16], v3(a)[:, :, 0:16], tq, ALU.add), t5, t6)
                        rope_done[tt] = [t7]
                        fin.append(t7)
                    g_free[pair] = free
                    for _ in range(wait):
                        yield
                    for tt in range(2):
                        i, b = pt()
                        w = [fin[tt]] + pt_free[i]
                        for c in range(4):
                            t = TR(b[:, c * P:c * P + P], sq[tt][:, c * P:c * P + P], ident, *w, inc=(c == 3))
                            w = []
                        was[tt] = [t]
                        (g, pr), ts_ = blocks[0], slice(tt * P, tt * P + P)
                        if blocks[1][0] == g:
                            o = T[:, g].rearrange("p (s r) t -> p r s t", s=2)[:, :, :, ts_]
                        else:
                            o = T[:, g:g + 2].rearrange("p g (s r) t -> p g s r t", s=2)[:, :, :, pr, ts_]
                        v = b.rearrange("p (j s t) -> p j s t", j=2, s=2)
                        t = A(lambda e, o=o, v=v: e.activation(o, v, ACT.Copy), t, *wfree)
                        pt_free[i] = [t]
                        ut.append(t)
                        yield
                g_free[pair] = None
                hiq.append(go())

            def finish_for(hg):
                def finish(toks):
                    qk_free[hg % 2] = toks
                    yield
                    out_tok[hg] = transposed(att[hg % 2], [0, 1], HH, HL, 2 * hg, toks)
                    att_free[hg % 2] = [(done["tensor"], count["tensor"], "tensor")]
                    yield
                return finish

            def group(hg, units):
                items = []
                T = qkT[hg % 2]
                tiles = [(0,), (1,)] if ng == 3 else [(0, 1)]
                for h in range(4):
                    pr, row = h // 2, slice(64 * (h % 2), 64 * (h % 2) + 64)
                    hc = 64 * (4 * hg + h)
                    need = [ut for bl, ut in units if any(b[1] == pr for b in bl)]
                    for tts in tiles:
                        segs = [[(T[row, g, pr, tt * P:tt * P + P], T[row, g, 2 + pr, 0:P * (tt + 1)], P * (tt + 1)) for g in range(ng)] for tt in tts]
                        v = [[Vt[:, b, g, hc:hc + 64] for g in range(ng) for b in range(tt + 1)] for tt in tts]
                        items.append(dict(segs=segs, mask=[tab(f"m{tt}") for tt in tts], v=v, need=need, deps=vt + [tdep],
                                          dst=att[hg % 2][:, tts[0]:tts[-1] + 1, 64 * h:64 * h + 64], dfree=att_free[hg % 2]))
                area = [ps[:, 2048:2048 + 768]] if ng == 3 else [bank[4], bank[5]]
                yield from attention(items, area, Pb, PTb, small[:, 192:224], finish_for(hg), len(tiles[0]), ng == 3)

            def free_of(pair):
                while g_free[pair] is None:
                    pump()
                return g_free[pair]

            for half in range(2):
                for g in range(ng):
                    pair = un[0] % 2
                    un[0] += 1
                    tok = unit_tok([bank[2 * pair], bank[2 * pair + 1]], act, free_of(pair))
                    toks = []
                    for tt in range(2):
                        o, b = Vt[:, tt, g, 512 * half:512 * half + 512], bank[2 * pair + tt]
                        toks.append(A(lambda e, o=o, b=b: e.activation(o, b, ACT.Copy), tok))
                    vt += toks
                    g_free[pair] = toks
                for hg in (2 * half, 2 * half + 1):
                    while hg >= 2 and (hg - 2) not in out_tok:
                        pump()
                    units = [(blocks, []) for blocks in qk_units(ng)]
                    loq.append(group(hg, units))
                    for blocks, ut in units:
                        pair = un[0] % 2
                        un[0] += 1
                        tok = unit_tok([bank[2 * pair], bank[2 * pair + 1]], act, free_of(pair))
                        heads(pair, tok, blocks, qkT[hg % 2], qk_free[hg % 2], ut, 3 if hg == 3 and ut is units[-1][1] else 6)
            for i in range(4):
                while i not in out_tok:
                    pump()
                tok = slot_wide((HH, HL, out_tok[i]), 2 * i, i == 0, i == 3, free_of)
            drain()
            return tok

        def ffn(cw, norm_gain, last):
            used[0] = 0
            Y = [ar(1024).rearrange("p (n t) -> p n t", n=4) for _ in range(2)]
            base = so_far("vector", "scalar", "gpsimd")
            act = (XH, XL, norm_x(norm_gain, last))
            free, hfree, htok, yfree = [b45_free[0] + base, pt_free[0] + pt_free[1] + base], {}, {}, [base, base]
            for i in range(13):
                if i < 11:
                    p = i % 2
                    y = Y[p]
                    bb = [bank[4 + 2 * p], bank[5 + 2 * p]]
                    tok = unit_chan(bb, act, free[p])
                    u = [bb[n // 2][:, (n % 2) * S:(n % 2) * S + S] for n in range(4)]
                    if cw is None:
                        t = A(lambda e, y=y, b=bb[0]: e.activation(y[:, 0:2, :].rearrange("p n t -> p (n t)"), b, ACT.Silu), tok, *yfree[p])
                        t2 = V(lambda e, y=y, b=bb[1]: e.tensor_tensor(y[:, 2:4, :].rearrange("p n t -> p (n t)"),
                                                                       y[:, 0:2, :].rearrange("p n t -> p (n t)"), b, ALU.mult), t, tok, *yfree[p])
                        free[p] = [t, t2]
                    else:
                        ts, t1 = [], []
                        each = []
                        for n in range(4):
                            ch = 2 * i + n if n < 2 else 22 + 2 * i + n - 2
                            w = cw[:, 4 * ch:4 * ch + 4]
                            yn, un = y[:, n, :], u[n]
                            each.append((n, w, yn, un))
                            t1.append(A(lambda e, yn=yn, un=un, w=w: e.activation(yn, un, ACT.Identity, bias=w[:, 3:4], scale=w[:, 2:3]), tok, *yfree[p]))
                        for n, w, yn, un in each:
                            t2 = V(lambda e, yn=yn, un=un, w=w: e.scalar_tensor_tensor(yn[:, 1:S], un[:, 0:S - 1], w[:, 1:2], yn[:, 1:S], ALU.mult, ALU.add), t1[n | 1], tok)
                            t3 = V(lambda e, yn=yn, un=un, w=w: e.scalar_tensor_tensor(yn[:, 2:S], un[:, 0:S - 2], w[:, 0:1], yn[:, 2:S], ALU.mult, ALU.add), t2)
                            ts.append(t3)
                        free[p] = [t1[3], t3]
                        t = A(lambda e, y=y: e.activation(y[:, 0:2, :], y[:, 0:2, :], ACT.Silu), ts[1])
                        t2 = V(lambda e, y=y: e.tensor_tensor(y[:, 2:4, :], y[:, 0:2, :], y[:, 2:4, :], ALU.mult), t, ts[3])
                    k = (2 * i) % 8
                    back = [hfree[i - 4]] if i >= 4 else []
                    th = A(lambda e, y=y, k=k: e.activation(HH[:, k:k + 2, :], y[:, 2:4, :], ACT.Copy), t2, *back)
                    tl = V(lambda e, y=y, k=k: e.tensor_tensor(HL[:, k:k + 2, :], y[:, 2:4, :], HH[:, k:k + 2, :].bitcast(F32), ALU.subtract), th, *back)
                    htok[i] = [th, tl]
                    yfree[p] = [th, tl]
                if i > 1:
                    d = i - 2
                    tok = slot_wide((HH, HL, htok[d]), (2 * d) % 8, d == 0, d == 10, lambda tt: g_free[tt])
                    hfree[d] = tok[3]
            return tok

        rot = [0]
        def rot4():
            i = rot[0] % 4
            rot[0] += 1
            return (b45_free, i) if i < 2 else (pt_free, i - 2), bank[4 + i]

        def third(norm_gain, last):
            used[0] = 0
            now = so_far("tensor", "vector", "scalar", "gpsimd")
            tab, tdep = load_table("c", now)
            R1, R2 = ar(3072), ar(3072).rearrange("p (t n) -> p t n", t=2)
            KQ = ar(2048)
            QE = ar(1024).rearrange("p (h t) -> p h t", h=4)
            KBE = ar(1024).rearrange("p (t n) -> p t n", t=2)
            Ar, AT = [ar(1024).rearrange("p (t n) -> p t n", t=2) for _ in range(2)]
            Er = ar(1024).rearrange("p (t n) -> p t n", t=2)
            QKT = ar(1024)
            ST = ar(512)
            kT = ar(256)
            SKVf = ar(512)
            SKV = SKVf.rearrange("p (t n) -> p t n", t=2)
            Z = ar(1024).rearrange("p (t n) -> p t n", t=2)
            GA = ar(4096)
            GAv = GA.rearrange("p (w t n) -> p w t n", w=2, t=2)
            XT = R1.rearrange("p (c t) -> p c t", c=12)
            KQv = KQ.rearrange("p (t h n) -> p t h n", t=2, h=4)
            T = KQ[:, 0:1024].rearrange("p (t n) -> p t n", t=2)
            TT = KQ[:, 1024:2048].rearrange("p (t n) -> p t n", t=2)
            ARG, DM, DT = [R1[:, 1024 * i:1024 * i + 1024].rearrange("p (t n) -> p t n", t=2) for i in range(3)]
            QKTv = QKT.rearrange("p (t n) -> p t n", t=2)
            B = GA[:, 0:2048].rearrange("p (h n) -> p h n", h=8)
            PP = [GA[:, 2048 + 384 * i:2432 + 384 * i] for i in range(5)]
            Aout, qT = Z, AT.rearrange("p t n -> p (t n)").rearrange("p (c t) -> p c t", c=4)
            h4 = lambda ap: ap.rearrange("p (h d) -> p h d", h=4)
            sv = lambda a, n: small[:, a:a + n]
            beta, gg, gc, eg, dk, bg = [sv(64 + 8 * i, 8) for i in range(6)]
            gl, egl, t8a, t8b, t8c, rsn = sv(112, 8), sv(120, 16), sv(136, 8), sv(144, 8), sv(152, 8), sv(160, 16)
            nsink, gq8, gk8, sqs = sv(176, 8), tab("gq"), tab("gk"), sv(224, 16)
            act = (XH, XL, norm_x(norm_gain, last))
            fence(now)
            act_tok = sum(act[2][0] + act[2][1], [])
            st, silu_tok, un = {}, {}, [0]
            onehot = QKT[0:32, 0:128]
            td1 = dma("gpsimd", onehot, dram["onehot"], "tab_onehot", now)
            for q in (gq8, gk8):
                tg8 = V(lambda e, q=q: e.tensor_scalar(q, q, 8.0, None, ALU.mult), tdep)
            tg8 = V(lambda e: e.tensor_scalar(nsink, tab("sink"), -1.0, None, ALU.mult), tdep)
            qt, kvt, bt = [], [], []

            def bias():
                lines = GA[:, 0:3072].rearrange("p (h n) -> p h n", h=8)
                relb = GA[0:32, 3072:4096].rearrange("p (h n) -> p h n", h=8)
                t = G(lambda e: e.tensor_copy(relb, bc(tab("relb")[0:32, :].unsqueeze(2), [32, 8, P])), tdep, *act_tok)
                for o in (0, 2 * P):
                    tm = G(lambda e, o=o: e.memset(lines[:, :, o:o + P], NEG), *act_tok)
                for _ in range(6):
                    yield
                rows = [tm]
                for hh in range(2):
                    i, b = pt()
                    w = [t, td1] + pt_free[i]
                    for h in range(4):
                        tt_ = MM(b[:, h * P:h * P + P], relb[:, 4 * hh + h, :], onehot, True, True, *w, inc=(h == 3))
                        w = []
                    rows.append(A(lambda e, hh=hh, b=b: e.activation(lines[:, 4 * hh:4 * hh + 4, P:2 * P], h4(b), ACT.Copy), tt_))
                    pt_free[i] = [rows[-1]]
                ts = dma("gpsimd", scr.rearrange("(p n) -> p n", p=P), GA[:, 0:3072], "scr_out", rows)
                for _ in range(5):
                    yield
                tB = dma("gpsimd", B, bass.AP(scr.tensor, 127, [[3071, P], [384, 8], [1, 256]]), "scr_in", [ts])
                bt.extend([tB, tB])

            def unit(chan=False):
                pair = un[0] % 2
                un[0] += 1
                while g_free[pair] is None:
                    pump()
                outs = [bank[2 * pair], bank[2 * pair + 1]]
                return pair, outs, (unit_chan if chan else unit_tok)(outs, act, g_free[pair])

            raw_rows = Er[:, :, 0:264]
            t8 = lambda ap: ap.rearrange("p (t h) -> p t h", t=2)

            def scalars(raws):
                b, a = raw_rows[:, :, 0:4], raw_rows[:, :, 4:8]
                k, kk = raw_rows[:, :, 8:136], SKV[:, :, 0:P]
                k4 = lambda ap: ap.rearrange("p t (h d) -> p t h d", h=2)
                sk = rsn[:, 0:4]
                tb = A(lambda e: e.activation(t8(t8a), b, ACT.Exp, scale=-1.0), *raws)
                tk = A(lambda e: e.activation(kk, k, ACT.Square), *raws)
                z, q, u1, l = gc, t8b, t8c, gg
                dtb = bc(tab("dtb").unsqueeze(1), [P, 2, 4])
                t = V(lambda e: e.tensor_tensor(t8(z), a, dtb, ALU.add), tdep, *raws)
                t = V(lambda e: e.scalar_tensor_tensor(q, z, -1.0, z, ALU.mult, ALU.max), t)
                tq = A(lambda e: e.activation(q, q, ACT.Exp, scale=-1.0), t)
                yield
                tb = V(lambda e: e.tensor_scalar(t8a, t8a, 1.0, None, ALU.add), tb)
                st["beta"] = tbeta = V(lambda e: e.reciprocal(beta, t8a), tb)
                tk = V(lambda e: e.tensor_reduce(sk.rearrange("p (t h) -> p t h", t=2), k4(kk), AX.X, ALU.add), tk)
                tk = rsqrt(sk, 4, 64 * EPS, tk)
                yield
                t1 = V(lambda e: e.tensor_scalar(u1, q, 1.0, None, ALU.add), tq)
                tl = A(lambda e: e.activation(l, u1, ACT.Ln), t1)
                t2 = V(lambda e: e.reciprocal(t8a, u1), t1, tbeta)
                yield
                t3 = V(lambda e: e.tensor_scalar(u1, u1, -1.0, None, ALU.add), t2, tl)
                t3 = V(lambda e: e.tensor_tensor(q, q, u1, ALU.subtract), t3)
                t3 = V(lambda e: e.tensor_tensor(q, q, t8a, ALU.mult), t3, t2)
                t3 = V(lambda e: e.tensor_tensor(l, l, q, ALU.add), t3, tl)
                t3 = V(lambda e: e.scalar_tensor_tensor(l, z, 0.0, l, ALU.max, ALU.add), t3)
                ta = A(lambda e: e.activation(t8c[:, 0:4], tab("alog"), ACT.Exp), t3, tdep)
                rs = bc(sk.rearrange("p (t h) -> p t h", t=2).unsqueeze(3), [P, 2, 2, 64])
                tk = V(lambda e: e.tensor_tensor(k4(kk), k4(k), rs, ALU.mult), tk)
                gkb = bc(gk8.unsqueeze(1).unsqueeze(1), [P, 2, 2, 64])
                tk = V(lambda e: e.tensor_tensor(k4(kk), k4(kk), gkb, ALU.mult), tk, tg8)
                tv = A(lambda e: e.activation(SKV[:, :, P:2 * P], raw_rows[:, :, 136:264], ACT.Copy), *raws)
                st["raw_end"] = [tk, tv]
                yield
                yield
                al = bc(t8c[:, 0:4].unsqueeze(1), [P, 2, 4])
                st["g"] = tg = V(lambda e: e.scalar_tensor_tensor(t8(l), t8(l), -1.0, al, ALU.mult, ALU.mult), ta, t3)
                i, bk = pt()
                for tt in range(2):
                    t = TR(bk[:, tt * P:tt * P + P], SKV[:, tt, 0:P], ident, tk, *pt_free[i], inc=(tt == 1))
                t = A(lambda e: e.activation(kT, bk[:, 0:S], ACT.Copy), t)
                pt_free[i] = [t]
                kvt.extend([t, tv])
                yield
                i, bsum = pt()
                w = [tg, tdep] + pt_free[i]
                for tt in range(2):
                    gs = gg[:, 4 * tt:4 * tt + 4]
                    MM(bsum[:, 4 * tt:4 * tt + 4], tab("cum"), gs, True, True, *w)
                    MM(bsum[:, 8 + 4 * tt:12 + 4 * tt], tab("blk"), gs, True, True)
                    for c in range(2):
                        o = 16 + 8 * tt + 4 * c
                        t = MM(bsum[:, o:o + 4], tab("sel")[:, P * c:P * c + P], gs, True, True, inc=True)
                    w = []
                t1 = V(lambda e: e.tensor_copy(gc, bsum[:, 0:8]), t)
                t2 = V(lambda e: e.tensor_tensor(gl, bsum[:, 8:16], gc, ALU.subtract), t, t1)
                t3 = A(lambda e: e.activation(egl, bsum[:, 16:32], ACT.Exp), t2)
                t4 = A(lambda e: e.activation(eg, gc, ACT.Exp), t1)
                t5 = A(lambda e: e.activation(dk, gl, ACT.Exp), t2)
                t6 = V(lambda e: e.tensor_tensor(bg, beta, eg, ALU.mult), t4, tbeta)
                pt_free[i] = [t2, t3]
                st["gc"], st["egl"], st["eg"], st["dk"], st["bg"] = t1, t3, t4, t5, t6

            def band_q(pair, outs, tok):
                ta = [A(lambda e, tt=tt: e.activation(R2[:, tt, 512:1024], outs[tt], ACT.Square), tok) for tt in range(2)]

                def go():
                    for tt in range(2):
                        t = V(lambda e, tt=tt: e.tensor_reduce(sqs[:, 8 * tt:8 * tt + 8], v3(R2[:, tt, 512:1024]), AX.X, ALU.add), ta[tt])
                    t = rsqrt(sqs, 16, 64 * EPS, t)
                    yield
                    yield
                    fin = []
                    for tt in range(2):
                        a, rs = R2[:, tt, 0:512], bc(sqs[:, 8 * tt:8 * tt + 8].unsqueeze(2), [P, 8, 64])
                        t1 = V(lambda e, a=a, rs=rs, tt=tt: e.tensor_tensor(v3(a), v3(outs[tt]), rs, ALU.mult), t, ta[tt])
                        fin.append(V(lambda e, a=a: e.tensor_tensor(v3(a), v3(a), bc(gq8.unsqueeze(1), [P, 8, 64]), ALU.mult), t1, tg8))
                    g_free[pair] = list(fin)
                    for _ in range(3):
                        yield
                    for tt in range(2):
                        i, b = pt()
                        w = [fin[tt]] + pt_free[i]
                        for c in range(4):
                            t = TR(b[:, c * P:c * P + P], R2[:, tt, c * P:c * P + P], ident, *w, inc=(c == 3))
                            w = []
                        t = A(lambda e, tt=tt, b=b: e.activation(qT[:, :, tt * P:tt * P + P], h4(b), ACT.Copy), t)
                        pt_free[i] = [t]
                        qt.append(t)
                        yield
                g_free[pair] = None
                hiq.append(go())

            def conv(i, pair, outs, tok):
                dnw = kt("dnw")
                each = [(4 * i + n, dnw[:, 16 * i + 4 * n:16 * i + 4 * n + 4], XT[:, 4 * i + n, :], outs[n // 2][:, (n % 2) * S:(n % 2) * S + S])
                        for n in range(4)]
                ta = [A(lambda e, yn=yn, u=u, w=w: e.activation(yn, u, ACT.Copy, scale=w[:, 3:4]), tok) for _, w, yn, u in each]

                def go():
                    for n, (ch, w, yn, u) in enumerate(each):
                        tv = ta[n | 1]
                        for d in range(1, 4):
                            tv = V(lambda e, yn=yn, u=u, w=w, d=d: e.scalar_tensor_tensor(yn[:, d:S], u[:, 0:S - d], w[:, 3 - d:4 - d], yn[:, d:S],
                                                                                         ALU.mult, ALU.add), tv, tok)
                        if n % 2:
                            yn2 = XT[:, ch - 1:ch + 1, :]
                            silu_tok[ch - 1] = silu_tok[ch] = A(lambda e, yn2=yn2: e.activation(yn2, yn2, ACT.Silu), tv)
                        if n == 3:
                            g_free[pair] = [ta[3], tv]
                        yield
                g_free[pair] = None
                hiq.append(go())

            def solve():
                while len(silu_tok) < 12 or "yswa" not in st:
                    yield
                b45_free[0], b45_free[1] = b45_free[0] + s_free[0], b45_free[1] + s_free[1]
                order = [(tt, g) for g in (1, 0, 2) for tt in range(2)]
                vt, hold, read = {}, {}, {}
                for j in range(8):
                    if j >= 2 and order[j - 2][1] != 2:
                        tt, g = order[j - 2]
                        fl, fi, b, t, s4, tp_ = hold[j - 2]
                        if g == 0:
                            tp_ = V(lambda e, s4=s4: e.tensor_scalar(s4, s4, float(P) ** -0.5, None, ALU.mult), tp_)
                        o, tb = R2[:, tt, 512 * g:512 * g + 512], bc(s4.unsqueeze(2), [P, 4, P])
                        vt[(tt, g)] = V(lambda e, o=o, b=b, tb=tb: e.tensor_tensor(h4(o), h4(b), tb, ALU.mult), tp_, t)
                        fl[fi] = [vt[(tt, g)]]
                    if 1 <= j <= 6 and order[j - 1][1] != 2:
                        tt, g = order[j - 1]
                        fl, fi, b, t, s4 = hold[j - 1]
                        read[(j - 1) % 2] = V(lambda e, j=j, s4=s4: e.tensor_reduce(s4, h4(Er[:, (j - 1) % 2, :]), AX.X, ALU.add), t)
                        hold[j - 1] = (fl, fi, b, t, s4, rsqrt(s4, 4, EPS, read[(j - 1) % 2]))
                    if j < 6:
                        tt, g = order[j]
                        (fl, fi), b = rot4()
                        w = [silu_tok[4 * g + 3], silu_tok[4 * g + 1]] + fl[fi]
                        for c in range(4):
                            t = TR(b[:, c * P:c * P + P], XT[:, 4 * g + c, tt * P:tt * P + P], ident, *w, inc=(c == 3))
                            w = []
                        st["xt_end"] = t
                        if g == 2:
                            o, tb = R2[:, tt, 1024:1536], bc(beta[:, 4 * tt:4 * tt + 4].unsqueeze(2), [P, 4, P])
                            vt[(tt, 2)] = V(lambda e, o=o, b=b, tb=tb: e.tensor_tensor(h4(o), h4(b), tb, ALU.mult), t, st["beta"])
                            fl[fi] = [vt[(tt, 2)]]
                        else:
                            back = [read[j % 2]] if j % 2 in read else []
                            t = A(lambda e, b=b, j=j: e.activation(Er[:, j % 2, :], b, ACT.Square), t, st["gc"], *back, *st["raw_end"])
                            hold[j] = (fl, fi, b, t, rsn[:, 4 * (j % 4):4 * (j % 4) + 4])
                    yield
                f = lambda s, tt: bc(s[:, 4 * tt:4 * tt + 4].unsqueeze(2), [P, 4, P])
                tgr = [A(lambda e, tt=tt, s=f(gg, tt): e.activation(h4(ARG[:, tt, :]), s, ACT.Copy), st["g"], st["xt_end"]) for tt in range(2)]
                tkq, tdm, tdt = {}, {}, {}
                for tt in range(2):
                    for which, col in ((1, 0), (0, P)):
                        (fl, fi), b = rot4()
                        w = [vt[(tt, which)]] + fl[fi]
                        for h in range(4):
                            t = TR(b[:, h * P:h * P + P], R2[:, tt, 512 * which + P * h:512 * which + P * h + P], ident, *w, inc=(h == 3))
                            w = []
                        o, v = KQv[:, tt, :, col:col + P], h4(b)
                        t = A(lambda e, o=o, v=v: e.activation(o, v, ACT.Copy), t)
                        fl[fi] = [t]
                        tkq[(tt, which)] = t
                    (fl, fi), b = rot4()
                    grow = ARG[:, tt, :]
                    w = [tgr[tt], tdep] + fl[fi]
                    for h in range(4):
                        t = MM(b[:, h * P:h * P + P], grow[:, h * P:h * P + P], tab("cum"), True, True, *w, inc=(h == 3))
                        w = []
                    t = V(lambda e, grow=grow, b=b, s=f(gc, tt): e.tensor_tensor(h4(grow), s, h4(b), ALU.subtract), t, st["gc"])
                    fl[fi] = [t]
                    d, dt = DM[:, tt, :], DT[:, tt, :]
                    ta = V(lambda e, d=d, grow=grow: e.tensor_scalar(d, grow, 0.0, None, ALU.min), t)
                    tb = V(lambda e, dt=dt, grow=grow: e.tensor_scalar(dt, grow, -1.0, 0.0, ALU.mult, ALU.min), t)
                    tdm[tt] = A(lambda e, d=d: e.activation(d, d, ACT.Exp), ta)
                    tdt[tt] = A(lambda e, dt=dt: e.activation(dt, dt, ACT.Exp), tb)
                    yield
                for tt in range(2):
                    d, dt = DM[:, tt, :], DT[:, tt, :]
                    m1, m2 = bc(tab("strict").unsqueeze(1), [P, 4, P]), bc(tab("cum").unsqueeze(1), [P, 4, P])
                    tb = G(lambda e, dt=dt, m2=m2: e.tensor_tensor(h4(dt), h4(dt), m2, ALU.mult), tdt[tt])
                    ta = V(lambda e, d=d, m1=m1: e.tensor_tensor(h4(d), h4(d), m1, ALU.mult), tdm[tt])
                    ta = V(lambda e, d=d, s=f(beta, tt): e.tensor_tensor(h4(d), h4(d), s, ALU.mult), ta)
                    for hp in range(2):
                        (fl, fi), b = rot4()
                        w = [tkq[(tt, 0)], tkq[(tt, 1)]] + fl[fi]
                        for h in range(2):
                            kq = KQv[:, tt, 2 * hp + h, :]
                            t = MM(b[:, h * S:h * S + S], kq[:, 0:P], kq, True, True, *w, inc=(h == 1))
                            w = []
                        bv = b.rearrange("p (h n) -> p h n", h=2)
                        hs = slice(256 * hp, 256 * hp + 256)
                        v2 = lambda ap: ap.rearrange("p (h n) -> p h n", h=2)
                        tA = V(lambda e, tt=tt, hs=hs, bv=bv, d=d: e.tensor_tensor(v2(Ar[:, tt, hs]), bv[:, :, 0:P], v2(d[:, hs]), ALU.mult), t, ta)
                        tQ = V(lambda e, tt=tt, hs=hs, bv=bv, dt=dt: e.tensor_tensor(v2(QKTv[:, tt, hs]), bv[:, :, P:S], v2(dt[:, hs]), ALU.mult), t, tb)
                        fl[fi] = [tA, tQ]
                    st[("A", tt)] = tA
                    st["qk"] = tQ
                    yield
                lev = lambda n: bc(tab("lev")[:, P * n:P * n + P].unsqueeze(1), [P, 4, P])
                l0t, idb = bc(tab("lev0t").unsqueeze(1), [P, 4, P]), bc(ident.unsqueeze(1), [P, 4, P])
                ring = [[Er[:, 0, :], Er[:, 1, :]], [ST, SKVf]]
                tat, tT, tTT, te, efree, tx, xfree = {}, {}, {}, {}, {}, {}, {}

                def mask(n, tt, E=G):
                    o = ring[n % 2][tt]
                    te[(n, tt)] = E(lambda e: e.tensor_tensor(h4(o), h4(AT[:, tt, :]), lev(n), ALU.mult), tat[tt], *efree.get((n - 2, tt), []))

                for tt in range(2):
                    (fl, fi), b = rot4()
                    w = [st[("A", tt)]] + fl[fi]
                    for h in range(4):
                        t = TR(b[:, h * P:h * P + P], Ar[:, tt, h * P:h * P + P], ident, *w, inc=(h == 3))
                        w = []
                    tat[tt] = A(lambda e, tt=tt, b=b: e.activation(AT[:, tt, :], b, ACT.Copy), t)
                    fl[fi] = [tat[tt]]
                    a, q = Ar[:, tt, :], T[:, tt, :]
                    t1 = V(lambda e, a=a, q=q: e.tensor_tensor(h4(q), h4(a), l0t, ALU.mult), st[("A", 1)], st["qk"], tat[tt])
                    tT[tt] = V(lambda e, q=q: e.tensor_tensor(h4(q), idb, h4(q), ALU.subtract), t1)
                    mask(1, tt, (G, V)[tt])
                    yield
                for tt, E in ((0, G), (1, V)):
                    qq = TT[:, tt, :]
                    t1 = E(lambda e, tt=tt, qq=qq: e.tensor_tensor(h4(qq), h4(AT[:, tt, :]), lev(0), ALU.mult), tat[tt], st["qk"], st[("A", 1)])
                    tTT[tt] = E(lambda e, qq=qq: e.tensor_tensor(h4(qq), idb, h4(qq), ALU.subtract), t1)

                def first(n, tt):
                    (fl, fi), b = rot4()
                    w = [te[(n, tt)], tT[tt]] + fl[fi]
                    E = ring[n % 2][tt]
                    for h in range(4):
                        c = slice(h * P, h * P + P)
                        t = MM(b[:, c], E[:, c], T[:, tt, c], True, True, *w, inc=(h == 3))
                        w = []
                    efree[(n, tt)] = [t]
                    tx[tt] = A(lambda e: e.activation(Ar[:, tt, :], b, ACT.Copy), t, tT[tt], *xfree.get(tt, []))
                    fl[fi] = [tx[tt]]
                    if n < 5:
                        mask(n + 1, tt)

                def second(n, tt):
                    (f1, i1), b1 = rot4()
                    (f2, i2), b2 = rot4()
                    w = [tx[tt], tTT[tt]] + f1[i1]
                    if n < 5:
                        for h in range(4):
                            c = slice(h * P, h * P + P)
                            t1 = MM(b1[:, c], TT[:, tt, c], Ar[:, tt, c], True, True, *w, inc=(h == 3))
                            w = []
                    w = w + f2[i2]
                    for h in range(4):
                        c = slice(h * P, h * P + P)
                        t2 = MM(b2[:, c], Ar[:, tt, c], TT[:, tt, c], True, True, *w, inc=(h == 3))
                        w = []
                    if n < 5:
                        tT[tt] = V(lambda e: e.tensor_tensor(T[:, tt, :], T[:, tt, :], b1, ALU.subtract), t1)
                        f1[i1] = [tT[tt]]
                    tTT[tt] = V(lambda e: e.tensor_tensor(TT[:, tt, :], TT[:, tt, :], b2, ALU.subtract), t2, tTT[tt])
                    f2[i2] = [tTT[tt]]
                    xfree[tt] = [t2]

                def apply(tt):
                    (f1, i1), b1 = rot4()
                    (f2, i2), b2 = rot4()
                    w = [tTT[tt], vt[(tt, 2)]] + f1[i1]
                    u = R2[:, tt, 1024:1536]
                    for h in range(4):
                        c = slice(h * P, h * P + P)
                        t1 = MM(b1[:, c], TT[:, tt, c], u[:, c], True, True, *w, inc=(h == 3))
                        w = []
                    w = [st[("kbe", tt)]] + f2[i2]
                    for h in range(4):
                        c = slice(h * P, h * P + P)
                        t2 = MM(b2[:, c], KBE[:, tt, c], TT[:, tt, c], True, True, *w, inc=(h == 3))
                        w = []
                    st[("u", tt)] = V(lambda e: e.tensor_copy(u, b1), t1)
                    st[("w", tt)] = A(lambda e: e.activation(Er[:, tt, :], b2, ACT.Copy), t2, *efree[(4, tt)])
                    f1[i1], f2[i2] = [st[("u", tt)]], [st[("w", tt)]]

                def queries(tt):
                    q, k = R2[:, tt, 0:512], R2[:, tt, 512:1024]
                    if ("qs", tt) not in st:
                        st[("kbe", tt)] = t = G(lambda e: e.tensor_tensor(h4(KBE[:, tt, :]), h4(k), f(bg, tt), ALU.mult), vt[(tt, 1)], st["bg"])
                        st[("kd", tt)] = G(lambda e: e.tensor_tensor(h4(k), h4(k), f(dk, tt), ALU.mult), t, st["dk"], tkq[(tt, 1)])
                        st[("qs", tt)] = V(lambda e: e.tensor_tensor(h4(q), h4(q), f(eg, tt), ALU.mult), st["eg"], tkq[(tt, 0)])
                        return
                    (fl, fi), b = rot4()
                    w = [st[("qs", tt)]] + fl[fi]
                    for h in range(4):
                        t = TR(b[:, h * P:h * P + P], q[:, h * P:h * P + P], ident, *w, inc=(h == 3))
                        w = []
                    st[("qe", tt)] = A(lambda e: e.activation(QE[:, :, tt * P:tt * P + P], h4(b), ACT.Copy), t)
                    fl[fi] = [st[("qe", tt)]]

                for n in range(1, 7):
                    if n <= 5:
                        first(n, 0)
                    if n >= 2:
                        second(n - 1, 1)
                    yield
                    if n <= 5:
                        second(n, 0)
                        first(n, 1)
                    if n in (2, 3):
                        queries(n - 2)
                    if n in (4, 5):
                        queries(n - 4)
                    yield
                    if n == 5:
                        apply(0)
                apply(1)
                yield
                yield from scan()

            O = T

            def out_norm(tt):
                o = O[:, tt, :]
                s4 = rsn[:, 4 * tt:4 * tt + 4]
                t = A(lambda e: e.activation(KBE[:, tt, :], o, ACT.Square), st[("o", 2 * tt)], st[("o", 2 * tt + 1)], st[("w", 1)])
                yield
                t = V(lambda e: e.tensor_reduce(s4, h4(KBE[:, tt, :]), AX.X, ALU.add), t)
                t = rsqrt(s4, 4, P * EPS, t)
                yield
                t = V(lambda e: e.tensor_scalar(s4, s4, float(P) ** 0.5, None, ALU.mult), t)
                t = V(lambda e: e.tensor_tensor(h4(o), h4(o), bc(s4.unsqueeze(2), [P, 4, P]), ALU.mult), t)
                st[("on", tt)] = V(lambda e: e.tensor_tensor(o, o, Z[:, tt, :], ALU.mult), t, st["z"])

            def scan():
                tS = None
                for n in range(4):
                    tt, ro = n // 2, 64 * (n % 2)
                    row = slice(ro, ro + 64)
                    u = R2[:, tt, 1024:1536]
                    k = R2[:, tt, 512:1024]
                    tv = st[("u", tt)]
                    if n:
                        (fl, fi), b = rot4()
                        w = [st[("w", tt)], tS] + fl[fi]
                        for h in range(4):
                            c = slice(h * P, h * P + P)
                            t = MM(b[row, c], Er[:, tt, h * P + ro:h * P + ro + 64], ST[:, c], True, True, *w, inc=(h == 3))
                            w = []
                        tv = V(lambda e, u=u, b=b, row=row: e.tensor_tensor(u[row, :], u[row, :], b[row, :], ALU.subtract), t, tv)
                        fl[fi] = [tv]
                        yield
                    if n < 3:
                        (fl, fi), b = rot4()
                        w = [tv, st[("kd", tt)]] + fl[fi]
                        for h in range(4):
                            c = slice(h * P, h * P + P)
                            t = MM(b[:, c], k[row, c], u[row, c], True, True, *w, inc=(h == 3))
                            w = []
                    (f2, i2), b2 = rot4()
                    w = [tv, st["qk"], st[("qe", tt)]] + f2[i2]
                    for h in range(4):
                        c = slice(h * P, h * P + P)
                        if n:
                            MM(b2[row, c], QE[:, h, tt * P + ro:tt * P + ro + 64], ST[:, c], True, False, *w)
                            w = []
                        t2 = MM(b2[row, c], QKTv[row, tt, h * P + ro:h * P + ro + 64], u[row, c], n == 0, True, *w, inc=(h == 3))
                        w = []
                    if n < 3:
                        if n == 0:
                            tS = V(lambda e, b=b: e.tensor_copy(ST, b), t)
                        else:
                            for h in range(4):
                                c = slice(h * P, h * P + P)
                                s = egl[:, 4 * n + h:4 * n + h + 1]
                                tS = V(lambda e, b=b, c=c, s=s: e.scalar_tensor_tensor(ST[:, c], ST[:, c], s, b[:, c], ALU.mult, ALU.add),
                                       t, t2, st["egl"])
                        fl[fi] = [tS]
                    st[("o", n)] = A(lambda e, tt=tt, row=row, b=b2: e.activation(O[row, tt, :], b[row, :], ACT.Copy), t2)
                    f2[i2] = [st[("o", n)]]
                    yield
                    if n == 1:
                        hiq.append(out_norm(0))
                yield from out_norm(1)
                yield
                st["ydn"] = transposed(O, [0, 1, 2, 3], HH, HL, 0, [st[("on", 0)], st[("on", 1)]])

            hiq.append(bias())
            pair, outs, tok = unit()
            raws = [A(lambda e, tt=tt, b=outs[tt]: e.activation(raw_rows[:, tt, :], b[:, 0:264], ACT.Copy), tok) for tt in range(2)]
            g_free[pair] = raws
            hiq.append(scalars(raws))
            band_q(*unit())
            items = []
            for h in range(8):
                c, row = h % 4, slice(64 * (h // 4), 64 * (h // 4) + 64)
                segs = [[(qT[row, c, tt * P:tt * P + P], kT[row, 0:P * (tt + 1)], P * (tt + 1))] for tt in range(2)]
                items.append(dict(segs=segs, mask=[B[:, h, 128:256], B[:, h, 0:256]],
                                  v=[[SKV[:, b, 128 + 64 * (h // 4):192 + 64 * (h // 4)] for b in range(tt + 1)] for tt in range(2)],
                                  need=[qt, kvt, bt], deps=[], sink=nsink[:, h:h + 1], dst=Aout[:, :, 64 * h:64 * h + 64]))

            def finish(toks):
                yield
                st["yswa"] = transposed(Aout, [0, 1, 2, 3], HH, HL, 4, toks)
                st["swa_end"] = so_far("tensor", "vector", "scalar")
                yield

            loq.append(attention(items, [bank[4], bank[5]], PP[0:3], PP[3:5], small[:, 192:224], finish, 2, False))
            for i in range(3):
                pair, outs, tok = unit(True)
                conv(i, pair, outs, tok)
            hiq.append(solve())
            pair, outs, tok = unit()
            while "yswa" not in st:
                pump()
            g_free[pair] = []
            for tt in range(2):
                t = A(lambda e, tt=tt, b=outs[tt]: e.activation(Z[:, tt, :], b, ACT.Sigmoid), tok, *st["swa_end"])
                t = V(lambda e, tt=tt, b=outs[tt]: e.tensor_tensor(Z[:, tt, :], Z[:, tt, :], b, ALU.mult), t, tok)
                g_free[pair].append(t)
                st["z"] = V(lambda e, tt=tt: e.tensor_tensor(h4(Z[:, tt, :]), h4(Z[:, tt, :]), bc(tab("gout").unsqueeze(1), [P, 4, P]), ALU.mult), t, tdep)
            gate_tok = []
            for gi in range(4):
                pair, outs, tok = unit()
                ts2 = []
                for tt in range(2):
                    o = GAv[:, gi // 2, tt, 512 * (gi % 2):512 * (gi % 2) + 512]
                    ts2.append(A(lambda e, o=o, b=outs[tt]: e.activation(o, b, ACT.Sigmoid), tok, *st["swa_end"]))
                g_free[pair] = ts2
                gate_tok += ts2
            for i in range(2):
                tok = slot_wide((HH, HL, st["yswa"][2 * i:2 * i + 2]), 4 + 2 * i, i == 0, i == 1, lambda tt: g_free[tt])

            def gated(w, tok):
                out = []
                for tt in range(2):
                    for hf in range(2):
                        o, b = GAv[:, w, tt, 512 * hf:512 * hf + 512], bank[2 * tt + hf]
                        out.append(V(lambda e, o=o, b=b: e.tensor_tensor(o, o, b, ALU.mult), tok[2 * tt + hf], *gate_tok))
                return out

            tm = gated(1, tok)
            while "ydn" not in st:
                pump()
            for i in range(2):
                tok = slot_wide((HH, HL, st["ydn"][2 * i:2 * i + 2]), 2 * i, i == 0, i == 1, lambda tt: tm[2 * tt:2 * tt + 2])
            tn = {}
            for hf in range(2):
                for tt in range(2):
                    c = slice(512 * hf, 512 * hf + 512)
                    m, o, b = GAv[:, 0, tt, c], GAv[:, 1, tt, c], bank[2 * tt + hf]
                    t = V(lambda e, m=m, b=b: e.tensor_tensor(m, m, b, ALU.mult), tok[2 * tt + hf], *gate_tok)
                    tn[(tt, hf)] = V(lambda e, o=o, m=m: e.tensor_tensor(m, m, o, ALU.add), t, *tm)
            th = []
            for hf in range(2):
                th += transposed(GAv[:, 0], list(range(4 * hf, 4 * hf + 4)), HH, HL, 4 * hf, [tn[(0, hf)], tn[(1, hf)]])
            for i in range(4):
                tok = slot_wide((HH, HL, th[2 * i:2 * i + 2]), 2 * i, i == 0, i == 3, lambda tt: [tn[(tt, 0)], tn[(tt, 1)]])
            return tok

        keep_tok[0] = dma("scalar", keep[:, :], dram["keep"], "keep")
        for tt in range(2):
            xt.append([dma("sync", x[:, tt, :], dram["x"][0, tt * P:tt * P + P, :], f"x{tt}")] * 2)
        for n in range(RAW):
            load(n)
        for n in range(RING):
            split(n)
        stages = [lambda t: mixer("a", 3, kt("an0"), t, lambda: [hurry() for _ in range(3)]), lambda t: ffn(kt("cw0"), kt("fn0"), t),
                  lambda t: mixer("b", 1, kt("an1"), t), lambda t: ffn(kt("cw1"), kt("fn1"), t),
                  lambda t: third(kt("an2"), t), lambda t: ffn(None, kt("fn2"), t)]
        tok = None
        for s in stages:
            tok = s(tok)
        ends = residual(tok, 0) + residual(tok, 1)
        assert cur[0] == len(slots), (cur, len(slots))
        for tt in range(2):
            dma("sync", out[0, tt * P:tt * P + P, :], x[:, tt, :], f"out{tt}", ends[2 * tt:2 * tt + 2])
        for name, (s, v) in dmas.items():
            queue["sync"].append(lambda s=s, v=v: nc.sync.wait_ge(s, v))

        block = ctx.enter_context(nc.Block())

        @block.sync
        def _(e):
            for f in queue["sync"]:
                f()

        @block.gpsimd
        def _(e):
            for f in queue["gpsimd"]:
                f()

        @block.scalar
        def _(e):
            for f in queue["scalar"]:
                f()

        @block.vector
        def _(e):
            for f in queue["vector"]:
                f()

        @block.tensor
        def _(e):
            for f in queue["tensor"]:
                f()


def layout(inputs):
    a = {k: np.asarray(v) for k, v in inputs.items()}
    slots = plan()
    w = np.zeros((len(slots), P, 2048), np.float32)
    for n, (name, layer, ks, cols) in enumerate(slots):
        o = 0
        for k in ks:
            for nm in (name if isinstance(name, tuple) else (name,)):
                w[n, :, o:o + len(cols)] = a[nm][layer][k * P:k * P + P][:, cols]
                o += len(cols)
    con, tabs = constants(), tables()

    def rows(v):
        return np.broadcast_to(np.ascontiguousarray(v).reshape(1, -1), (P, v.size))

    def col(v):
        return v.reshape(-1, P).T

    def taps(*v):
        return np.stack([col(q) for q in v], 2).reshape(P, -1)

    relb = np.zeros((P, 8), np.float32)
    relb[0:32] = a["rel_bias_2"]
    cw, cb, dw = a["ffn_conv_w"], a["ffn_conv_b"], a["dn_conv_2"][0]
    values = {
        "keep": dict(ident=con["ident"], an0=col(a["attn_norm"][0]), an1=col(a["attn_norm"][1]), fn0=col(a["ffn_norm"][0]),
                     fn1=col(a["ffn_norm"][1]), an2=col(a["attn_norm_2"][0]), fn2=col(a["ffn_norm_2"][0]),
                     cw0=taps(cw[0, 0], cw[0, 1], cw[0, 2], cb[0]), cw1=taps(cw[1, 0], cw[1, 1], cw[1, 2], cb[1]),
                     dnw=taps(dw[0], dw[1], dw[2], dw[3]), mhalf=np.full((P, 16), -0.5, np.float32)),
        "a": dict(cos=con["cos"], sin=con["sin"], m0=con["am0"], m1=con["am1"],
                  gain=rows(np.stack([a["a_q_norm"][0], a["a_k_norm"][0]], 1))),
        "b": dict(cos=con["cos"], sin=con["sin"], m0=con["bm0"], m1=con["bm1"],
                  gain=rows(np.stack([a["b_q_norm"][0], a["b_k_norm"][0]], 0))),
        "c": dict(gq=rows(a["swa_q_norm_2"]), gk=rows(a["swa_k_norm_2"]), gout=rows(a["dn_out_norm_2"]), alog=rows(a["dn_a_log_2"]),
                  dtb=rows(a["dn_dt_bias_2"]), sink=rows(a["swa_sinks_2"]), relb=relb,
                  **{k: con[k] for k in ("cum", "blk", "sel", "strict", "lev", "lev0t")}),
    }
    arrays = {"x": a["x"], "w": w, "onehot": con["onehot"]}
    for name, t in tabs.items():
        v = np.zeros((P, t.n), np.float32)
        for k, (o, n) in t.at.items():
            v[:, o:o + n] = values[name][k]
        arrays[name] = v
    return arrays


def kernel(**inputs):
    import concourse.bacc as bacc
    from concourse.bass_utils import run_bass_kernel_spmd

    nc = bacc.Bacc("TRN2", target_bir_lowering=False, num_devices=1)
    arrays = layout(inputs)
    dram = {k: nc.dram_tensor(f"in_{k}", v.shape, F32, kind="ExternalInput").ap() for k, v in arrays.items()}
    out = nc.dram_tensor("out", (1, S, D), F32, kind="ExternalOutput").ap()
    build(nc, dram, out)
    r = run_bass_kernel_spmd(nc, [{f"in_{k}": v for k, v in arrays.items()}], core_ids=[0])
    return r.results[0]["out"]
```
